# Optimizing a Trainium2 kernel written in Bass

```python
import math
import jax
import jax.numpy as jnp
from jax import lax
import numpy as np

D_MODEL = 1024
BATCH = 1
SEQ = 1024
DEPTH = 1

CTX_LEN = 256
GRID_W = 64
GDN_HEADS = 4
GDN_DK = 128
GDN_DV = 128
GDN_CONV = 5
GDN_CHUNK = 64
DIFF_HEADS = 4
DIFF_DK = 64
DIFF_DV = 2 * DIFF_DK
Q_BLOCK = 128
ROPE_THETA = 10000.0
D_MIX = GDN_HEADS * GDN_DV + DIFF_HEADS * DIFF_DV
GDN_QK = GDN_HEADS * GDN_DK
GDN_QKV = 2 * GDN_QK + GDN_HEADS * GDN_DV
GDN_Z = GDN_HEADS * GDN_DV
GDN_GATES = 2 * GDN_HEADS
GDN_COLS = GDN_QKV + GDN_Z + 2 * GDN_GATES
DIFF_QK = DIFF_HEADS * 2 * DIFF_DK
DIFF_COLS = 2 * DIFF_QK + DIFF_HEADS * DIFF_DV
IN_COLS = GDN_COLS + DIFF_COLS
MOE_GROUPS = 4
EXPERTS_PER_GROUP = 8
N_EXPERTS = MOE_GROUPS * EXPERTS_PER_GROUP
TOPK_IN_GROUP = 2
D_EXPERT = 512
EXPERT_BLOCK = 128
LN_EPS = 1e-5
NORM_EPS = 1e-6

kernel_name = 'hybrid_gdn_diffattn_hmoe_block'

def normalize(u):
    uf = u.astype(jnp.float32)
    mu = jnp.mean(uf, axis=-1, keepdims=True)
    var = jnp.mean(jnp.square(uf - mu), axis=-1, keepdims=True)
    return ((uf - mu) * lax.rsqrt(var + LN_EPS)).astype(u.dtype)

def layer_norm(u, g, b):
    return normalize(u) * g + b

def modulate(u, shift, scale):
    return normalize(u) * (1 + scale) + shift

def rms_norm(u, w):
    uf = u.astype(jnp.float32)
    y = uf * lax.rsqrt(jnp.mean(jnp.square(uf), axis=-1, keepdims=True) + NORM_EPS)
    return y.astype(w.dtype) * w

def l2_normalize(u):
    uf = u.astype(jnp.float32)
    return uf * lax.rsqrt(jnp.sum(jnp.square(uf), axis=-1, keepdims=True) + NORM_EPS)

def centred_dwconv(u, w):
    taps = w.shape[0]
    pad = taps // 2
    seq_len = u.shape[1]
    up = jnp.pad(u, ((0, 0), (pad, pad), (0, 0)))
    return sum(up[:, j:j + seq_len] * w[j] for j in range(taps))

def axial_rope(u):
    seq_len = u.shape[1]
    rows = seq_len // GRID_W
    row = jnp.repeat(jnp.arange(rows), GRID_W)
    col = jnp.tile(jnp.arange(GRID_W), rows)
    half = u.shape[-1] // 2
    inv_freq = ROPE_THETA ** (-jnp.arange(0, half, 2, dtype=jnp.float32) / half)

    def rot(v, pos):
        ang = pos.astype(jnp.float32)[:, None] * inv_freq
        ang = ang.reshape((1, seq_len) + (1,) * (v.ndim - 3) + (half // 2,))
        cos, sin = jnp.cos(ang).astype(v.dtype), jnp.sin(ang).astype(v.dtype)
        v1, v2 = jnp.split(v, 2, axis=-1)
        return jnp.concatenate([v1 * cos - v2 * sin, v2 * cos + v1 * sin], axis=-1)

    return jnp.concatenate([rot(u[..., :half], row), rot(u[..., half:], col)], axis=-1)

def gated_delta_chunked(q, k, v, g, beta, s0, with_out):
    f32 = jnp.float32
    bn, seq_len, heads, _ = q.shape
    dv = v.shape[-1]
    n_chunks = seq_len // GDN_CHUNK

    def chunks(t):
        t = t.astype(f32).reshape((bn, n_chunks, GDN_CHUNK) + t.shape[2:])
        return jnp.moveaxis(t, 3, 2)

    q, k, v, beta = chunks(q), chunks(k), chunks(v), chunks(beta)
    gc = jnp.cumsum(chunks(g), axis=-1)
    tri = jnp.tril(jnp.ones((GDN_CHUNK, GDN_CHUNK), dtype=bool))
    strict = jnp.tril(jnp.ones((GDN_CHUNK, GDN_CHUNK), dtype=bool), k=-1)
    decay = jnp.exp(jnp.where(tri, gc[..., :, None] - gc[..., None, :], -jnp.inf))
    k_beta = k * beta[..., None]
    a_kk = jnp.where(strict, jnp.einsum('bnhid,bnhjd->bnhij', k_beta, k) * decay, 0.0)
    eye = jnp.eye(GDN_CHUNK, dtype=f32)
    t_inv = lax.linalg.triangular_solve(a_kk + eye, jnp.broadcast_to(eye, a_kk.shape),
                                        left_side=True, lower=True, unit_diagonal=True)
    u = t_inv @ (v * beta[..., None])
    w = t_inv @ (k_beta * jnp.exp(gc)[..., None])
    g_last = gc[..., -1]
    k_tail = k * jnp.exp(g_last[..., None] - gc)[..., None]
    xs = [u, w, k_tail, g_last]
    if with_out:
        xs += [q * jnp.exp(gc)[..., None], jnp.einsum('bnhid,bnhjd->bnhij', q, k) * decay]
    xs = [jnp.moveaxis(t, 1, 0) for t in xs]

    def step(s, inp):
        v_new = inp[0] - inp[1] @ s
        s_next = s * jnp.exp(inp[3])[..., None, None] + jnp.einsum('bhcd,bhce->bhde', inp[2], v_new)
        o = inp[4] @ s + inp[5] @ v_new if with_out else None
        return s_next, o

    s_final, o = lax.scan(step, s0.astype(f32), xs)
    if with_out:
        o = jnp.moveaxis(jnp.moveaxis(o, 0, 1), 2, 3).reshape(bn, seq_len, heads, dv)
    return s_final, o

def gdn_inputs(p, conv_w, a_log, dt_bias):
    bn, seq_len, _ = p.shape
    qkv = jax.nn.silu(centred_dwconv(p[..., :GDN_QKV], conv_w))
    q = l2_normalize(qkv[..., :GDN_QK].reshape(bn, seq_len, GDN_HEADS, GDN_DK)) * GDN_DK ** -0.5
    k = l2_normalize(qkv[..., GDN_QK:2 * GDN_QK].reshape(bn, seq_len, GDN_HEADS, GDN_DK))
    v = qkv[..., 2 * GDN_QK:].reshape(bn, seq_len, GDN_HEADS, GDN_DV)
    off = GDN_QKV + GDN_Z
    beta = jax.nn.sigmoid(p[..., off:off + GDN_GATES].astype(jnp.float32)).reshape(bn, seq_len, 2, GDN_HEADS)
    a = p[..., off + GDN_GATES:GDN_COLS].astype(jnp.float32).reshape(bn, seq_len, 2, GDN_HEADS)
    g = -jnp.exp(a_log.astype(jnp.float32)) * jax.nn.softplus(a + dt_bias.astype(jnp.float32))
    return q, k, v, beta, g

def gdn_direction(q, k, v, beta, g, s0, reverse, with_out):
    if reverse:
        q, k, v, beta, g = (jnp.flip(t, axis=1) for t in (q, k, v, beta, g))
    s, o = gated_delta_chunked(q, k, v, g, beta, s0, with_out)
    if reverse and with_out:
        o = jnp.flip(o, axis=1)
    return s, o

def gated_out(o, z, norm_w):
    bn, seq_len = o.shape[:2]
    zh = z.reshape(bn, seq_len, GDN_HEADS, GDN_DV)
    return (rms_norm(o, norm_w) * jax.nn.silu(zh)).reshape(bn, seq_len, GDN_Z)

def gdn_group(p, pc, conv_w, a_log, dt_bias, norm_w, need_ctx):
    lat = gdn_inputs(p, conv_w, a_log, dt_bias)
    con = gdn_inputs(pc, conv_w, a_log, dt_bias)
    s0 = jnp.zeros((p.shape[0], GDN_HEADS, GDN_DK, GDN_DV), jnp.float32)
    outs_lat, outs_ctx = [], []
    for d, reverse in enumerate((False, True)):
        qc, kc, vc, bc, gc = con
        s_ctx, oc = gdn_direction(qc, kc, vc, bc[:, :, d], gc[:, :, d], s0, reverse, need_ctx)
        q, k, v, b, g = lat
        _, o = gdn_direction(q, k, v, b[:, :, d], g[:, :, d], s_ctx, reverse, True)
        outs_lat.append(o)
        outs_ctx.append(oc)
    y = gated_out(outs_lat[0] + outs_lat[1], p[..., GDN_QKV:GDN_QKV + GDN_Z], norm_w)
    yc = gated_out(outs_ctx[0] + outs_ctx[1], pc[..., GDN_QKV:GDN_QKV + GDN_Z], norm_w) if need_ctx else None
    return y, yc

def diff_attend(q, k, v, lam):
    bn, lq, heads = q.shape[:3]
    dv = v.shape[-1]
    nb = lq // Q_BLOCK
    qb = jnp.moveaxis(q.reshape((bn, nb, Q_BLOCK) + q.shape[2:]), 1, 0)
    scale = DIFF_DK ** -0.5

    def one(q_blk):
        s = jnp.einsum('bqhcd,bkhcd->bhcqk', q_blk, k).astype(jnp.float32) * scale
        pr = jax.nn.softmax(s, axis=-1)
        a = pr[:, :, 0] - lam * pr[:, :, 1]
        return jnp.einsum('bhqk,bkhd->bqhd', a.astype(v.dtype), v)

    o = lax.map(one, qb)
    return jnp.moveaxis(o, 0, 1).reshape(bn, lq, heads, dv)

def diff_heads(u):
    bn, seq_len, _ = u.shape
    q = u[..., :DIFF_QK].reshape(bn, seq_len, DIFF_HEADS, 2, DIFF_DK)
    k = u[..., DIFF_QK:2 * DIFF_QK].reshape(bn, seq_len, DIFF_HEADS, 2, DIFF_DK)
    v = u[..., 2 * DIFF_QK:].reshape(bn, seq_len, DIFF_HEADS, DIFF_DV)
    return q, k, v

def diff_group(p, pc, lam, lam_init, norm_w, need_ctx):
    q, k, v = diff_heads(p)
    qc, kc, vc = diff_heads(pc)
    q, k = axial_rope(q), axial_rope(k)
    lf = lam.astype(jnp.float32)
    lam_full = jnp.exp(jnp.sum(lf[0] * lf[1])) - jnp.exp(jnp.sum(lf[2] * lf[3])) + lam_init
    bn, seq_len = p.shape[:2]
    o = diff_attend(q, jnp.concatenate([k, kc], axis=1), jnp.concatenate([v, vc], axis=1), lam_full)
    y = (rms_norm(o, norm_w) * (1 - lam_init)).reshape(bn, seq_len, DIFF_HEADS * DIFF_DV)
    if need_ctx:
        oc = diff_attend(qc, kc, vc, lam_full)
        yc = (rms_norm(oc, norm_w) * (1 - lam_init)).reshape(bn, pc.shape[1], DIFF_HEADS * DIFF_DV)
    else:
        yc = None
    return y, yc

def hybrid_mixer(h, hc, w_in, conv_w, a_log, dt_bias, gdn_norm_w, lam, lam_init, diff_norm_w, w_out, need_ctx):
    p = h @ w_in
    pc = hc @ w_in
    y_gdn, yc_gdn = gdn_group(p[..., :GDN_COLS], pc[..., :GDN_COLS], conv_w, a_log, dt_bias, gdn_norm_w, need_ctx)
    y_diff, yc_diff = diff_group(p[..., GDN_COLS:], pc[..., GDN_COLS:], lam, lam_init, diff_norm_w, need_ctx)
    y = jnp.concatenate([y_gdn, y_diff], axis=-1) @ w_out
    yc = jnp.concatenate([yc_gdn, yc_diff], axis=-1) @ w_out if need_ctx else None
    return y, yc

def routed_experts(t, expert, gate, w_gate, w_up, w_down):
    n_tok, d = t.shape
    n_assign = n_tok * TOPK_IN_GROUP
    e_flat = expert.reshape(-1)
    tok = jnp.repeat(jnp.arange(n_tok), TOPK_IN_GROUP)
    order = jnp.argsort(e_flat)
    e_s, tok_s, g_s = e_flat[order], tok[order], gate.reshape(-1)[order]
    counts = jnp.bincount(e_flat, length=N_EXPERTS)
    start = jnp.cumsum(counts) - counts
    padded = (counts + EXPERT_BLOCK - 1) // EXPERT_BLOCK * EXPERT_BLOCK
    p_end = jnp.cumsum(padded)
    p_start = p_end - padded
    dest = p_start[e_s] + (jnp.arange(n_assign) - start[e_s])
    n_blocks = (n_assign + EXPERT_BLOCK - 1) // EXPERT_BLOCK + N_EXPERTS
    buf = jnp.zeros((n_blocks * EXPERT_BLOCK, d), t.dtype).at[dest].set(t[tok_s])
    block_e = jnp.clip(jnp.searchsorted(p_end, jnp.arange(n_blocks) * EXPERT_BLOCK, side='right'), 0, N_EXPERTS - 1)

    def block_ffn(args):
        xb, e = args
        return (jax.nn.silu(xb @ w_gate[e]) * (xb @ w_up[e])) @ w_down[e]

    yb = lax.map(block_ffn, (buf.reshape(n_blocks, EXPERT_BLOCK, d), block_e))
    y = yb.reshape(n_blocks * EXPERT_BLOCK, d)[dest] * g_s[:, None]
    return jnp.zeros((n_tok, d), y.dtype).at[tok_s].add(y)

def hier_moe(h, w_rg, b_rg, w_re, b_re, w_gate, w_up, w_down):
    bn, seq_len, d = h.shape
    t = h.reshape(bn * seq_len, d)
    n_tok = t.shape[0]
    p_group = jax.nn.softmax((t @ w_rg + b_rg).astype(jnp.float32), axis=-1)
    p_g, grp = lax.top_k(p_group, 1)
    logits_e = (t @ w_re + b_re).astype(jnp.float32).reshape(n_tok, MOE_GROUPS, EXPERTS_PER_GROUP)
    logits_in = jnp.take_along_axis(logits_e, grp[:, :, None], axis=1)[:, 0]
    p_e, local = lax.top_k(jax.nn.softmax(logits_in, axis=-1), TOPK_IN_GROUP)
    gate = p_g * p_e / jnp.sum(p_e, axis=-1, keepdims=True)
    expert = grp * EXPERTS_PER_GROUP + local
    y = routed_experts(t, expert, gate.astype(t.dtype), w_gate, w_up, w_down)
    return y.reshape(bn, seq_len, d)

def setup_inputs(seed: int = 0) -> dict:
    key = jax.random.key(seed)
    ks = jax.random.split(key, 26)
    f32 = jnp.float32

    def nrm(k, shape, s):
        return jax.random.normal(k, shape, f32) * s

    beta_dn = (8.0 * DEPTH) ** -0.25
    dt = jnp.exp(jax.random.uniform(ks[9], (DEPTH, 2, GDN_HEADS), f32, math.log(1e-3), math.log(1e-1)))
    return {
        'x': nrm(ks[0], (BATCH, SEQ, D_MODEL), 1.0),
        'c': nrm(ks[1], (BATCH, D_MODEL), 1.0),
        'ctx': nrm(ks[2], (BATCH, CTX_LEN, D_MODEL), 1.0),
        'c_ctx': nrm(ks[3], (D_MODEL,), 1.0),
        'w_ada': nrm(ks[4], (DEPTH, D_MODEL, 6 * D_MODEL), D_MODEL ** -0.5),
        'b_ada': nrm(ks[5], (DEPTH, 6 * D_MODEL), 0.01),
        'w_in': nrm(ks[6], (DEPTH, D_MODEL, IN_COLS), D_MODEL ** -0.5),
        'conv_w': nrm(ks[7], (DEPTH, GDN_CONV, GDN_QKV), GDN_CONV ** -0.5),
        'gdn_a_log': jnp.log(jax.random.uniform(ks[8], (DEPTH, 2, GDN_HEADS), f32, 1.0, 16.0)),
        'gdn_dt_bias': dt + jnp.log(-jnp.expm1(-dt)),
        'gdn_norm_w': 1.0 + nrm(ks[10], (DEPTH, GDN_DV), 0.02),
        'diff_lambda': nrm(ks[11], (DEPTH, 4, DIFF_DK), 0.1),
        'diff_norm_w': 1.0 + nrm(ks[12], (DEPTH, DIFF_DV), 0.02),
        'w_out': nrm(ks[13], (DEPTH, D_MIX, D_MODEL), D_MIX ** -0.5 * beta_dn),
        'ln1_g': 1.0 + nrm(ks[14], (DEPTH, D_MODEL), 0.02),
        'ln1_b': nrm(ks[15], (DEPTH, D_MODEL), 0.02),
        'w_router_group': nrm(ks[16], (DEPTH, D_MODEL, MOE_GROUPS), D_MODEL ** -0.5),
        'b_router_group': nrm(ks[17], (DEPTH, MOE_GROUPS), 0.01),
        'w_router_expert': nrm(ks[18], (DEPTH, D_MODEL, N_EXPERTS), D_MODEL ** -0.5),
        'b_router_expert': nrm(ks[19], (DEPTH, N_EXPERTS), 0.01),
        'w_expert_gate': nrm(ks[20], (DEPTH, N_EXPERTS, D_MODEL, D_EXPERT), D_MODEL ** -0.5),
        'w_expert_up': nrm(ks[21], (DEPTH, N_EXPERTS, D_MODEL, D_EXPERT), D_MODEL ** -0.5),
        'w_expert_down': nrm(ks[22], (DEPTH, N_EXPERTS, D_EXPERT, D_MODEL), D_EXPERT ** -0.5 * beta_dn),
        'ln2_g': 1.0 + nrm(ks[23], (DEPTH, D_MODEL), 0.02),
        'ln2_b': nrm(ks[24], (DEPTH, D_MODEL), 0.02),
    }

def reference(x, c, ctx, c_ctx, w_ada, b_ada, w_in, conv_w, gdn_a_log, gdn_dt_bias, gdn_norm_w,
              diff_lambda, diff_norm_w, w_out, ln1_g, ln1_b, w_router_group, b_router_group,
              w_router_expert, b_router_expert, w_expert_gate, w_expert_up, w_expert_down, ln2_g, ln2_b):
    alpha = (2.0 * DEPTH) ** 0.25
    for i in range(DEPTH):
        need_ctx = i < DEPTH - 1
        mod = jax.nn.silu(c) @ w_ada[i] + b_ada[i]
        mod_c = jax.nn.silu(c_ctx) @ w_ada[i] + b_ada[i]
        sh1, sc1, g1, sh2, sc2, g2 = jnp.split(mod[:, None, :], 6, axis=-1)
        csh1, csc1, cg1, csh2, csc2, cg2 = jnp.split(mod_c, 6, axis=-1)
        lam_init = 0.8 - 0.6 * math.exp(-0.3 * i)
        y, yc = hybrid_mixer(modulate(x, sh1, sc1), modulate(ctx, csh1, csc1), w_in[i], conv_w[i],
                             gdn_a_log[i], gdn_dt_bias[i], gdn_norm_w[i], diff_lambda[i], lam_init,
                             diff_norm_w[i], w_out[i], need_ctx)
        moe_w = (w_router_group[i], b_router_group[i], w_router_expert[i], b_router_expert[i],
                 w_expert_gate[i], w_expert_up[i], w_expert_down[i])
        x = layer_norm(alpha * x + g1 * y, ln1_g[i], ln1_b[i])
        x = layer_norm(alpha * x + g2 * hier_moe(modulate(x, sh2, sc2), *moe_w), ln2_g[i], ln2_b[i])
        if need_ctx:
            ctx = layer_norm(alpha * ctx + cg1 * yc, ln1_g[i], ln1_b[i])
            ctx = layer_norm(alpha * ctx + cg2 * hier_moe(modulate(ctx, csh2, csc2), *moe_w), ln2_g[i], ln2_b[i])
    return x


_drawn_inputs = setup_inputs


def setup_inputs(seed=0):
    import zlib

    import numpy as np

    out = dict(_drawn_inputs(seed))
    spreads = {}
    factors = {'b_ada': 3.036,
     'gdn_norm_w': 18.01,
     'diff_norm_w': 24.393,
     'b_router_group': 7.948,
     'b_router_expert': 5.405,
     'ln2_g': 8.609,
     'ln2_b': 8.274}
    for name, (base, spread) in spreads.items():
        noise = np.random.default_rng([zlib.crc32(name.encode()), seed]).standard_normal(out[name].shape)
        drawn = base * np.exp(spread * noise) if base else spread * noise
        out[name] = jnp.asarray(drawn.astype(out[name].dtype))
    for name, factor in factors.items():
        out[name] = (out[name] * factor).astype(out[name].dtype)
    return out
```

```python
import math
from contextlib import contextmanager

import numpy as np
import concourse.bass as bass
from concourse import mybir

F32 = mybir.dt.float32
I32 = mybir.dt.int32
ALU = mybir.AluOpType
ACT = mybir.ActivationFunctionType
AX = mybir.AxisListType.X

P = 128
D = 1024
KD = D // P
SEQ, CTX = 1024, 256
TL, TC = SEQ // P, CTX // P
TT = TL + TC
TOK = SEQ + CTX
H = 4
HD = H * P
DK = 64
NC = 512
CONV = 5
NMOD = 6 * D
NG, NE, EG = 4, 32, 8
DE = 512
BLOCKS = 2 * SEQ // P + NE
ALPHA = 2.0 ** 0.25
LN_EPS, NORM_EPS = 1e-5, 1e-6
LAM_INIT = 0.8 - 0.6 * math.exp(0.0)
GDN_GATES_AT = 4 * HD
DIFF_AT = GDN_GATES_AT + 16
IN_COLS = DIFF_AT + 3 * HD
TAIL = IN_COLS - 3 * HD
BIG = 1.0e30
LEVELS = 7


class Link:

    def __init__(self, eng, sem):
        self.eng, self.sem, self.base, self.n = eng, sem, 0, 0

    def __call__(self, ins, plain=False):
        ins.then_inc(self.sem, 1)
        self.n += 1
        self.eng.wait_ge(self.sem, self.base + self.n)
        if plain:
            self.eng.sem_inc(self.sem, 1)
            self.n += 1

    @contextmanager
    def loop(self, count, per):
        start = self.base + self.n
        with self.eng.Fori(0, count) as i:
            self.base, self.n = start + i * per, 0
            yield i
            assert self.n == per, f"the body links {self.n}"
        self.base, self.n = start + count * per, 0


class Machine:

    def __init__(self, nc, dram):
        self.nc, self.dram = nc, dram
        self.top, self.limit = 16512, 229312
        self.high = 229312 - 4 * (H * TOK + TT * HD + TT * 16)
        self.psum = nc.alloc_psum_tensor("psum", [P, 8 * NC], F32)
        self.keep = {}

    def sb(self, name, shape, dt=F32):
        size = 4 * int(np.prod(shape[1:]))
        t = self.nc.alloc_sbuf_tensor_at(name, shape, dt, offset=self.top)
        self.top += -(-size // 32) * 32
        assert self.top <= self.limit, f"{name} ends at {self.top}"
        return t

    def bank(self, b, n=NC, at=0):
        return self.psum[:, b * NC + at:b * NC + at + n]

    def sem(self, name, lasting=False):
        s = self.nc.alloc_semaphore(name)
        if not lasting:
            self.phase_sems.append(s)
        return s

    def scratch(self, name, shape, dt=F32):
        self.dram[name] = self.nc.dram_tensor(name, shape, dt, kind="Internal").ap()
        return self.dram[name]


def one(ap, i):
    return ap[bass.ds(i, 1)]


def cols(ap):
    return ap.rearrange("p a n -> p (a n)")


def flat(ap):
    return ap.rearrange("a b n -> (a b) n")


def modulation(m):
    nc, d = m.nc, m.dram
    mask = m.sb("mask", [P, 7 + 2 * LEVELS, P])
    modT = m.sb("modT", [P, 6 * KD, 2])
    small = m.sb("small", [P, 96])
    m.keep.update(mask=mask, modT=modT, ident=mask[:, 0, :], ones=mask[:, 1, :], tri=[mask[:, 2, :], mask[:, 3, :]],
                  before=mask[:, 4, :], neg=[mask[:, 5, :], mask[:, 6, :]],
                  level=[[mask[:, 7 + LEVELS * r + lv, :] for lv in range(LEVELS)] for r in range(2)])
    m.keep.update(small=small, eps_ln=small[:, 68:69], eps_norm=small[:, 69:70])
    ident = m.keep["ident"]
    top = m.top
    m.scratch("mod_rows", [2, NMOD])
    craw = m.sb("craw", [P, KD, 2])
    csil = m.sb("csil", [P, KD, 2])
    brow = m.sb("brow", [2, NMOD])
    mod = m.sb("mod", [2, NMOD])
    wa = [m.sb(f"wa{u}", [P, KD, NC]) for u in range(2)]
    small_loaded, c_ready, cols_ready = m.sem("ada_small"), m.sem("ada_c"), m.sem("ada_cols")
    cols_kept, rows_stored = m.sem("ada_cols_kept"), m.sem("ada_rows_stored")
    loaded = [m.sem(f"ada_loaded{u}") for u in range(2)]
    product = [m.sem(f"ada_product{u}") for u in range(2)]
    kept = [m.sem(f"ada_kept{u}") for u in range(2)]
    w = d["w_ada"].rearrange("(k p) (j n) -> j p k n", p=P, n=NC)
    steps = NMOD // NC // 2

    with nc.Block() as block:
        @block.sync
        def _(sp):
            sp.dma_start(craw[:, :, :], d["c_cols"].rearrange("p (k r) -> p k r", r=2)).then_inc(small_loaded, 16)
            sp.dma_start(brow[:, :], d["b_ada"]).then_inc(small_loaded, 16)
            sp.dma_start(mask[:, :, :], d["masks"].rearrange("p (s n) -> p s n", n=P)).then_inc(small_loaded, 16)
            sp.dma_start(small[:, :], d["small"]).then_inc(small_loaded, 16)
            with sp.Fori(0, steps) as i:
                for u in range(2):
                    sp.wait_ge(product[u], i)
                    sp.dma_start(wa[u][:, :, :], one(w, 2 * i + u).rearrange("j p k n -> (j p) k n")).then_inc(loaded[u], 16)
            sp.wait_ge(kept[0], steps)
            sp.wait_ge(kept[1], steps)
            sp.dma_start(d["mod_rows"], mod[:, :]).then_inc(rows_stored, 16)
            sp.wait_ge(rows_stored, 16)

        @block.scalar
        def _(act):
            act.wait_ge(small_loaded, 64)
            nc.scalar.activation(csil[:, :, :], craw[:, :, :], ACT.Silu).then_inc(c_ready, 1)

        @block.tensor
        def _(pe):
            pe.wait_ge(small_loaded, 64)
            pe.wait_ge(c_ready, 1)
            with pe.Fori(0, steps) as i:
                for u in range(2):
                    pe.wait_ge(loaded[u], 16 * i + 16)
                    pe.wait_ge(kept[u], i)
                    for k in range(KD):
                        last = nc.tensor.matmul(m.bank(u)[0:2, :], csil[:, k, :], wa[u][:, k, :],
                                                start=(k == 0), stop=(k == KD - 1))
                    last.then_inc(product[u], 1)
            pe.wait_ge(kept[0], steps)
            pe.wait_ge(kept[1], steps)
            for j in range(6 * KD):
                last = nc.tensor.matmul(m.bank(2)[:, 2 * j:2 * j + 2], mod[:, j * P:(j + 1) * P], ident[0:2, 0:2],
                                        start=True, stop=True)
            last.then_inc(cols_ready, 1)

        @block.vector
        def _(dve):
            dve.wait_ge(small_loaded, 64)
            with dve.Fori(0, steps) as i:
                for u in range(2):
                    dve.wait_ge(product[u], i + 1)
                    here = bass.ds((2 * i + u) * NC, NC)
                    nc.vector.tensor_tensor(mod[:, here], m.bank(u)[0:2, :], brow[:, here], ALU.add).then_inc(kept[u], 1)
            dve.wait_ge(cols_ready, 1)
            nc.vector.tensor_copy(modT[:, :, :], m.bank(2, 12 * KD).rearrange("p (j r) -> p j r", r=2)).then_inc(cols_kept, 1)
            dve.wait_ge(cols_kept, 1)
            for part in (1, 4):
                nc.vector.tensor_scalar(modT[:, part * KD:(part + 1) * KD, :], modT[:, part * KD:(part + 1) * KD, :],
                                        1.0, None, ALU.add).then_inc(cols_kept, 1)
    m.top = top


def normed_transposed(m):
    nc, d, ident, modT = m.nc, m.dram, m.keep["ident"], m.keep["modT"]
    m.base = m.top
    hT = m.keep["hT"] = m.sb("hT", [P, KD, TOK])
    top = m.top
    xt = [m.sb(f"xt{u}", [P, D]) for u in range(2)]
    xn = [m.sb(f"xn{u}", [P, D]) for u in range(2)]
    st = m.sb("ln_st", [P, 2, 6])
    mv = [m.sb(f"ln_mv{u}", [P, 2]) for u in range(2)]
    sd = [m.sb(f"ln_sd{u}", [P, 1]) for u in range(2)]
    loaded = [m.sem(f"x_loaded{u}") for u in range(2)]
    stats, std = m.sem("x_stats"), m.sem("x_std")
    normed = [m.sem(f"x_normed{u}") for u in range(2)]
    turned = [m.sem(f"x_turned{u}") for u in range(2)]
    kept = [m.sem(f"x_kept{u}") for u in range(2)]
    own = m.sem("x_dve_link")
    x = d["tokens"].rearrange("(t p) n -> t p n", p=P)

    with nc.Block() as block:
        @block.sync
        def _(sp):
            with sp.Fori(0, TT // 2) as i:
                for u in range(2):
                    sp.wait_ge(normed[u], i)
                    sp.dma_start(xt[u][:, :], flat(one(x, 2 * i + u))).then_inc(loaded[u], 16)

        @block.vector
        def _(dve):
            link = Link(dve, own)
            with link.loop(TT // 2, 8) as i:
                for u in range(2):
                    dve.wait_ge(loaded[u], 16 * i + 16)
                    for c in range(2):
                        last = nc.vector.bn_stats(st[:, c, :], xt[u][:, c * NC:(c + 1) * NC])
                    link(last, plain=True)
                    link(nc.vector.bn_aggr(mv[u][:, :], st[:, :, :].rearrange("p a b -> p (a b)")))
                    dve.sem_inc(stats, 1)
                    dve.wait_ge(std, 2 * i + u + 1)
                    link(nc.vector.reciprocal(sd[u][:, :], sd[u][:, :]))
                    dve.wait_ge(turned[u], i)
                    nc.vector.tensor_scalar(xn[u][:, :], xt[u][:, :], mv[u][:, 0:1], sd[u][:, :],
                                            ALU.subtract, ALU.mult).then_inc(normed[u], 1)

        @block.tensor
        def _(pe):
            with pe.Fori(0, TT // 2) as i:
                for u in range(2):
                    pe.wait_ge(normed[u], i + 1)
                    pe.wait_ge(kept[u], i)
                    for k in range(KD):
                        last = nc.tensor.transpose(m.bank(2 * u + k // 4)[:, k % 4 * P:(k % 4 + 1) * P],
                                                   xn[u][:, k * P:(k + 1) * P], ident)
                    last.then_inc(turned[u], 1)

        @block.scalar
        def _(act):
            def tile(i, r):
                for u in range(2):
                    act.wait_ge(stats, 2 * i + u + 1)
                    act.wait_ge(normed[u], i)
                    nc.scalar.activation(sd[u][:, :], mv[u][:, 1:2], ACT.Sqrt, bias=m.keep["eps_ln"]).then_inc(std, 1)
                for u in range(2):
                    act.wait_ge(turned[u], i + 1)
                    for k in range(KD):
                        last = nc.scalar.activation(hT[:, k, bass.ds((2 * i + u) * P, P)],
                                                    m.bank(2 * u + k // 4)[:, k % 4 * P:(k % 4 + 1) * P], ACT.Identity,
                                                    scale=modT[:, KD + k, r:r + 1], bias=modT[:, k, r:r + 1])
                    last.then_inc(kept[u], 1)

            with act.Fori(0, TL // 2) as i:
                tile(i, 0)
            tile(TL // 2, 1)
    m.top = top


def delta_inputs(m):
    nc, d, ident, hT = m.nc, m.dram, m.keep["ident"], m.keep["hT"]
    gap = CONV // 2
    wide = TOK + gap
    wt = m.keep["wt"] = m.sb("wt", [P, KD, TAIL])
    m.keep["wt_loaded"] = m.sem("wt_loaded", lasting=True)
    top = m.top
    m.scratch("qT", [H, P, SEQ])
    m.scratch("kT", [H, P, TOK])
    m.scratch("k", [TT, P, HD])
    m.scratch("v", [TT, P, HD])
    cw = m.sb("cw", [P, 3 * H * CONV])
    wm = [m.sb(f"wm{u}", [P, KD, P]) for u in range(2)]
    padded = [m.sb(f"padded{u}", [P, TOK + 3 * gap]) for u in range(2)]
    conv = [m.sb(f"conv{u}", [P, wide]) for u in range(2)]
    act_out = [m.sb(f"silu{u}", [P, wide]) for u in range(2)]
    raw = [m.sb(f"raw{u}", [P, TT, P]) for u in range(2)]
    nrm = [m.sb(f"nrm{u}", [P, TT, P]) for u in range(2)]
    back = [m.sb(f"back{u}", [P, TOK]) for u in range(2)]
    ssq = m.sb("ssq", [P, TT])
    sd = m.sb("ssd", [P, TT])
    cw_loaded, zeroed = m.sem("cw_loaded"), m.sem("pads_zeroed")
    wm_loaded = [m.sem(f"wm_loaded{u}") for u in range(2)]
    tok_stored = [m.sem(f"heads_tok_stored{u}") for u in range(2)]
    ch_stored = [m.sem(f"heads_ch_stored{u}") for u in range(2)]
    proj, evac, conved, silued = m.sem("c_proj"), m.sem("c_evac"), m.sem("c_conved"), m.sem("c_silued")
    turned, kept, summed, rooted = m.sem("c_turned"), m.sem("c_kept"), m.sem("c_summed"), m.sem("c_rooted")
    normed, returned, rekept = m.sem("c_normed"), m.sem("c_returned"), m.sem("c_rekept")
    own = m.sem("c_dve_link")
    PARTS = 3 * H
    QK = 2 * H

    def tiles(c):
        return TL if c < H else TT

    def groups(c):
        return 2 * c if c < H else 3 * c - H

    def tok_count(c, u):
        return 16 * sum(b >= H for b in range(c) if b % 2 == u)

    with nc.Block() as block:
        @block.sync
        def _(sp):
            sp.dma_start(cw[:, :], d["conv_cols"]).then_inc(cw_loaded, 16)
            for c in range(PARTS):
                if c >= 2:
                    sp.wait_ge(proj, c - 1)
                sp.dma_start(wm[c % 2][:, :, :], d["w_in"][:, c * P:(c + 1) * P].rearrange("(k p) n -> p k n", p=P)
                             ).then_inc(wm_loaded[c % 2], 16)
                if c == 1:
                    sp.dma_start(wt[:, :, :], d["w_in"][:, 3 * HD:].rearrange("(k p) n -> p k n", p=P)
                                 ).then_inc(m.keep["wt_loaded"], 16)

        @block.gpsimd
        def _(pool):
            for u in range(2):
                for at in (0, gap + SEQ, 2 * gap + TOK):
                    last = nc.gpsimd.memset(padded[u][:, at:at + gap], 0.0)
            last.then_inc(zeroed, 1)
            for c in range(PARTS):
                u, h = c % 2, c % H
                if c >= H:
                    pool.wait_ge(normed if c < QK else kept, c + 1)
                    src = nrm[u] if c < QK else raw[u]
                    dst = d["k" if c < QK else "v"][:, :, h * P:(h + 1) * P].rearrange("t p n -> p t n")
                    pool.dma_start(dst, src[:, :, :]).then_inc(tok_stored[u], 16)
                if c < QK:
                    pool.wait_ge(rekept, groups(c + 1))
                    pool.dma_start(d["qT" if c < H else "kT"][h], back[u][:, 0:tiles(c) * P]).then_inc(ch_stored[u], 16)
            for u in range(2):
                pool.wait_ge(tok_stored[u], tok_count(PARTS, u))
                pool.wait_ge(ch_stored[u], 16 * (QK // 2))

        @block.tensor
        def _(pe):
            def project(c):
                pe.wait_ge(wm_loaded[c % 2], 16 * (c // 2 + 1))
                pe.wait_ge(evac, c)
                for b, n in ((0, NC), (1, NC), (2, CTX))[:2 if c < H else 3]:
                    for k in range(KD):
                        last = nc.tensor.matmul(m.bank(b, n), wm[c % 2][:, k, :], hT[:, k, b * NC:b * NC + n],
                                                start=(k == 0), stop=(k == KD - 1))
                last.then_inc(proj, 1)

            def turn(c):
                pe.wait_ge(silued, c + 1)
                pe.wait_ge(kept, c)
                for t in range(tiles(c)):
                    at = t * P + (gap if t >= TL else 0)
                    last = nc.tensor.transpose(m.psum[:, 3 * NC + t * P:3 * NC + (t + 1) * P],
                                               act_out[c % 2][:, at:at + P], ident)
                last.then_inc(turned, 1)

            def turn_back(c):
                pe.wait_ge(normed, c + 1)
                for g, t0 in enumerate(range(0, tiles(c), 4)):
                    n = groups(c) + g
                    if n >= 2:
                        pe.wait_ge(rekept, n - 1)
                    for t in range(t0, min(t0 + 4, tiles(c))):
                        last = nc.tensor.transpose(m.bank(6 + n % 2, P, (t - t0) * P), nrm[c % 2][:, t, :], ident)
                    last.then_inc(returned, 1)

            for c in range(PARTS + 1):
                if c < PARTS:
                    project(c)
                if 2 <= c < QK + 2:
                    turn_back(c - 2)
                if c:
                    turn(c - 1)

        @block.scalar
        def _(act):

            for c in range(PARTS + 1):
                if c < PARTS:
                    u = c % 2
                    act.wait_ge(proj, c + 1)
                    if c >= 2:
                        act.wait_ge(conved, c - 1)
                    if c >= H or c < 2:
                        src = m.psum[:, SEQ:TOK] if c >= H else hT[:, 0, SEQ:TOK]
                        nc.scalar.activation(padded[u][:, 2 * gap + SEQ:2 * gap + TOK], src, ACT.Copy)
                    nc.scalar.activation(padded[u][:, gap:gap + SEQ], m.psum[:, 0:SEQ], ACT.Copy).then_inc(evac, 1)
                if c:
                    b, u = c - 1, (c - 1) % 2
                    act.wait_ge(conved, b + 1)
                    if b >= 2:
                        act.wait_ge(turned, b - 1)
                    nc.scalar.activation(act_out[u][:, :], conv[u][:, :], ACT.Silu).then_inc(silued, 1)
                if 2 <= c < QK + 2:
                    b, u = c - 2, (c - 2) % 2
                    if b >= 2:
                        act.wait_ge(ch_stored[u], 16 * (b // 2))
                    for g, t0 in enumerate(range(0, tiles(b), 4)):
                        n = groups(b) + g
                        act.wait_ge(returned, n + 1)
                        w = (min(t0 + 4, tiles(b)) - t0) * P
                        nc.scalar.activation(back[u][:, t0 * P:t0 * P + w], m.bank(6 + n % 2, w), ACT.Copy
                                             ).then_inc(rekept, 1)
                if c:
                    b, u = c - 1, (c - 1) % 2
                    act.wait_ge(turned, b + 1)
                    if 2 <= b < QK + 2:
                        act.wait_ge(normed, b - 1)
                    if b - 2 >= QK:
                        act.wait_ge(tok_stored[u], tok_count(b - 1, u))
                    n = tiles(b)
                    nc.scalar.activation(raw[u][:, 0:n, :], m.psum[:, 3 * NC:3 * NC + n * P].rearrange("p (t n) -> p t n", n=P),
                                         ACT.Copy).then_inc(kept, 1)
                    if b < QK:
                        act.wait_ge(summed, b + 1)
                        nc.scalar.activation(sd[:, :], ssq[:, :], ACT.Sqrt, bias=m.keep["eps_norm"]).then_inc(rooted, 1)

        @block.vector
        def _(dve):
            link = Link(dve, own)
            dve.wait_ge(cw_loaded, 16)
            dve.wait_ge(zeroed, 1)
            for c in range(PARTS):
                if c < PARTS:
                    u = c % 2
                    dve.wait_ge(evac, c + 1)
                    if c >= 2:
                        dve.wait_ge(silued, c - 1)
                    y = conv[u][:, :]
                    link(nc.vector.tensor_scalar(y, padded[u][:, 0:wide], cw[:, c * CONV:c * CONV + 1], None, ALU.mult))
                    for j in range(1, CONV):
                        ins = nc.vector.scalar_tensor_tensor(y, padded[u][:, j:j + wide], cw[:, c * CONV + j:c * CONV + j + 1],
                                                             y, ALU.mult, ALU.add)
                        if j < CONV - 1:
                            link(ins)
                    ins.then_inc(conved, 1)
                if 1 <= c <= QK:
                    b, u = c - 1, (c - 1) % 2
                    n = tiles(b)
                    dve.wait_ge(kept, b + 1)
                    if b >= 2:
                        dve.wait_ge(returned, groups(b - 1))
                        if b - 2 >= H:
                            dve.wait_ge(tok_stored[u], tok_count(b - 1, u))
                    link(nc.vector.tensor_tensor(nrm[u][:, 0:n, :], raw[u][:, 0:n, :], raw[u][:, 0:n, :], ALU.mult))
                    if n < TT and b == 0:
                        link(nc.vector.memset(ssq[:, TL:TT], 1.0))
                    if b:
                        dve.wait_ge(rooted, b)
                    nc.vector.tensor_reduce(ssq[:, 0:n], nrm[u][:, 0:n, :], AX, ALU.add).then_inc(summed, 1)
                    dve.wait_ge(rooted, b + 1)
                    link(nc.vector.reciprocal(sd[:, :], sd[:, :]))
                    if b < H:
                        link(nc.vector.tensor_scalar(sd[:, :], sd[:, :], float(P) ** -0.5, None, ALU.mult))
                    nc.vector.tensor_tensor(nrm[u][:, 0:n, :], raw[u][:, 0:n, :], sd[:, 0:n].unsqueeze(2).to_broadcast([P, n, P]),
                                            ALU.mult).then_inc(normed, 1)
    m.top = top


def token_inputs(m):
    nc, d, ident, hT, wt = m.nc, m.dram, m.keep["ident"], m.keep["hT"], m.keep["wt"]
    top, m.limit = m.top, m.high
    dkT = m.keep["dkT"] = m.nc.alloc_sbuf_tensor_at("dkT", [P, H, TOK], F32, offset=m.high)
    dv = m.keep["dv"] = m.nc.alloc_sbuf_tensor_at("dv", [P, TT, HD], F32, offset=m.high + 4 * H * TOK)
    gates = m.keep["gates"] = m.nc.alloc_sbuf_tensor_at("gates", [P, TT, 16], F32, offset=m.high + 4 * (H * TOK + TT * HD))
    m.scratch("z", [TL, P, HD])
    m.scratch("dqT", [TL, P, HD])
    lhs = [m.sb(f"lhs{u}", [P, KD, P]) for u in range(2)]
    rope = m.sb("rope", [P, TL, 2, DK])
    qs = [m.sb(f"rope_{n}", [P, HD]) for n in ("qcos", "qsin", "q")]
    ks = [m.sb(f"rope_{n}", [P, HD]) for n in ("kcos", "ksin", "k")]
    zst = [m.sb(f"zst{u}", [P, HD]) for u in range(2)]
    qst = [m.sb(f"qst{u}", [P, HD]) for u in range(2)]
    rope_loaded, lhs_ready = m.sem("rope_loaded"), m.sem("d_lhs_ready")
    qk_proj, rest_kept = m.sem("d_qk_proj"), m.sem("d_rest_kept")
    qk_read, roped, turned, turned_kept = m.sem("d_qk_read"), m.sem("d_roped"), m.sem("d_turned"), m.sem("d_turned_kept")
    rest_proj = [m.sem(f"d_rest_proj{u}") for u in range(2)]
    z_stored = [m.sem(f"z_stored{u}") for u in range(2)]
    q_stored = [m.sem(f"q_stored{u}") for u in range(2)]
    own = m.sem("d_dve_link")
    Z, G, Q, K, V = 0, HD, HD + 16, 2 * HD + 16, 3 * HD + 16

    def tiles(eng, body):
        with eng.Fori(0, TL // 2) as i:
            for u in range(2):
                body(i, u, True)
        for u in range(2):
            body(TL // 2, u, False)

    with nc.Block() as block:
        @block.sync
        def _(sp):
            sp.dma_start(rope[:, :, :, :], d["rope"].rearrange("(t p) (f n) -> p t f n", p=P, f=2)).then_inc(rope_loaded, 16)
            with sp.Fori(0, TL // 2) as i:
                for u in range(2):
                    sp.wait_ge(rest_kept, 2 * i + u + 1)
                    sp.dma_start(flat(one(d["z"], 2 * i + u)), zst[u][:, :]).then_inc(z_stored[u], 16)
                    sp.wait_ge(turned_kept, 2 * i + u + 1)
                    sp.dma_start(flat(one(d["dqT"], 2 * i + u)), qst[u][:, :]).then_inc(q_stored[u], 16)
            for u in range(2):
                sp.wait_ge(z_stored[u], 16 * TL // 2)
                sp.wait_ge(q_stored[u], 16 * TL // 2)

        @block.gpsimd
        def _(pool):
            def body(i, u, latent):
                pool.wait_ge(rest_proj[u], i)
                nc.gpsimd.tensor_copy(lhs[u][:, :, :], hT[:, :, bass.ds((2 * i + u) * P, P)]).then_inc(lhs_ready, 1)
            tiles(pool, body)

        @block.tensor
        def _(pe):
            def group(b, u, at, n):
                for k in range(KD):
                    last = nc.tensor.matmul(m.bank(b, n), lhs[u][:, k, :], wt[:, k, at:at + n],
                                            start=(k == 0), stop=(k == KD - 1))
                return last

            def body(i, u, latent):
                t = 2 * i + u
                pe.wait_ge(lhs_ready, t + 1)
                pe.wait_ge(qk_read, t)
                if latent:
                    group(2, u, Q, HD)
                group(3, u, K, HD).then_inc(qk_proj, 1)
                pe.wait_ge(rest_kept, t)
                if latent:
                    group(0, u, Z, HD)
                group(1, u, V, HD)
                group(4, u, G, 16).then_inc(rest_proj[u], 1)
                pe.wait_ge(roped, t + 1)
                pe.wait_ge(turned_kept, t)
                for b, src in ((5, qs[2]), (6, ks[2])):
                    if latent or b == 6:
                        for h in range(H):
                            last = nc.tensor.transpose(m.bank(b, P, h * P), src[:, h * P:(h + 1) * P], ident)
                last.then_inc(turned, 1)

            pe.wait_ge(m.keep["wt_loaded"], 16)
            tiles(pe, body)

        @block.scalar
        def _(act):
            def body(i, u, latent):
                t = 2 * i + u
                act.wait_ge(rest_proj[u], i + 1)
                if latent:
                    act.wait_ge(z_stored[u], 16 * i)
                    nc.scalar.activation(zst[u][:, :], m.bank(0), ACT.Copy)
                nc.scalar.activation(cols(dv[:, bass.ds(t, 1), :]), m.bank(1), ACT.Copy)
                nc.scalar.activation(cols(gates[:, bass.ds(t, 1), :]), m.bank(4, 16), ACT.Copy).then_inc(rest_kept, 1)
                act.wait_ge(turned, t + 1)
                if latent:
                    act.wait_ge(q_stored[u], 16 * i)
                    nc.scalar.activation(qst[u][:, :], m.bank(5), ACT.Copy)
                nc.scalar.activation(dkT[:, :, bass.ds(t * P, P)], m.bank(6).rearrange("p (h n) -> p h n", h=H),
                                     ACT.Copy).then_inc(turned_kept, 1)
            tiles(act, body)

        @block.vector
        def _(dve):
            def heads(ap):
                return ap.rearrange("p (h n) -> p h n", n=DK)

            def rotate(out, c, s):
                o, c, s = (x[:, :].rearrange("p (h a n) -> p h a n", a=2, n=16) for x in (out, c, s))
                nc.vector.tensor_tensor(o[:, :, 0, :], c[:, :, 0, :], s[:, :, 1, :], ALU.subtract)
                return nc.vector.tensor_tensor(o[:, :, 1, :], c[:, :, 1, :], s[:, :, 0, :], ALU.add)

            dve.wait_ge(rope_loaded, 16)
            with dve.Fori(0, TL // 2) as i:
                for u in range(2):
                    t = 2 * i + u
                    dve.wait_ge(qk_proj, t + 1)
                    for b, (c, s, _) in ((2, qs), (3, ks)):
                        for f, x in enumerate((c, s)):
                            table = rope[:, bass.ds(t, 1), f, :].to_broadcast([P, 2 * H, DK])
                            last = nc.vector.tensor_tensor(heads(x[:, :]), heads(m.bank(b)), table, ALU.mult)
                    last.then_inc(qk_read, 1)
                    dve.wait_ge(qk_read, t + 1)
                    dve.wait_ge(turned, t)
                    rotate(qs[2], qs[0], qs[1])
                    rotate(ks[2], ks[0], ks[1]).then_inc(roped, 1)
                    dve.wait_ge(roped, t + 1)
            for u in range(2):
                t = TL + u
                dve.wait_ge(qk_proj, t + 1)
                dve.wait_ge(turned, t)
                nc.vector.tensor_copy(ks[2][:, :], m.bank(3)).then_inc(roped, 1)
                dve.wait_ge(roped, t + 1)
                dve.sem_inc(qk_read, 1)
    m.top = top


class Events:

    def __init__(self, m, label, names):
        self.names = names.split()
        self.sems = [m.sem(f"{label}_{way}") for way in ("forward", "reverse")]

    def at(self, name, s):
        return s * len(self.names) + self.names.index(name) + 1

    def done(self, ins, name, r):
        assert name in self.names
        ins.then_inc(self.sems[r], 1)

    def wait(self, eng, name, r, s):
        eng.wait_ge(self.sems[r], self.at(name, s))

    def wait_last(self, eng, name, r, s):
        if isinstance(s, int) and s == 0:
            return
        eng.wait_ge(self.sems[r], self.at(name, s - 1))


GATE_KINDS = 7
G_G, G_BETA, G_NGC, G_NEGC, G_EGC, G_ETOT, G_TAIL = range(GATE_KINDS)


def delta_gates(m):
    nc, d = m.nc, m.dram
    gates, tri, ones = m.keep["gates"], m.keep["tri"], m.keep["ones"]
    m.top = m.base
    G = m.keep["G"] = m.sb("G", [P, 2, TT, GATE_KINDS, H])
    top = m.top
    rg = m.sb("rg", [P, 2, 2, H])
    a = m.sb("ga", [P, 2, TT, H])
    b = m.sb("gb", [P, 2, TT, H])
    e = m.sb("ge", [P, 2, TT, H])
    gc = m.sb("ggc", [P, 2, 2, TT, H])
    loaded, dve_did, act_did, sums = m.sem("g_loaded"), m.sem("g_dve"), m.sem("g_act"), m.sem("g_sums")

    def gate(raw, r):
        return raw.rearrange("p t (k r h) -> p t k r h", k=2, r=2)[:, :, :, r, :]

    with nc.Block() as block:
        @block.sync
        def _(sp):
            sp.dma_start(rg[:, :, :, :], d["rep_gates"].rearrange("p (w r h) -> p w r h", w=2, r=2)).then_inc(loaded, 16)

        @block.vector
        def _(dve):
            link = Link(dve, dve_did)
            cp = nc.vector.tensor_copy
            dve.wait_ge(loaded, 16)
            for k, dst in ((0, b), (1, a)):
                cp(dst[:, 0, TC:TT, :], gate(gates, 0)[:, 0:TL, k, :])
                cp(dst[:, 0, 0:TC, :], gate(gates, 0)[:, TL:TT, k, :])
                for s in range(TT):
                    last = cp(dst[:, 1, s, :], gate(gates, 1)[:, TT - 1 - s, k, :])
            link(last)
            link(nc.vector.tensor_tensor(a[:, :, :, :], a[:, :, :, :], rg[:, 0, :, :].unsqueeze(2).to_broadcast([P, 2, TT, H]),
                                         ALU.add))
            link(nc.vector.tensor_scalar(e[:, :, :, :], a[:, :, :, :], -1.0, None, ALU.mult))
            link(nc.vector.tensor_tensor(e[:, :, :, :], e[:, :, :, :], a[:, :, :, :], ALU.min))
            dve.wait_ge(act_did, 4)
            nc.vector.tensor_scalar(a[:, :, :, :], a[:, :, :, :], 0.0, None, ALU.max)
            link(nc.vector.tensor_copy(G[:, :, :, G_BETA, :], b[:, :, :, :]))
            link(nc.vector.tensor_tensor(a[:, :, :, :], a[:, :, :, :], e[:, :, :, :], ALU.add))
            link(nc.vector.tensor_tensor(a[:, :, :, :], a[:, :, :, :], rg[:, 1, :, :].unsqueeze(2).to_broadcast([P, 2, TT, H]),
                                         ALU.mult))
            link(nc.vector.tensor_scalar(a[:, :, :, :], a[:, :, :, :], -1.0, None, ALU.mult))
            nc.vector.tensor_copy(G[:, :, :, G_G, :], a[:, :, :, :])
            dve.wait_ge(sums, 1)
            link(nc.vector.tensor_copy(gc[:, :, :, :, :], m.bank(0, 4 * TT * H).rearrange("p (w r t h) -> p w r t h", w=2, r=2, h=H)))
            link(nc.vector.tensor_scalar(G[:, :, :, G_NGC, :], gc[:, 0], -1.0, None, ALU.mult))
            link(nc.vector.tensor_tensor(e[:, :, :, :], gc[:, 1], gc[:, 0], ALU.subtract))
            dve.wait_ge(act_did, 7)
            nc.vector.tensor_scalar(G[:, :, :, G_NEGC, :], G[:, :, :, G_EGC, :], -1.0, None, ALU.mult)

        @block.scalar
        def _(act):
            link = Link(act, act_did)
            act.wait_ge(dve_did, 4)
            link(nc.scalar.activation(e[:, :, :, :], e[:, :, :, :], ACT.Exp))
            link(nc.scalar.activation(rg[:, 1, :, :], rg[:, 1, :, :], ACT.Exp))
            link(nc.scalar.activation(e[:, :, :, :], e[:, :, :, :], ACT.Ln, bias=1.0))
            link(nc.scalar.activation(b[:, :, :, :], b[:, :, :, :], ACT.Sigmoid))
            act.wait_ge(dve_did, 11)
            link(nc.scalar.activation(G[:, :, :, G_EGC, :], gc[:, 0], ACT.Exp))
            link(nc.scalar.activation(G[:, :, :, G_ETOT, :], gc[:, 1], ACT.Exp))
            link(nc.scalar.activation(G[:, :, :, G_TAIL, :], e[:, :, :, :], ACT.Exp))

        @block.tensor
        def _(pe):
            pe.wait_ge(dve_did, 8)
            n = TT * H
            for w in range(2):
                for r in range(2):
                    last = nc.tensor.matmul(m.bank(0, n, (2 * w + r) * n), ones if w else tri[r],
                                            a[:, r].rearrange("p t h -> p (t h)"), start=True, stop=True)
            last.then_inc(sums, 1)
    m.top = top


def delta_rule(m):
    nc, d = m.nc, m.dram
    BF = mybir.dt.bfloat16
    G, ident, ones, tri, level, neg = (m.keep[n] for n in ("G", "ident", "ones", "tri", "level", "neg"))
    top = m.top
    R2 = range(2)
    m.scratch("o", [2, TT, P, HD])
    W = [P, H, P]
    Q32 = P // 4

    def both(name, shape=W, dt=F32):
        return [m.sb(f"{name}{r}", shape, dt) for r in R2]

    def twice(name):
        return [[m.sb(f"{name}{r}{u}", W) for u in R2] for r in R2]

    kT, qT, kt, vt = twice("e_kT"), twice("e_qT"), twice("e_k"), twice("e_v")
    TTf, attn = twice("e_TT"), twice("e_attn")
    am = twice("e_am")
    tg, dec, at = both("e_tg"), both("e_dec"), both("e_at")
    Tf, pf, R, vn, vn2, osb, S = (both("e_" + n) for n in ("T", "pf", "R", "vn", "vn2", "o", "S"))
    Tc, TTc, pc = (both("e_" + n, [P, H, Q32]) for n in ("Tc", "TTc", "pc"))
    identc = m.sb("identc", [P, Q32])
    quad = m.sb("quad", [P, P])
    nego = m.sb("nego", [P, 2, H, P], BF)
    identb = m.sb("identb", [P, P], BF)
    quad_loaded = m.sem("quad_loaded")
    A, B, C, Sb = (lambda r: r), (lambda r: 2 + r), (lambda r: 4 + r), (lambda r: 6 + r)

    loaded = [[m.sem(f"e_loaded{r}{u}") for u in R2] for r in R2]
    stored = [m.sem(f"o_stored{r}") for r in R2]
    own, ready = m.sem("e_dve_link"), m.sem("e_ready")
    pool_prep = Events(m, "e_pool_prep", "TG " + " ".join(f"AM{lv}" for lv in range(LEVELS)))
    pe_prep = Events(m, "e_pe_prep", "RB KK P0 P1 X1 P2 X2 P3 X3 P4 X4 P5 X5 Y5 KQ P6 Y6")
    act_prep = Events(m, "e_act_prep", "dec P1 P2 P3 P4 P5 P6")
    dve_prep = Events(m, "e_dve_prep", "AT Tc0 T0 Tc1 T1 Tc2 T2 Tc3 T3 Tc4 T4 Tf T5 attn TT")
    pe_scan = Events(m, "e_pe_scan", "KS QS TR AV KV")
    act_scan = Events(m, "e_act_scan", "QS vn2")
    dve_scan = Events(m, "e_dve_scan", "R vn S o")

    def gs(r, s, kind, h=None):
        g = G[:, r, bass.ds(s, 1), kind, :].rearrange("p t h -> p (t h)")
        return g if h is None else g[:, h:h + 1]

    def heads(b, n=P):
        return m.bank(b, H * n).rearrange("p (h n) -> p h n", h=H)

    def halves(ap, b, later):
        v = ap.rearrange("p (g t n) -> p g t n", t=2, n=b)
        return v[:, :, int(later), :]

    def halves_h(ap, b, later):
        v = ap.rearrange("p h (g t n) -> p h g t n", t=2, n=b)
        return v[:, :, :, int(later), :]

    def rounds(eng, order, stages, link=None, links=0):
        def run(s_scan, s_prep):
            for name in order.split():
                kind, s = ("scan", s_scan) if name.startswith("*") else ("prep", s_prep)
                if s is not None:
                    for r in R2:
                        stages[kind, name.lstrip("*")](r, *s)

        link = link or Link(eng, None)
        run(None, (0, 0))
        run((0, 0), (1, 1))
        run((1, 1), (2, 0))
        with link.loop(TT // 2 - 2, 2 * links) as i:
            run((2 * i + 2, 0), (2 * i + 3, 1))
            run((2 * i + 3, 1), (2 * i + 4, 0))
        run((TT - 2, 0), (TT - 1, 1))
        run((TT - 1, 1), None)

    with nc.Block() as block:
        @block.sync
        def _(sp):
            sp.dma_start(quad[:, :], d["quad"][:, 0:P]).then_inc(quad_loaded, 16)
            sp.dma_start(identc[:, :], d["quad"][:, P:P + Q32]).then_inc(quad_loaded, 16)

            def load(r, u, q_src, t, s):
                span = bass.ds(t * P, P)
                for h_src, dst in ((d["kT"], kT), (q_src, qT)):
                    sp.dma_start(dst[r][u][:, :, :], h_src[:, :, span].rearrange("h p n -> p h n")).then_inc(loaded[r][u], 16)
                for src, dst in ((d["k"], kt), (d["v"], vt)):
                    sp.dma_start(dst[r][u][:, :, :], flat(one(src, t)).rearrange("p (h n) -> p h n", h=H)
                                 ).then_inc(loaded[r][u], 16)

            def store(r, s):
                dve_scan.wait(sp, "o", r, s)
                sp.dma_start(flat(one(d["o"][r], s)), osb[r][:, :, :].rearrange("p h n -> p (h n)")).then_inc(stored[r], 16)

            for s in R2:
                for r in R2:
                    load(r, s, d["kT"], TL + s if r == 0 else TT - 1 - s, s)
            with sp.Fori(0, TL // 2) as i:
                mirrored = [i * -2 + (TL - 1 - u) for u in R2]
                for u in R2:
                    s = 2 * i + u
                    for r in R2:
                        pe_scan.wait(sp, "KV", r, s)
                        load(r, u, d["qT"], s if r == 0 else mirrored[u], s)
                        store(r, s)
            for s in (TL, TL + 1):
                for r in R2:
                    store(r, s)
            for r in R2:
                sp.wait_ge(stored[r], 16 * TT)

        @block.gpsimd
        def _(pool):
            def TG(r, s, u):
                pe_prep.wait_last(pool, "RB", r, s)
                ins = nc.gpsimd.tensor_tensor(tg[r][:, :, :], tri[r].unsqueeze(1).to_broadcast(W),
                                              gs(r, s, G_G).unsqueeze(2).to_broadcast(W), ALU.mult)
                pool_prep.done(ins, "TG", r)

            def masked(lv):
                def AM(r, s, u):
                    if lv == 0:
                        dve_prep.wait(pool, "AT", r, s)
                    if lv < 2:
                        pe_prep.wait_last(pool, "P6" if lv == 0 else "P5", r, s)
                    else:
                        pe_prep.wait(pool, f"P{lv - 2}", r, s)
                    ins = nc.gpsimd.tensor_tensor(am[r][lv % 2][:, :, :], at[r][:, :, :],
                                                  level[r][lv].unsqueeze(1).to_broadcast(W), ALU.mult)
                    pool_prep.done(ins, f"AM{lv}", r)
                return AM

            stages = {("prep", "TG"): TG} | {("prep", f"AM{lv}"): masked(lv) for lv in range(LEVELS)}
            rounds(pool, "TG " + " ".join(f"AM{lv}" for lv in range(LEVELS)), stages)

        @block.tensor
        def _(pe):
            mm = nc.tensor.matmul

            def each(out, lhsT, rhs):
                for h in range(H):
                    last = mm(out(h), lhsT(h), rhs(h), start=True, stop=True)
                return last

            def RB(r, s, u):
                pool_prep.wait(pe, "TG", r, s)
                dve_prep.wait_last(pe, "TT", r, s)
                mm(m.bank(A(r)), identb[:, :], nego[:, r, :, :].rearrange("p h n -> p (h n)"), start=True, stop=False)
                pe_prep.done(mm(m.bank(A(r)), ones, tg[r][:, :, :].rearrange("p h n -> p (h n)"), start=False, stop=True),
                             "RB", r)

            def KK(r, s, u):
                pe.wait_ge(loaded[r][u], (s - u) * 32 + 64)
                dve_prep.wait_last(pe, "T5", r, s)
                k = kT[r][u]
                pe_prep.done(each(lambda h: heads(B(r))[:, h, :], lambda h: k[:, h, :], lambda h: k[:, h, :]), "KK", r)

            def KQ(r, s, u):
                dve_scan.wait_last(pe, "o", r, s)
                pe_prep.done(each(lambda h: heads(C(r))[:, h, :], lambda h: kT[r][u][:, h, :], lambda h: qT[r][u][:, h, :]),
                             "KQ", r)

            def product(lv):
                def PL(r, s, u):
                    pool_prep.wait(pe, f"AM{lv}", r, s)
                    a = am[r][lv % 2]
                    if lv == 0:
                        act_prep.wait(pe, "dec", r, s)
                        last = each(lambda h: heads(A(r), Q32)[:, h, :], lambda h: a[:, h, :], lambda h: identc[:, :])
                    elif lv < 5:
                        dve_prep.wait(pe, f"Tc{lv - 1}", r, s)
                        last = each(lambda h: heads(A(r), Q32)[:, h, :], lambda h: a[:, h, :], lambda h: Tc[r][:, h, :])
                    else:
                        dve_prep.wait(pe, "Tf" if lv == 5 else "T5", r, s)
                        last = each(lambda h: heads(A(r))[:, h, :], lambda h: a[:, h, :], lambda h: Tf[r][:, h, :])
                    pe_prep.done(last, f"P{lv}", r)
                return PL

            def left(lv):
                def XL(r, s, u):
                    act_prep.wait(pe, f"P{lv}", r, s)
                    dve_prep.wait(pe, f"T{lv - 1}", r, s)
                    if lv < 5:
                        last = each(lambda h: heads(B(r), Q32)[:, h, :], lambda h: TTf[r][u][:, h, :], lambda h: pc[r][:, h, :])
                    else:
                        last = each(lambda h: heads(B(r), P // 2)[:, h, :], lambda h: TTf[r][u][:, h, :],
                                    lambda h: halves(pf[r][:, h, :], 32, r == 1))
                    pe_prep.done(last, f"X{lv}", r)
                return XL

            def right(lv):
                def YL(r, s, u):
                    act_prep.wait(pe, f"P{lv}", r, s)
                    last = each(lambda h: heads(A(r), P // 2)[:, h, :], lambda h: pf[r][:, h, :],
                                lambda h: halves(TTf[r][u][:, h, :], 1 << lv, r == 0))
                    pe_prep.done(last, f"Y{lv}", r)
                return YL

            def KS(r, s, u):
                dve_scan.wait_last(pe, "S", r, s)
                pe_scan.done(each(lambda h: heads(Sb(r))[:, h, :], lambda h: kT[r][u][:, h, :], lambda h: S[r][:, h, :]), "KS", r)

            def QS(r, s, u):
                dve_prep.wait(pe, "attn", r, s)
                pe_scan.done(each(lambda h: heads(C(r))[:, h, :], lambda h: qT[r][u][:, h, :], lambda h: S[r][:, h, :]), "QS", r)

            def TR(r, s, u):
                dve_scan.wait(pe, "R", r, s)
                dve_prep.wait(pe, "TT", r, s)
                pe_scan.done(each(lambda h: heads(Sb(r))[:, h, :], lambda h: TTf[r][u][:, h, :], lambda h: R[r][:, h, :]), "TR", r)

            def AV(r, s, u):
                dve_scan.wait(pe, "vn", r, s)
                act_scan.wait(pe, "QS", r, s)
                pe_scan.done(each(lambda h: heads(C(r))[:, h, :], lambda h: attn[r][u][:, h, :], lambda h: vn[r][:, h, :]), "AV", r)

            def KV(r, s, u):
                act_scan.wait(pe, "vn2", r, s)
                pe_scan.done(each(lambda h: heads(Sb(r))[:, h, :], lambda h: kt[r][u][:, h, :], lambda h: vn2[r][:, h, :]), "KV", r)

            stages = {("prep", "RB"): RB, ("prep", "KK"): KK, ("prep", "KQ"): KQ, ("prep", "X5"): left(5),
                      ("prep", "Y5"): right(5), ("prep", "Y6"): right(6), ("scan", "KS"): KS, ("scan", "QS"): QS,
                      ("scan", "TR"): TR, ("scan", "AV"): AV, ("scan", "KV"): KV}
            stages |= {("prep", f"P{lv}"): product(lv) for lv in range(LEVELS)}
            stages |= {("prep", f"X{lv}"): left(lv) for lv in range(1, 5)}
            pe.wait_ge(ready, 1)
            pe.wait_ge(quad_loaded, 32)
            rounds(pe, "RB KK *KS *QS P0 P1 X1 *TR P2 X2 P3 X3 *AV *KV P4 X4 P5 X5 Y5 KQ P6 Y6", stages)

        @block.scalar
        def _(act):
            def dec_(r, s, u):
                pe_prep.wait(act, "RB", r, s)
                dve_prep.wait_last(act, "attn", r, s)
                for h in range(H):
                    last = nc.scalar.activation(dec[r][:, h, :], heads(A(r))[:, h, :], ACT.Exp, bias=gs(r, s, G_NGC, h))
                act_prep.done(last, "dec", r)

            def copy(lv):
                def CP(r, s, u):
                    pe_prep.wait(act, f"P{lv}", r, s)
                    if lv == 1:
                        pe_prep.wait_last(act, "X4", r, s)
                    elif lv == 5:
                        pe_prep.wait_last(act, "Y6", r, s)
                    src, dst = (heads(A(r), Q32), pc[r]) if lv < 5 else (heads(A(r)), pf[r])
                    act_prep.done(nc.scalar.activation(dst[:, :, :], src, ACT.Copy), f"P{lv}", r)
                return CP

            def QS(r, s, u):
                pe_scan.wait(act, "QS", r, s)
                act.wait_ge(stored[r], s * 16)
                for h in range(H):
                    last = nc.scalar.activation(osb[r][:, h, :], heads(C(r))[:, h, :], ACT.Copy, scale=gs(r, s, G_EGC, h))
                act_scan.done(last, "QS", r)

            def vn2_(r, s, u):
                dve_scan.wait(act, "vn", r, s)
                pe_scan.wait_last(act, "KV", r, s)
                for h in range(H):
                    last = nc.scalar.activation(vn2[r][:, h, :], vn[r][:, h, :], ACT.Copy, scale=gs(r, s, G_TAIL, h))
                act_scan.done(last, "vn2", r)

            stages = {("prep", "dec"): dec_, ("scan", "QS"): QS, ("scan", "vn2"): vn2_}
            stages |= {("prep", f"P{lv}"): copy(lv) for lv in range(1, LEVELS)}
            rounds(act, "dec *QS P1 *vn2 P2 P3 P4 P5 P6", stages)

        @block.vector
        def _(dve):
            link = Link(dve, own)
            tt, cp, stt = nc.vector.tensor_tensor, nc.vector.tensor_copy, nc.vector.scalar_tensor_tensor
            cp(nego[:, 0, :, :], neg[0].unsqueeze(1).to_broadcast(W))
            cp(nego[:, 1, :, :], neg[1].unsqueeze(1).to_broadcast(W))
            for r in R2:
                nc.vector.memset(S[r][:, :, :], 0.0)
            cp(identb[:, :], ident).then_inc(ready, 1)
            dve.wait_ge(quad_loaded, 32)

            def AT(r, s, u):
                pe_prep.wait(dve, "KK", r, s)
                act_prep.wait(dve, "dec", r, s)
                pool_prep.wait_last(dve, "AM6", r, s)
                for h in range(H):
                    last = stt(at[r][:, h, :], heads(B(r))[:, h, :], gs(r, s, G_BETA, h), dec[r][:, h, :], ALU.mult, ALU.mult)
                dve_prep.done(last, "AT", r)

            def spread(dst, src):
                return tt(dst[:, :, :].rearrange("p h (q n) -> p h q n", q=4), src[:, :, :].unsqueeze(2).to_broadcast([P, H, 4, Q32]),
                          quad[:, :].rearrange("p (q n) -> p q n", q=4).unsqueeze(1).to_broadcast([P, H, 4, Q32]), ALU.mult)

            def doubled(lv):
                def TL_(r, s, u):
                    if lv == 0:
                        pe_prep.wait(dve, "P0", r, s)
                        new = tt(Tc[r][:, :, :], identc[:, :].unsqueeze(1).to_broadcast([P, H, Q32]), heads(A(r), Q32), ALU.subtract)
                        dve_prep.done(new, "Tc0", r)
                    else:
                        pe_prep.wait(dve, f"X{lv}", r, s)
                        dve_prep.done(tt(Tc[r][:, :, :], Tc[r][:, :, :], heads(B(r), Q32), ALU.subtract), f"Tc{lv}", r)
                    dve_prep.wait(dve, f"Tc{lv}", r, s)
                    link(nc.vector.transpose(TTc[r][:, :, :].rearrange("p h n -> p (h n)"),
                                             Tc[r][:, :, :].rearrange("p h n -> p (h n)")))
                    if lv == 0 and not (isinstance(s, int) and s < 2):
                        pe_scan.wait(dve, "TR", r, s - 2)
                    dve_prep.done(spread(TTf[r][u], TTc[r]), f"T{lv}", r)
                return TL_

            def Tf_(r, s, u):
                dve_prep.done(spread(Tf[r], Tc[r]), "Tf", r)

            def T5(r, s, u):
                pe_prep.wait(dve, "Y5", r, s)
                dve_prep.wait(dve, "Tf", r, s)
                for dst, b, later in ((Tf[r], B(r), r == 1), (TTf[r][u], A(r), r == 0)):
                    for h in range(H):
                        v = halves(dst[:, h, :], 32, later)
                        last = tt(v, v, m.bank(b, P // 2, h * P // 2).rearrange("p (g n) -> p g n", g=2), ALU.subtract)
                dve_prep.done(last, "T5", r)

            def TT_(r, s, u):
                pe_prep.wait(dve, "Y6", r, s)
                v = halves_h(TTf[r][u][:, :, :], 64, r == 0).rearrange("p h g n -> p h (g n)")
                dve_prep.done(tt(v, v, heads(A(r), P // 2), ALU.subtract), "TT", r)

            def attn_(r, s, u):
                pe_prep.wait(dve, "KQ", r, s)
                if not (isinstance(s, int) and s < 2):
                    pe_scan.wait(dve, "AV", r, s - 2)
                dve_prep.done(tt(attn[r][u][:, :, :], heads(C(r)), dec[r][:, :, :], ALU.mult), "attn", r)

            def R_(r, s, u):
                pe_scan.wait(dve, "KS", r, s)
                pe_scan.wait_last(dve, "TR", r, s)
                for h in range(H):
                    last = stt(R[r][:, h, :], heads(Sb(r))[:, h, :], gs(r, s, G_NEGC, h), vt[r][u][:, h, :], ALU.mult, ALU.add)
                dve_scan.done(last, "R", r)

            def vn_(r, s, u):
                pe_scan.wait(dve, "TR", r, s)
                dve_scan.done(tt(vn[r][:, :, :], heads(Sb(r)), gs(r, s, G_BETA).unsqueeze(2).to_broadcast(W), ALU.mult), "vn", r)

            def S_(r, s, u):
                pe_scan.wait(dve, "KV", r, s)
                for h in range(H):
                    last = stt(S[r][:, h, :], S[r][:, h, :], gs(r, s, G_ETOT, h), heads(Sb(r))[:, h, :], ALU.mult, ALU.add)
                dve_scan.done(last, "S", r)

            def o_(r, s, u):
                pe_scan.wait(dve, "AV", r, s)
                dve_scan.done(tt(osb[r][:, :, :], osb[r][:, :, :], heads(C(r)), ALU.add), "o", r)

            stages = {("prep", "AT"): AT, ("prep", "Tf"): Tf_, ("prep", "T5"): T5, ("prep", "TT"): TT_, ("prep", "attn"): attn_,
                      ("scan", "R"): R_, ("scan", "vn"): vn_, ("scan", "S"): S_, ("scan", "o"): o_}
            stages |= {("prep", f"T{lv}"): doubled(lv) for lv in range(5)}
            rounds(dve, "AT *R T0 T1 *vn T2 T3 *S *o T4 Tf T5 attn TT", stages, link, 2 * 5)
    m.top = top


def attention(m):
    nc, d, ident = m.nc, m.dram, m.keep["ident"]
    dkT, dv = m.keep["dkT"], m.keep["dv"]
    top = m.top
    m.scratch("od", [TL, P, HD])
    SC = float(DK) ** -0.5
    lamr = m.sb("lamr", [P, 4, DK])
    lprod = m.sb("lprod", [P, 2, DK])
    lsum = m.sb("lsum", [P, 2])
    nlam = m.sb("nlam", [P, 1])
    qT = [m.sb(f"f_qT{u}", [P, H, P]) for u in range(2)]
    E = [[m.sb(f"f_E{p}{c}", [P, TOK]) for c in range(2)] for p in range(2)]
    A = [m.sb(f"f_A{p}", [P, TOK]) for p in range(2)]
    AT = [m.sb(f"f_AT{p}", [P, TT, P]) for p in range(2)]
    mx = [[m.sb(f"f_mx{p}{c}", [P, 1]) for c in range(2)] for p in range(2)]
    rs = [[m.sb(f"f_rs{p}{c}", [P, 1]) for c in range(2)] for p in range(2)]
    cf = m.sb("f_cf", [P, 1])
    r1 = [m.sb(f"f_r1{u}", [P, H]) for u in range(2)]
    ob = [m.sb(f"f_o{u}", [P, H, P]) for u in range(2)]
    lam_loaded, dve_lam, act_lam = m.sem("lam_loaded"), m.sem("lam_dve"), m.sem("lam_act")
    q_loaded = [m.sem(f"f_q_loaded{u}") for u in range(2)]
    stored = [m.sem(f"f_stored{u}") for u in range(2)]
    shared = m.sem("f_shared_bank")
    scored, maxed = m.sem("f_scored"), m.sem("f_maxed")
    exped = [m.sem(f"f_exped{c}") for c in range(2)]
    mixed, summed, tile_kept = m.sem("f_mixed"), m.sem("f_summed"), m.sem("f_tile_kept")
    turned = [m.sem(f"f_turned{p}") for p in range(2)]
    kept = [m.sem(f"f_kept{b}") for b in range(2)]
    own = m.sem("f_dve_link")
    GROUPS = [(0, 4), (4, 4), (8, 2)]

    def tiles(eng, body, link=None, links=0):
        link = link or Link(eng, None)
        with link.loop(TL // 2 - 1, 2 * links) as i:
            for u in range(2):
                body(2 * i + u, i, u, False)
        body(TL - 2, TL // 2 - 1, 0, False)
        body(TL - 1, TL // 2 - 1, 1, True)

    with nc.Block() as block:
        @block.sync
        def _(sp):
            sp.dma_start(lamr[:, :, :], d["rep_lambda"].rearrange("p (a n) -> p a n", n=DK)).then_inc(lam_loaded, 16)

            def load(t, i, u):
                sp.dma_start(qT[u][:, :, :], flat(one(d["dqT"], t)).rearrange("p (h n) -> p h n", h=H)).then_inc(q_loaded[u], 16)

            def store(t, u):
                sp.wait_ge(tile_kept, t + 1)
                sp.dma_start(flat(one(d["od"], t)), ob[u][:, :, :].rearrange("p h n -> p (h n)")).then_inc(stored[u], 16)

            load(0, 0, 0)
            load(1, 0, 1)
            with sp.Fori(0, TL // 2 - 1) as i:
                for u in range(2):
                    t = 2 * i + u
                    store(t, u)
                    load(t + 2, i, u)
            for t in (TL - 2, TL - 1):
                store(t, t % 2)
            for u in range(2):
                sp.wait_ge(stored[u], 16 * (TL // 2))

        @block.tensor
        def _(pe):
            def score(n, u, h):
                def piece(c, at, key, w):
                    rows = slice(c * DK, (c + 1) * DK)
                    return nc.tensor.matmul(m.psum[:, at:at + w], qT[u][rows, h, :], dkT[rows, h, key:key + w],
                                            start=True, stop=True)

                pe.wait_ge(exped[0], n)
                piece(0, 0, 0, NC)
                piece(0, NC, NC, NC)
                pe.wait_ge(exped[1], n)
                piece(0, 2 * NC, 2 * NC, CTX).then_inc(shared, 1)
                piece(1, 3 * NC, CTX, NC)
                piece(1, 4 * NC, CTX + NC, NC)
                pe.wait_ge(shared, n + 1)
                piece(1, TOK, 0, CTX).then_inc(scored, 1)

            def apply(n, h):
                pe.wait_ge(mixed, n + 1)
                for g, (t0, w) in enumerate(GROUPS):
                    pe.wait_ge(kept[g % 2], n if g == 1 else 2 * n + g // 2)
                    for t in range(t0, t0 + w):
                        last = nc.tensor.transpose(m.bank(5 + g % 2, P, (t - t0) * P), A[h % 2][:, t * P:(t + 1) * P], ident)
                    last.then_inc(turned[h % 2], 1)
                pe.wait_ge(kept[0], 2 * n + 2)
                pe.wait_ge(kept[1], n + 1)
                for t in range(TT):
                    last = nc.tensor.matmul(m.bank(7, P, h * P), AT[h % 2][:, t, :], dv[:, t, h * P:(h + 1) * P],
                                            start=(t == 0), stop=(t == TT - 1))
                last.then_inc(summed, 1)

            def body(t, i, u, final):
                for h in range(H):
                    n = t * H + h
                    if h < H - 1:
                        score(n + 1, u, h + 1)
                    elif not final:
                        pe.wait_ge(q_loaded[1 - u], 16 * (i + u) + 16)
                        score(n + 1, 1 - u, 0)
                    if h == 0:
                        pe.wait_ge(tile_kept, t)
                    apply(n, h)

            pe.wait_ge(q_loaded[0], 16)
            score(0, 0, 0)
            tiles(pe, body)

        @block.scalar
        def _(act):
            act.wait_ge(dve_lam, 2)
            nc.scalar.activation(lsum[:, :], lsum[:, :], ACT.Exp).then_inc(act_lam, 1)

            def exps(n, h):
                for c in range(2):
                    act.wait_ge(maxed, n + 1)
                    nc.scalar.activation(E[h % 2][c][:, :], m.psum[:, c * TOK:(c + 1) * TOK], ACT.Exp, bias=mx[h % 2][c][:, :],
                                         scale=SC, accum_out=rs[h % 2][c][:, :]).then_inc(exped[c], 1)

            def keep(t, h):
                for g, (t0, w) in enumerate(GROUPS):
                    act.wait_ge(turned[h % 2], 3 * (t * (H // 2) + h // 2) + g + 1)
                    nc.scalar.activation(AT[h % 2][:, t0:t0 + w, :].rearrange("p t n -> p (t n)"), m.bank(5 + g % 2, w * P), ACT.Copy
                                         ).then_inc(kept[g % 2], 1)

            def body(t, i, u, final):
                for h in range(H):
                    n = t * H + h
                    if h < H - 1 or not final:
                        exps(n + 1, (h + 1) % H)
                    keep(t, h)

            exps(0, 0)
            tiles(act, body)

        @block.vector
        def _(dve):
            link = Link(dve, own)
            dve.wait_ge(lam_loaded, 16)
            for w in range(2):
                last = nc.vector.tensor_tensor(lprod[:, w, :], lamr[:, 2 * w, :], lamr[:, 2 * w + 1, :], ALU.mult)
            last.then_inc(dve_lam, 1)
            dve.wait_ge(dve_lam, 1)
            nc.vector.tensor_reduce(lsum[:, :], lprod[:, :, :], AX, ALU.add).then_inc(dve_lam, 1)
            dve.wait_ge(act_lam, 1)
            link(nc.vector.tensor_tensor(nlam[:, :], lsum[:, 1:2], lsum[:, 0:1], ALU.subtract))
            link(nc.vector.tensor_scalar(nlam[:, :], nlam[:, :], -LAM_INIT, None, ALU.add))

            def maxes(n, h):
                for c in range(2):
                    dve.wait_ge(scored, n + 1)
                    link(nc.vector.tensor_reduce(mx[h % 2][c][:, :], m.psum[:, c * TOK:(c + 1) * TOK], AX, ALU.max))
                    last = nc.vector.tensor_scalar(mx[h % 2][c][:, :], mx[h % 2][c][:, :], -SC, None, ALU.mult)
                last.then_inc(maxed, 1)

            def mix(t, n, h, u):
                dve.wait_ge(exped[1], n + 1)
                nc.vector.reciprocal(r1[u][:, h:h + 1], rs[h % 2][0][:, :])
                link(nc.vector.reciprocal(cf[:, :], rs[h % 2][1][:, :]))
                link(nc.vector.scalar_tensor_tensor(cf[:, :], rs[h % 2][0][:, :], nlam[:, :], cf[:, :], ALU.mult, ALU.mult))
                dve.wait_ge(turned[h % 2], 3 * (t * (H // 2) + h // 2))
                nc.vector.scalar_tensor_tensor(A[h % 2][:, :], E[h % 2][1][:, :], cf[:, :], E[h % 2][0][:, :], ALU.mult, ALU.add
                                               ).then_inc(mixed, 1)

            def body(t, i, u, final):
                for h in range(H):
                    n = t * H + h
                    mix(t, n, h, u)
                    if h < H - 1 or not final:
                        maxes(n + 1, (h + 1) % H)
                dve.wait_ge(summed, H * t + H)
                dve.wait_ge(stored[u], 16 * i)
                nc.vector.tensor_tensor(ob[u][:, :, :], m.bank(7).rearrange("p (h n) -> p h n", h=H),
                                        r1[u][:, :].unsqueeze(2).to_broadcast([P, H, P]), ALU.mult).then_inc(tile_kept, 1)

            maxes(0, 0)
            tiles(dve, body, link, 4 * H)
    m.top = top


def mixed_output(m):
    nc, d, ident = m.nc, m.dram, m.keep["ident"]
    m.top, m.limit = m.base, 229312
    rep_mod = m.keep["rep_mod"] = m.sb("rep_mod", [P, 2, D])
    rep_ln = m.keep["rep_ln"] = m.sb("rep_ln", [P, 4, D])
    m.keep["rows_loaded"] = m.sem("rows_loaded", lasting=True)
    lg = m.keep["lg"] = m.sb("lg", [P, TL, NG + NE])
    m.after = m.top
    yo = m.keep["yo"] = m.sb("yo", [P, TL, D])
    w_route = m.keep["w_route"] = m.sb("w_route", [P, KD, NG + NE])
    top = m.top
    w_out = m.sb("w_out", [P, KD, D])
    nw = m.sb("nw", [P, 2, P])
    of = [m.sb(f"g_of{u}", [P, HD]) for u in range(2)]
    orv = [m.sb(f"g_or{u}", [P, HD]) for u in range(2)]
    zt = [m.sb(f"g_z{u}", [P, HD]) for u in range(2)]
    Y = [m.sb(f"g_Y{u}", [P, 2 * H, P]) for u in range(2)]
    sq = m.sb("g_sq", [P, 2 * H, P])
    ms = [m.sb(f"g_ms{u}", [P, 2 * H]) for u in range(2)]
    yT = [m.sb(f"g_yT{u}", [P, KD, P]) for u in range(2)]
    w_loaded = m.sem("g_w_loaded")
    loaded = [m.sem(f"g_loaded{u}") for u in range(2)]
    gated, summed, rooted, normed = m.sem("g_gated"), m.sem("g_summed"), m.sem("g_rooted"), m.sem("g_normed")
    turned, projected = m.sem("g_turned"), m.sem("g_projected")
    left = [m.sem(f"g_left{u}") for u in range(2)]
    kept = [m.sem(f"g_kept{u}") for u in range(2)]
    own = m.sem("g_dve_link")

    with nc.Block() as block:
        @block.sync
        def _(sp):
            sp.dma_start(nw[:, :, :], d["rep_norm"].rearrange("p (w n) -> p w n", w=2)).then_inc(w_loaded, 16)
            sp.dma_start(w_out[:, :, :], d["w_out"].rearrange("(k p) n -> p k n", p=P)).then_inc(w_loaded, 16)
            with sp.Fori(0, TL // 2) as i:
                for u in range(2):
                    t = 2 * i + u
                    back = i * -2 + (TT - 1 - u)
                    sp.wait_ge(kept[u], i)
                    sp.dma_start(of[u][:, :], flat(one(d["o"][0], t + TC))).then_inc(loaded[u], 16)
                    sp.dma_start(orv[u][:, :], flat(one(d["o"][1], back))).then_inc(loaded[u], 16)
                    sp.dma_start(zt[u][:, :], flat(one(d["z"], t))).then_inc(loaded[u], 16)
                    sp.dma_start(Y[u][:, H:, :], flat(one(d["od"], t)).rearrange("p (h n) -> p h n", h=H)).then_inc(loaded[u], 16)
            sp.dma_start(rep_ln[:, :, :], d["rep_ln"].rearrange("p (w n) -> p w n", w=4)).then_inc(m.keep["rows_loaded"], 16)
            for w, part in ((0, 2), (1, 5)):
                row = d["mod_rows"][0:1, part * D:(part + 1) * D]
                sp.dma_start(rep_mod[:, w, :], row.to_broadcast([P, D])).then_inc(m.keep["rows_loaded"], 16)
            sp.dma_start(w_route[:, :, :], d["w_route"].rearrange("(k p) n -> p k n", p=P)).then_inc(m.keep["rows_loaded"], 16)

        @block.scalar
        def _(act):
            def gate_and_turn(t, i, u):
                act.wait_ge(loaded[u], 64 * i + 64)
                nc.scalar.activation(zt[u][:, :], zt[u][:, :], ACT.Silu).then_inc(gated, 1)
                act.wait_ge(summed, t + 1)
                nc.scalar.activation(ms[u][:, :], ms[u][:, :], ACT.Sqrt, bias=m.keep["eps_norm"], scale=1.0 / P).then_inc(rooted, 1)
                act.wait_ge(turned, t + 1)
                nc.scalar.activation(yT[u][:, :, :].rearrange("p k n -> p (k n)"), m.psum[:, 2 * u * NC:2 * u * NC + D], ACT.Copy
                                     ).then_inc(kept[u], 1)

            def leave(t, u):
                act.wait_ge(projected, t + 1)
                nc.scalar.activation(cols(yo[:, bass.ds(t, 1), :]), m.psum[:, (4 + 2 * u) * NC:(6 + 2 * u) * NC], ACT.Copy
                                     ).then_inc(left[u], 1)

            gate_and_turn(0, 0, 0)
            with act.Fori(0, TL // 2 - 1) as i:
                gate_and_turn(2 * i + 1, i, 1)
                leave(2 * i, 0)
                gate_and_turn(2 * i + 2, i + 1, 0)
                leave(2 * i + 1, 1)
            gate_and_turn(TL - 1, TL // 2 - 1, 1)
            leave(TL - 2, 0)
            leave(TL - 1, 1)

        @block.vector
        def _(dve):
            link = Link(dve, own)
            tt = nc.vector.tensor_tensor
            W8 = [P, 2 * H, P]
            dve.wait_ge(w_loaded, 32)
            link(nc.vector.tensor_scalar(nw[:, 1, :], nw[:, 1, :], 1.0 - LAM_INIT, None, ALU.mult))
            with link.loop(TL // 2, 2 * 5) as i:
                for u in range(2):
                    t = 2 * i + u
                    dve.wait_ge(loaded[u], 64 * i + 64)
                    link(tt(Y[u][:, 0:H, :].rearrange("p h n -> p (h n)"), of[u][:, :], orv[u][:, :], ALU.add))
                    link(tt(sq[:, :, :], Y[u][:, :, :], Y[u][:, :, :], ALU.mult))
                    nc.vector.tensor_reduce(ms[u][:, :], sq[:, :, :], AX, ALU.add).then_inc(summed, 1)
                    dve.wait_ge(rooted, t + 1)
                    link(nc.vector.reciprocal(ms[u][:, :], ms[u][:, :]))
                    link(tt(Y[u][:, :, :], Y[u][:, :, :], ms[u][:, :].unsqueeze(2).to_broadcast(W8), ALU.mult))
                    nc.vector.tensor_tensor(Y[u][:, 0:H, :], Y[u][:, 0:H, :], nw[:, 0, :].unsqueeze(1).to_broadcast([P, H, P]), ALU.mult)
                    link(tt(Y[u][:, H:, :], Y[u][:, H:, :], nw[:, 1, :].unsqueeze(1).to_broadcast([P, H, P]), ALU.mult))
                    dve.wait_ge(gated, t + 1)
                    tt(Y[u][:, 0:H, :].rearrange("p h n -> p (h n)"), Y[u][:, 0:H, :].rearrange("p h n -> p (h n)"), zt[u][:, :],
                       ALU.mult).then_inc(normed, 1)

        @block.tensor
        def _(pe):
            def turn(t, i, u):
                pe.wait_ge(normed, t + 1)
                pe.wait_ge(kept[u], i)
                for k in range(KD):
                    last = nc.tensor.transpose(m.psum[:, 2 * u * NC + k * P:2 * u * NC + (k + 1) * P], Y[u][:, k, :], ident)
                last.then_inc(turned, 1)

            def project(i, u):
                pe.wait_ge(kept[u], i + 1)
                pe.wait_ge(left[u], i)
                for c in range(2):
                    for k in range(KD):
                        last = nc.tensor.matmul(m.bank(4 + 2 * u + c), yT[u][:, k, :], w_out[:, k, c * NC:(c + 1) * NC],
                                                start=(k == 0), stop=(k == KD - 1))
                last.then_inc(projected, 1)

            pe.wait_ge(w_loaded, 32)
            turn(0, 0, 0)
            with pe.Fori(0, TL // 2 - 1) as i:
                turn(2 * i + 1, i, 1)
                project(i, 0)
                turn(2 * i + 2, i + 1, 0)
                project(i, 1)
            turn(TL - 1, TL // 2 - 1, 1)
            project(TL // 2 - 1, 0)
            project(TL // 2 - 1, 1)
    m.top = top


def layer_norm_stats(nc, dve, link, st, mv, src):
    for c in range(2):
        last = nc.vector.bn_stats(st[:, c, :], src[:, c * NC:(c + 1) * NC])
    link(last, plain=True)
    link(nc.vector.bn_aggr(mv[:, :], st[:, :, :].rearrange("p a b -> p (a b)")))


def residual_and_logits(m):
    nc, d, ident, modT = m.nc, m.dram, m.keep["ident"], m.keep["modT"]
    rep_mod, rep_ln, yo, lg = (m.keep[n] for n in ("rep_mod", "rep_ln", "yo", "lg"))
    w_route = m.keep["w_route"]
    m.scratch("x1", [TL, P, D])
    m.scratch("xn2", [SEQ, D])
    m.scratch("token_of", [(BLOCKS + 2) * P, 1], I32)
    st = m.sb("h_st", [P, 2, 6])
    mv = [[m.sb(f"h_mv{w}{u}", [P, 2]) for u in range(2)] for w in range(2)]
    sd = [[m.sb(f"h_sd{w}{u}", [P, 1]) for u in range(2)] for w in range(2)]
    xt = [m.sb(f"h_x{u}", [P, D]) for u in range(2)]
    x1 = [m.sb(f"h_x1{u}", [P, D]) for u in range(2)]
    xn = [m.sb(f"h_xn{u}", [P, D]) for u in range(2)]
    h2T = [m.sb(f"h_h2T{u}", [P, KD, P]) for u in range(2)]
    none = m.sb("h_none", [P, BLOCKS + 2], I32)
    loaded = [m.sem(f"h_loaded{u}") for u in range(2)]
    x1_stored = [m.sem(f"h_x1_stored{u}") for u in range(2)]
    xn_stored = [m.sem(f"h_xn_stored{u}") for u in range(2)]
    scaled, stats, std, shaped, normed = m.sem("h_scaled"), m.sem("h_stats"), m.sem("h_std"), m.sem("h_shaped"), m.sem("h_normed")
    added, routed, biased = m.sem("h_added"), m.sem("h_routed"), m.sem("h_logits_kept")
    turned = [m.sem(f"h_turned{u}") for u in range(2)]
    kept = [m.sem(f"h_kept{u}") for u in range(2)]
    cleared, clear_stored, own = m.sem("h_cleared"), m.sem("h_clear_stored"), m.sem("h_dve_link")
    x = d["tokens"].rearrange("(t p) n -> t p n", p=P)
    xn2 = d["xn2"].rearrange("(t p) n -> t p n", p=P)

    with nc.Block() as block:
        @block.sync
        def _(sp):
            def load(t, u):
                sp.dma_start(xt[u][:, :], flat(one(x, t))).then_inc(loaded[u], 16)

            def store(t, u):
                sp.wait_ge(shaped, t + 1)
                sp.dma_start(flat(one(d["x1"], t)), x1[u][:, :]).then_inc(x1_stored[u], 16)
                sp.wait_ge(normed, t + 1)
                sp.dma_start(flat(one(xn2, t)), xn[u][:, :]).then_inc(xn_stored[u], 16)

            sp.wait_ge(cleared, 1)
            sp.dma_start(d["token_of"].rearrange("(p b) a -> p (b a)", p=P), none[:, :]).then_inc(clear_stored, 16)
            for u in range(2):
                load(u, u)
            with sp.Fori(0, TL // 2 - 1) as i:
                for u in range(2):
                    store(2 * i + u, u)
                    load(2 * i + u + 2, u)
            for u in range(2):
                store(TL - 2 + u, u)
            for u in range(2):
                sp.wait_ge(x1_stored[u], 16 * (TL // 2))
                sp.wait_ge(xn_stored[u], 16 * (TL // 2))
            sp.wait_ge(clear_stored, 16)

        @block.gpsimd
        def _(pool):
            nc.gpsimd.memset(none[:, :], 0).then_inc(cleared, 1)
            pool.wait_ge(m.keep["rows_loaded"], 64)
            with pool.Fori(0, TL) as t:
                y = cols(yo[:, bass.ds(t, 1), :])
                nc.gpsimd.tensor_tensor(y, y, rep_mod[:, 0, :], ALU.mult).then_inc(scaled, 1)

        @block.vector
        def _(dve):
            link = Link(dve, own)
            tt = nc.vector.tensor_tensor
            dve.wait_ge(m.keep["rows_loaded"], 64)
            with link.loop(TL // 2, 2 * 10) as i:
                for u in range(2):
                    t = 2 * i + u
                    dve.wait_ge(scaled, t + 1)
                    dve.wait_ge(loaded[u], 16 * i + 16)
                    dve.wait_ge(x1_stored[u], 16 * i)
                    nc.vector.scalar_tensor_tensor(x1[u][:, :], xt[u][:, :], ALPHA, cols(yo[:, bass.ds(t, 1), :]), ALU.mult, ALU.add
                                                   ).then_inc(added, 1)
                    dve.wait_ge(added, t + 1)
                    layer_norm_stats(nc, dve, link, st, mv[0][u], x1[u])
                    dve.sem_inc(stats, 1)
                    dve.wait_ge(std, 4 * i + 2 * u + 1)
                    link(nc.vector.reciprocal(sd[0][u][:, :], sd[0][u][:, :]))
                    link(nc.vector.tensor_scalar(x1[u][:, :], x1[u][:, :], mv[0][u][:, 0:1], sd[0][u][:, :], ALU.subtract, ALU.mult))
                    link(tt(x1[u][:, :], x1[u][:, :], rep_ln[:, 0, :], ALU.mult))
                    tt(x1[u][:, :], x1[u][:, :], rep_ln[:, 1, :], ALU.add).then_inc(shaped, 1)
                    dve.wait_ge(shaped, t + 1)
                    layer_norm_stats(nc, dve, link, st, mv[1][u], x1[u])
                    dve.sem_inc(stats, 1)
                    dve.wait_ge(std, 4 * i + 2 * u + 2)
                    link(nc.vector.reciprocal(sd[1][u][:, :], sd[1][u][:, :]))
                    dve.wait_ge(turned[u], i)
                    dve.wait_ge(xn_stored[u], 16 * i)
                    nc.vector.tensor_scalar(xn[u][:, :], x1[u][:, :], mv[1][u][:, 0:1], sd[1][u][:, :], ALU.subtract,
                                            ALU.mult).then_inc(normed, 1)

        @block.scalar
        def _(act):
            with act.Fori(0, TL // 2) as i:
                for u in range(2):
                    t = 2 * i + u
                    for w in range(2):
                        act.wait_ge(stats, 4 * i + 2 * u + w + 1)
                        nc.scalar.activation(sd[w][u][:, :], mv[w][u][:, 1:2], ACT.Sqrt, bias=m.keep["eps_ln"]).then_inc(std, 1)
                    act.wait_ge(turned[u], i + 1)
                    for k in range(KD):
                        last = nc.scalar.activation(h2T[u][:, k, :], m.bank(2 * u + k // 4)[:, k % 4 * P:(k % 4 + 1) * P], ACT.Identity,
                                                    scale=modT[:, 4 * KD + k, 0:1], bias=modT[:, 3 * KD + k, 0:1])
                    last.then_inc(kept[u], 1)
                    act.wait_ge(routed, t + 1)
                    nc.scalar.activation(cols(lg[:, bass.ds(t, 1), :]), m.bank(4, NG + NE), ACT.Copy).then_inc(biased, 1)

        @block.tensor
        def _(pe):
            pe.wait_ge(m.keep["rows_loaded"], 64)
            with pe.Fori(0, TL // 2) as i:
                for u in range(2):
                    t = 2 * i + u
                    pe.wait_ge(normed, t + 1)
                    pe.wait_ge(kept[u], i)
                    for k in range(KD):
                        last = nc.tensor.transpose(m.bank(2 * u + k // 4)[:, k % 4 * P:(k % 4 + 1) * P],
                                                   xn[u][:, k * P:(k + 1) * P], ident)
                    last.then_inc(turned[u], 1)
                    pe.wait_ge(kept[u], i + 1)
                    pe.wait_ge(biased, t)
                    for k in range(KD):
                        last = nc.tensor.matmul(m.bank(4, NG + NE), h2T[u][:, k, :], w_route[:, k, :], start=(k == 0), stop=(k == KD - 1))
                    last.then_inc(routed, 1)
    m.top = m.after


def routing(m):
    nc, d, small, ones, before, lg = m.nc, m.dram, m.keep["small"], m.keep["ones"], m.keep["before"], m.keep["lg"]
    gate = m.keep["gate"] = m.sb("gate", [P, 2, TL])
    row = m.keep["row"] = m.sb("row", [P, 2, TL], I32)
    plan = m.keep["plan"] = m.sb("plan", [P, BLOCKS + 1], I32)
    tok = m.keep["tok"] = m.sb("tok", [P, BLOCKS + 1], I32)
    top = m.top
    T8 = [P, TL]
    names = "gmax gsum pg best tie m1 m2 e2 den".split()
    v = {n: m.sb("r_" + n, T8) for n in names}
    rb = m.sb("r_bias", [P, NG + NE])
    oh = m.sb("r_group", [P, TL, NG])
    eg = m.sb("r_eg", [P, TL, NG])
    pick = m.sb("r_pick", [P, TL, NG, EG])
    li = m.sb("r_li", [P, TL, EG])
    ohs = [m.sb(f"r_first{j}", [P, TL, EG]) for j in range(2)]
    E = [m.sb(f"r_E{j}", [P, TL, NE]) for j in range(2)]
    M = m.sb("r_M", [P, TL, NE])
    rank = m.sb("r_rank", [P, TL, NE])
    cnt = m.sb("r_cnt", [P, NE])
    nblk = m.sb("r_nblk", [P, NE])
    ends = m.sb("r_ends", [P, NE])
    base = m.sb("r_base", [P, NE])
    onesr = m.sb("r_ones", [P, NE])
    over = m.sb("r_over", [P, NE, EG])
    own_of = m.sb("r_own", [P, BLOCKS, NE])
    planf = m.sb("r_planf", [P, BLOCKS + 1])
    rowf = m.sb("r_rowf", [P, 2, TL])
    ids = m.sb("r_ids", [P, TL], I32)
    loaded, dve_did, act_did, counted = m.sem("r_loaded"), m.sem("r_dve"), m.sem("r_act"), m.sem("r_counted")
    rows_ready, chosen, scattered, tok_loaded = m.sem("r_rows_ready"), m.sem("r_chosen"), m.sem("r_scattered"), m.sem("r_tok_loaded")
    desc = {NG: small[:, 0:4], EG: small[:, 4:12]}

    with nc.Block() as block:
        @block.sync
        def _(sp):
            sp.dma_start(ids[:, :], d["ids"]).then_inc(loaded, 16)
            sp.dma_start(rb[:, :], d["rep_route"]).then_inc(loaded, 16)
            sp.wait_ge(scattered, 16 * 2 * TL)
            sp.dma_start(tok[:, :], d["token_of"].rearrange("(b p) a -> p (b a)", p=P)[:, 0:BLOCKS + 1],
                         allow_slow_non_contiguous=True).then_inc(tok_loaded, 16)
            sp.wait_ge(tok_loaded, 16)

        @block.gpsimd
        def _(pool):
            pool.wait_ge(loaded, 32)
            pool.wait_ge(rows_ready, 1)
            for j in range(2):
                for t in range(TL):
                    pool.indirect_dma_start(out=d["token_of"], out_offset=bass.IndirectOffsetOnAxis(ap=row[:, j, t:t + 1], axis=0),
                                            in_=ids[:, t:t + 1], in_offset=None).then_inc(scattered, 16)

        @block.vector
        def _(dve):
            link = Link(dve, dve_did)
            tt, ts, red = nc.vector.tensor_tensor, nc.vector.tensor_scalar, nc.vector.tensor_reduce

            def wide(ap, n):
                return ap.unsqueeze(2).to_broadcast([P, TL, n])

            def first_of(out, values, top_, n):
                link(tt(out, values, wide(top_[:, :], n), ALU.is_equal))
                link(tt(out, out, desc[n].unsqueeze(1).to_broadcast([P, TL, n]), ALU.mult))
                link(red(v["tie"][:, :], out, AX, ALU.max))
                link(tt(out, out, wide(v["tie"][:, :], n), ALU.is_equal))

            dve.wait_ge(loaded, 32)
            link(tt(lg[:, :, :], lg[:, :, :], rb[:, :].unsqueeze(1).to_broadcast([P, TL, NG + NE]), ALU.add))
            g, e = lg[:, :, 0:NG], lg[:, :, NG:]
            link(red(v["gmax"][:, :], g, AX, ALU.max))
            link(tt(eg[:, :, :], g, wide(v["gmax"][:, :], NG), ALU.subtract))
            dve.sem_inc(chosen, 1)
            first_of(oh[:, :, :], g, v["gmax"], NG)
            link(tt(pick[:, :, :, :], e.rearrange("p t (g e) -> p t g e", g=NG),
                    oh[:, :, :].unsqueeze(3).to_broadcast([P, TL, NG, EG]), ALU.mult))
            link(red(li[:, :, :], pick[:, :, :, :].rearrange("p t g e -> p t e g"), AX, ALU.add))
            link(red(v["m1"][:, :], li[:, :, :], AX, ALU.max))
            first_of(ohs[0][:, :, :], li[:, :, :], v["m1"], EG)
            link(nc.vector.scalar_tensor_tensor(li[:, :, :], ohs[0][:, :, :], -BIG, li[:, :, :], ALU.mult, ALU.add))
            link(red(v["m2"][:, :], li[:, :, :], AX, ALU.max))
            first_of(ohs[1][:, :, :], li[:, :, :], v["m2"], EG)
            link(tt(v["e2"][:, :], v["m2"][:, :], v["m1"][:, :], ALU.subtract))
            dve.sem_inc(chosen, 1)
            for j in range(2):
                last = tt(E[j][:, :, :].rearrange("p t (g e) -> p t g e", g=NG), oh[:, :, :].unsqueeze(3).to_broadcast([P, TL, NG, EG]),
                          ohs[j][:, :, :].unsqueeze(2).to_broadcast([P, TL, NG, EG]), ALU.mult)
            link(last)
            link(tt(M[:, :, :], E[0][:, :, :], E[1][:, :, :], ALU.add))
            dve.sem_inc(chosen, 1)
            dve.wait_ge(act_did, 2)
            link(red(v["gsum"][:, :], eg[:, :, :], AX, ALU.add))
            link(ts(v["den"][:, :], v["e2"][:, :], 1.0, None, ALU.add))
            link(tt(v["den"][:, :], v["den"][:, :], v["gsum"][:, :], ALU.mult))
            link(nc.vector.reciprocal(gate[:, 0, :], v["den"][:, :]))
            link(tt(gate[:, 1, :], gate[:, 0, :], v["e2"][:, :], ALU.mult))
            dve.wait_ge(counted, 1)
            nc.vector.tensor_copy(rank[:, :, :], m.bank(0, TL * NE).rearrange("p (t e) -> p t e", e=NE))
            nc.vector.memset(onesr[:, :], 1.0)
            link(nc.vector.tensor_copy(cnt[:, :], m.bank(1, NE)))
            link(tt(over[:, :, :], cnt[:, :].unsqueeze(2).to_broadcast([P, NE, EG]), small[:, 12:20].unsqueeze(1).to_broadcast([P, NE, EG]),
                    ALU.is_gt))
            link(red(nblk[:, :], over[:, :, :], AX, ALU.add))
            link(nc.vector.tensor_tensor_scan(ends[:, :], onesr[:, :], nblk[:, :], 0.0, ALU.mult, ALU.add))
            link(tt(base[:, :], ends[:, :], nblk[:, :], ALU.subtract))
            link(ts(base[:, :], base[:, :], float(P), None, ALU.mult))
            link(tt(rank[:, :, :], rank[:, :, :], base[:, :].unsqueeze(1).to_broadcast([P, TL, NE]), ALU.add))
            for j in range(2):
                link(tt(M[:, :, :], E[j][:, :, :], rank[:, :, :], ALU.mult))
                link(red(rowf[:, j, :], M[:, :, :], AX, ALU.add))
            nc.vector.tensor_copy(row[:, :, :], rowf[:, :, :]).then_inc(rows_ready, 1)
            link(tt(own_of[:, :, :], ends[:, :].unsqueeze(1).to_broadcast([P, BLOCKS, NE]),
                    small[:, 20:20 + BLOCKS].unsqueeze(2).to_broadcast([P, BLOCKS, NE]), ALU.is_le))
            link(red(planf[:, 0:BLOCKS], own_of[:, :, :], AX, ALU.add))
            link(ts(planf[:, 0:BLOCKS], planf[:, 0:BLOCKS], float(NE - 1), None, ALU.min))
            link(nc.vector.tensor_copy(planf[:, BLOCKS:], ends[:, NE - 1:NE]))
            link(nc.vector.tensor_copy(plan[:, :], planf[:, :]))

        @block.scalar
        def _(act):
            act.wait_ge(chosen, 1)
            nc.scalar.activation(eg[:, :, :], eg[:, :, :], ACT.Exp).then_inc(act_did, 1)
            act.wait_ge(chosen, 2)
            nc.scalar.activation(v["e2"][:, :], v["e2"][:, :], ACT.Exp).then_inc(act_did, 1)

        @block.tensor
        def _(pe):
            pe.wait_ge(chosen, 3)
            for t in range(TL):
                for b in range(t):
                    nc.tensor.matmul(m.bank(0, NE, t * NE), ones, M[:, b, :], start=(b == 0), stop=False)
                nc.tensor.matmul(m.bank(0, NE, t * NE), before, M[:, t, :], start=(t == 0), stop=True)
            for t in range(TL):
                last = nc.tensor.matmul(m.bank(1, NE), ones, M[:, t, :], start=(t == 0), stop=(t == TL - 1))
            last.then_inc(counted, 1)
    m.top = top


def experts(m):
    nc, d, ident, modT, plan, tok = m.nc, m.dram, m.keep["ident"], m.keep["modT"], m.keep["plan"], m.keep["tok"]
    top = m.top
    m.scratch("yb", [BLOCKS * P, D])
    KE = DE // P
    Wg, Wu = ([m.sb(f"w_{n}{u}", [P, KD, DE]) for u in range(2)] for n in ("gate", "up"))
    Wd = [m.sb(f"w_down{u}", [P, KE, D]) for u in range(2)]
    idx = [m.sb(f"i_idx{u}", [P, 1], I32) for u in range(2)]
    xg = [m.sb(f"i_x{u}", [P, D]) for u in range(2)]
    xT = [m.sb(f"i_xT{u}", [P, KD, P]) for u in range(2)]
    nothing = m.sb("i_nothing", [P, D])
    nothing_ready, nothing_stored = m.sem("i_nothing_ready"), m.sem("i_nothing_stored")
    hs = m.sb("i_silu", [P, DE])
    hh = m.sb("i_h", [P, DE])
    hT = m.sb("i_hT", [P, KE, P])
    yo = [m.sb(f"i_y{u}", [P, D]) for u in range(2)]
    U2 = range(2)
    loads = {n: [m.sem(f"i_{n}_loaded{u}") for u in U2] for n in ("gate", "up", "down")}
    used = {n: [m.sem(f"i_{n}_used{u}") for u in U2] for n in ("gate", "up", "down")}
    idx_ready, all_stored = m.sem("i_idx_ready"), m.sem("i_all_stored")
    gathered = [m.sem(f"i_gathered{u}") for u in U2]
    stored = [m.sem(f"i_stored{u}") for u in U2]
    x_turned = [m.sem(f"i_x_turned{u}") for u in U2]
    x_kept = [m.sem(f"i_x_kept{u}") for u in U2]
    silued, mixed, h_turned, h_kept, y_kept = (m.sem("i_" + n) for n in ("silued", "mixed", "h_turned", "h_kept", "y_kept"))
    ybt = d["yb"].rearrange("(b p) n -> b p n", p=P)
    wg, wu, wd = (d[n].rearrange("e (k p) n -> e p k n", p=P) for n in ("w_gate", "w_up", "w_down"))
    LOW = 2 * SEQ // P

    def blocks(eng, body):
        nb = eng.value_load(plan[0:1, BLOCKS:BLOCKS + 1], min_val=LOW, max_val=BLOCKS)
        with eng.Fori(0, BLOCKS // 2) as i:
            for u in range(2):
                with eng.If(2 * i + u < nb):
                    body(2 * i + u, i, u)
        return nb

    with nc.Block() as block:
        @block.sync
        def _(sp):
            def body(b, i, u):
                e = sp.value_load(plan[0:1, bass.ds(b, 1)], min_val=0, max_val=NE - 1)
                for n, W, src in (("gate", Wg, wg), ("up", Wu, wu), ("down", Wd, wd)):
                    sp.wait_ge(used[n][u], i)
                    sp.dma_start(W[u][:, :, :], one(src, e).rearrange("e p k n -> (e p) k n")).then_inc(loads[n][u], 16)
            nb = blocks(sp, body)
            sp.wait_ge(nothing_ready, 1)
            with sp.Fori(0, BLOCKS - LOW) as j:
                with sp.If(nb < j + LOW + 1):
                    sp.dma_start(flat(one(ybt, j + LOW)), nothing[:, :]).then_inc(nothing_stored, 16)
                with sp.If(j + LOW < nb):
                    sp.sem_inc(nothing_stored, 16)
            sp.wait_ge(nothing_stored, 16 * (BLOCKS - LOW))
            sp.sem_inc(all_stored, 1)

        @block.gpsimd
        def _(pool):
            nc.gpsimd.memset(nothing[:, :], 0.0).then_inc(nothing_ready, 1)

            def gather(b, i, u):
                pool.wait_ge(x_turned[u], i)
                nc.gpsimd.tensor_copy(idx[u][:, :], tok[:, bass.ds(b, 1)]).then_inc(idx_ready, 1)
                pool.wait_ge(idx_ready, 2 * b + 1)
                pool.sem_inc(idx_ready, 1)
                pool.indirect_dma_start(out=xg[u][:, :], out_offset=None, in_=d["xn2"],
                                        in_offset=bass.IndirectOffsetOnAxis(ap=idx[u][:, :], axis=0)).then_inc(gathered[u], 16)
            gather(0, 0, 0)
            blocks(pool, lambda b, i, u: gather(b + 1, i + u, 1 - u))

        @block.tensor
        def _(pe):
            def turn(i, u):
                pe.wait_ge(gathered[u], 16 * i + 16)
                pe.wait_ge(x_kept[u], i)
                for k in range(KD):
                    last = nc.tensor.transpose(m.bank(k // 4)[:, k % 4 * P:(k % 4 + 1) * P], xg[u][:, k * P:(k + 1) * P], ident)
                last.then_inc(x_turned[u], 1)

            def body(b, i, u):
                pe.wait_ge(x_kept[u], i + 1)
                pe.wait_ge(mixed, b)
                for bank, W, n in ((2, Wg, "gate"), (3, Wu, "up")):
                    pe.wait_ge(loads[n][u], 16 * i + 16)
                    for k in range(KD):
                        last = nc.tensor.matmul(m.bank(bank), xT[u][:, k, :], W[u][:, k, :], start=(k == 0), stop=(k == KD - 1))
                    last.then_inc(used[n][u], 1)
                turn(i + u, 1 - u)
                pe.wait_ge(mixed, b + 1)
                for k in range(KE):
                    last = nc.tensor.transpose(m.bank(4, P, k * P), hh[:, k * P:(k + 1) * P], ident)
                last.then_inc(h_turned, 1)
                pe.wait_ge(h_kept, b + 1)
                pe.wait_ge(y_kept, b)
                pe.wait_ge(loads["down"][u], 16 * i + 16)
                for c in range(2):
                    for k in range(KE):
                        last = nc.tensor.matmul(m.bank(5 + c), hT[:, k, :], Wd[u][:, k, c * NC:(c + 1) * NC],
                                                start=(k == 0), stop=(k == KE - 1))
                last.then_inc(used["down"][u], 1)

            turn(0, 0)
            blocks(pe, body)

        @block.scalar
        def _(act):
            def body(b, i, u):
                act.wait_ge(used["gate"][u], i + 1)
                act.wait_ge(mixed, b)
                nc.scalar.activation(hs[:, :], m.bank(2), ACT.Silu).then_inc(silued, 1)
                act.wait_ge(h_turned, b + 1)
                nc.scalar.activation(hT[:, :, :].rearrange("p k n -> p (k n)"), m.bank(4), ACT.Copy).then_inc(h_kept, 1)
                act.wait_ge(used["down"][u], i + 1)
                act.wait_ge(stored[u], 16 * i)
                nc.scalar.activation(yo[u][:, :], m.psum[:, 5 * NC:5 * NC + D], ACT.Copy).then_inc(y_kept, 1)
                act.wait_ge(y_kept, b + 1)
                act.dma_start(flat(one(ybt, b)), yo[u][:, :]).then_inc(stored[u], 16)
            nb = blocks(act, body)
            act.wait_ge(stored[0], ((nb + 1) >> 1) * 16)
            act.wait_ge(stored[1], (nb >> 1) * 16)
            act.sem_inc(all_stored, 1)

        @block.vector
        def _(dve):
            def shape(i, u):
                dve.wait_ge(x_turned[u], i + 1)
                for k in range(KD):
                    last = nc.vector.tensor_scalar(xT[u][:, k, :], m.bank(k // 4)[:, k % 4 * P:(k % 4 + 1) * P],
                                                   modT[:, 4 * KD + k, 0:1], modT[:, 3 * KD + k, 0:1], ALU.mult, ALU.add)
                last.then_inc(x_kept[u], 1)

            def body(b, i, u):
                dve.wait_ge(silued, b + 1)
                dve.wait_ge(used["up"][u], i + 1)
                dve.wait_ge(h_turned, b)
                nc.vector.tensor_tensor(hh[:, :], hs[:, :], m.bank(3), ALU.mult).then_inc(mixed, 1)
                shape(i + u, 1 - u)
            shape(0, 0)
            blocks(dve, body)
    m.top = top


def combine(m):
    nc, d, gate, row = m.nc, m.dram, m.keep["gate"], m.keep["row"]
    rep_mod, rep_ln = m.keep["rep_mod"], m.keep["rep_ln"]
    x1, y1, y2, acc = ([m.sb(f"j_{n}{u}", [P, D]) for u in range(2)] for n in ("x1", "y1", "y2", "acc"))
    idx = [[m.sb(f"j_idx{j}{u}", [P, 1], I32) for u in range(2)] for j in range(2)]
    st = m.sb("j_st", [P, 2, 6])
    mv = [m.sb(f"j_mv{u}", [P, 2]) for u in range(2)]
    sd = [m.sb(f"j_sd{u}", [P, 1]) for u in range(2)]
    loaded = [m.sem(f"j_loaded{u}") for u in range(2)]
    gathered = [m.sem(f"j_gathered{u}") for u in range(2)]
    stored = [m.sem(f"j_stored{u}") for u in range(2)]
    summed = [m.sem(f"j_summed{u}") for u in range(2)]
    idx_ready, stats, std, ready, own = (m.sem("j_" + n) for n in ("idx_ready", "stats", "std", "ready", "dve_link"))
    out = d["out"].rearrange("(t p) n -> t p n", p=P)

    with nc.Block() as block:
        @block.sync
        def _(sp):
            def load(t, u):
                sp.dma_start(x1[u][:, :], flat(one(d["x1"], t))).then_inc(loaded[u], 16)

            def store(t, u):
                sp.wait_ge(ready, t + 1)
                sp.dma_start(flat(one(out, t)), acc[u][:, :]).then_inc(stored[u], 16)

            for u in range(2):
                load(u, u)
            with sp.Fori(0, TL // 2 - 1) as i:
                for u in range(2):
                    store(2 * i + u, u)
                    load(2 * i + u + 2, u)
            for u in range(2):
                store(TL - 2 + u, u)
            for u in range(2):
                sp.wait_ge(stored[u], 16 * (TL // 2))

        @block.gpsimd
        def _(pool):
            with pool.Fori(0, TL // 2) as i:
                for u in range(2):
                    t = 2 * i + u
                    pool.wait_ge(summed[u], i)
                    for j in range(2):
                        nc.gpsimd.tensor_copy(idx[j][u][:, :], row[:, j, bass.ds(t, 1)]).then_inc(idx_ready, 1)
                    pool.wait_ge(idx_ready, 3 * t + 2)
                    pool.sem_inc(idx_ready, 1)
                    for j, y in enumerate((y1, y2)):
                        pool.indirect_dma_start(out=y[u][:, :], out_offset=None, in_=d["yb"],
                                                in_offset=bass.IndirectOffsetOnAxis(ap=idx[j][u][:, :], axis=0)).then_inc(gathered[u], 16)

        @block.vector
        def _(dve):
            link = Link(dve, own)
            tt = nc.vector.tensor_tensor
            with link.loop(TL // 2, 2 * 9) as i:
                for u in range(2):
                    t = 2 * i + u
                    dve.wait_ge(gathered[u], 32 * i + 32)
                    dve.wait_ge(stored[u], 16 * i)
                    link(nc.vector.tensor_scalar(acc[u][:, :], y1[u][:, :], gate[:, 0, bass.ds(t, 1)], None, ALU.mult))
                    nc.vector.scalar_tensor_tensor(acc[u][:, :], y2[u][:, :], gate[:, 1, bass.ds(t, 1)], acc[u][:, :],
                                                   ALU.mult, ALU.add).then_inc(summed[u], 1)
                    dve.wait_ge(summed[u], i + 1)
                    link(tt(acc[u][:, :], acc[u][:, :], rep_mod[:, 1, :], ALU.mult))
                    dve.wait_ge(loaded[u], 16 * i + 16)
                    link(nc.vector.scalar_tensor_tensor(acc[u][:, :], x1[u][:, :], ALPHA, acc[u][:, :], ALU.mult, ALU.add))
                    layer_norm_stats(nc, dve, link, st, mv[u], acc[u])
                    dve.sem_inc(stats, 1)
                    dve.wait_ge(std, t + 1)
                    link(nc.vector.reciprocal(sd[u][:, :], sd[u][:, :]))
                    link(nc.vector.tensor_scalar(acc[u][:, :], acc[u][:, :], mv[u][:, 0:1], sd[u][:, :], ALU.subtract, ALU.mult))
                    link(tt(acc[u][:, :], acc[u][:, :], rep_ln[:, 2, :], ALU.mult))
                    tt(acc[u][:, :], acc[u][:, :], rep_ln[:, 3, :], ALU.add).then_inc(ready, 1)

        @block.scalar
        def _(act):
            with act.Fori(0, TL // 2) as i:
                for u in range(2):
                    act.wait_ge(stats, 2 * i + u + 1)
                    nc.scalar.activation(sd[u][:, :], mv[u][:, 1:2], ACT.Sqrt, bias=m.keep["eps_ln"]).then_inc(std, 1)


def program(nc, dram):
    m = Machine(nc, dram)
    for phase in PHASES:
        m.phase_sems = []
        phase(m)
        nc.clear_and_free_semaphores(m.phase_sems)
        nc.all_engine_barrier()


PHASES = [modulation, normed_transposed, delta_inputs, token_inputs,
          delta_gates, delta_rule, attention, mixed_output, residual_and_logits,
          routing, experts, combine]


def constants():
    i = np.arange(P)
    row, col = i[:, None], i[None, :]
    parts = [row == col, np.ones((P, P)), row <= col, row >= col, row < col,
             -BIG * (row > col), -BIG * (row < col)]
    for r in range(2):
        for lv in range(LEVELS):
            b = 1 << lv
            a, z = (row, col) if r == 0 else (col, row)
            parts.append((a // (2 * b) == z // (2 * b)) & (a // b % 2 == 0) & (z // b % 2 == 1))
    masks = np.concatenate([np.asarray(x, np.float32) for x in parts], axis=1)
    half = DK // 2
    freq = np.float32(10000.0) ** (-np.arange(0, half, 2, dtype=np.float32) / np.float32(half))
    t = np.arange(SEQ)
    ang = [(p.astype(np.float32)[:, None] * freq[None, :]).astype(np.float32) for p in (t // 64, t % 64)]
    rope = np.concatenate([f(a) for f in (np.cos, np.sin) for a in ang for _ in range(2)], axis=1).astype(np.float32)
    small = np.zeros((P, 96), np.float32)
    small[:, 0:4] = [4, 3, 2, 1]
    small[:, 4:12] = [8, 7, 6, 5, 4, 3, 2, 1]
    small[:, 12:20] = np.arange(8) * P
    small[:, 20:68] = np.arange(48)
    small[:, 68] = LN_EPS
    small[:, 69] = NORM_EPS
    ids = (np.arange(P)[:, None] + P * np.arange(TL)[None, :]).astype(np.int32)
    quad = np.zeros((P, P + 32), np.float32)
    quad[:, :P] = row // 32 == col // 32
    quad[:, P:] = row % 32 == np.arange(32)[None, :]
    return {"quad": quad, "masks": masks, "rope": rope, "small": small, "ids": ids}


def kernel(x, c, ctx, c_ctx, w_ada, b_ada, w_in, conv_w, gdn_a_log, gdn_dt_bias, gdn_norm_w,
           diff_lambda, diff_norm_w, w_out, ln1_g, ln1_b, w_router_group, b_router_group,
           w_router_expert, b_router_expert, w_expert_gate, w_expert_up, w_expert_down, ln2_g, ln2_b):
    import concourse.bacc as bacc
    from concourse.bass_utils import run_bass_kernel_spmd as run

    def rep(a):
        return np.ascontiguousarray(np.broadcast_to(np.asarray(a).reshape(1, -1), (P, np.asarray(a).size)))

    cc = np.stack([np.asarray(c).reshape(KD, P), np.asarray(c_ctx).reshape(KD, P)], axis=-1)
    arrays = {
        "tokens": np.concatenate([np.asarray(x)[0], np.asarray(ctx)[0]], axis=0),
        "c_cols": np.ascontiguousarray(cc.transpose(1, 0, 2)).reshape(P, 2 * KD),
        "w_ada": w_ada[0], "b_ada": np.concatenate([b_ada, b_ada], axis=0), "w_in": w_in[0],
        "conv_cols": np.ascontiguousarray(np.asarray(conv_w)[0].reshape(CONV, 3 * H, P).transpose(2, 1, 0)).reshape(P, -1),
        "rep_gates": np.concatenate([rep(gdn_dt_bias), rep(gdn_a_log)], axis=1),
        "rep_norm": np.concatenate([rep(gdn_norm_w), rep(diff_norm_w)], axis=1),
        "rep_lambda": rep(diff_lambda), "w_out": w_out[0],
        "rep_ln": np.concatenate([rep(ln1_g), rep(ln1_b), rep(ln2_g), rep(ln2_b)], axis=1),
        "w_route": np.concatenate([w_router_group[0], w_router_expert[0]], axis=1),
        "rep_route": np.concatenate([rep(b_router_group), rep(b_router_expert)], axis=1),
        "w_gate": w_expert_gate[0], "w_up": w_expert_up[0], "w_down": w_expert_down[0],
    }
    arrays.update(constants())
    nc = bacc.Bacc("TRN2", target_bir_lowering=False, num_devices=1)
    dram = {}
    for name, a in arrays.items():
        a = arrays[name] = np.ascontiguousarray(a)
        dram[name] = nc.dram_tensor("in_" + name, a.shape, mybir.dt.from_np(a.dtype), kind="ExternalInput").ap()
    dram["out"] = nc.dram_tensor("out", (SEQ, D), F32, kind="ExternalOutput").ap()
    program(nc, dram)
    r = run(nc, [{"in_" + k: a for k, a in arrays.items()}], core_ids=[0])
    return r.results[0]["out"].reshape(1, SEQ, D)
```

```python
import math
from contextlib import contextmanager

import numpy as np
import concourse.bass as bass
from concourse import mybir

F32 = mybir.dt.float32
I32 = mybir.dt.int32
F32R = mybir.dt.float32r
ALU = mybir.AluOpType
ACT = mybir.ActivationFunctionType
AX = mybir.AxisListType.X

P = 128
D = 1024
KD = D // P
SEQ, CTX = 1024, 256
TL, TC = SEQ // P, CTX // P
TT = TL + TC
TOK = SEQ + CTX
H = 4
HD = H * P
DK = 64
NC = 512
CONV = 5
NMOD = 6 * D
NG, NE, EG = 4, 32, 8
DE = 512
BLOCKS = 2 * SEQ // P + NE
PLAN_EXPERT, PLAN_END, PLAN_RANK, PLAN_BLOCKS, PLAN_EXPERTS = 0, NE, 2 * NE, 2 * NE + BLOCKS, 2 * NE + BLOCKS + 1
PLAN = PLAN_EXPERTS + 1
ALPHA = 2.0 ** 0.25
LN_EPS, NORM_EPS = 1e-5, 1e-6
LAM_INIT = 0.8 - 0.6 * math.exp(0.0)
GDN_GATES_AT = 4 * HD
DIFF_AT = GDN_GATES_AT + 16
IN_COLS = DIFF_AT + 3 * HD
TAIL = IN_COLS - 3 * HD
BIG = 1.0e30
LEVELS = 7


class Link:

    def __init__(self, eng, sem):
        self.eng, self.sem, self.base, self.n = eng, sem, 0, 0

    def __call__(self, ins, plain=False):
        ins.then_inc(self.sem, 1)
        self.n += 1
        self.eng.wait_ge(self.sem, self.base + self.n)
        if plain:
            self.eng.sem_inc(self.sem, 1)
            self.n += 1

    @contextmanager
    def loop(self, count, per):
        start = self.base + self.n
        with self.eng.Fori(0, count) as i:
            self.base, self.n = start + i * per, 0
            yield i
            assert self.n == per, f"the body links {self.n}"
        self.base, self.n = start + count * per, 0


class Machine:

    def __init__(self, nc, dram):
        self.nc, self.dram = nc, dram
        self.top, self.limit = 16512, 229312
        self.high = 229312 - 4 * (H * TOK + TT * HD + TT * 16)
        self.psum = nc.alloc_psum_tensor("psum", [P, 8 * NC], F32)
        self.keep = {}

    def sb(self, name, shape, dt=F32):
        size = 4 * int(np.prod(shape[1:]))
        t = self.nc.alloc_sbuf_tensor_at(name, shape, dt, offset=self.top)
        self.top += -(-size // 32) * 32
        assert self.top <= self.limit, f"{name} ends at {self.top}"
        return t

    def bank(self, b, n=NC, at=0):
        return self.psum[:, b * NC + at:b * NC + at + n]

    def sem(self, name, lasting=False):
        s = self.nc.alloc_semaphore(name)
        if not lasting:
            self.phase_sems.append(s)
        return s

    def scratch(self, name, shape, dt=F32):
        self.dram[name] = self.nc.dram_tensor(name, shape, dt, kind="Internal").ap()
        return self.dram[name]


def one(ap, i):
    return ap[bass.ds(i, 1)]


def cols(ap):
    return ap.rearrange("p a n -> p (a n)")


def flat(ap):
    return ap.rearrange("a b n -> (a b) n")


def modulation(m):
    nc, d = m.nc, m.dram
    mask = m.sb("mask", [P, 7 + 2 * LEVELS, P])
    modT = m.sb("modT", [P, 6 * KD, 2])
    small = m.sb("small", [P, 96])
    m.keep.update(mask=mask, modT=modT, ident=mask[:, 0, :], ones=mask[:, 1, :], tri=[mask[:, 2, :], mask[:, 3, :]],
                  before=mask[:, 4, :], neg=[mask[:, 5, :], mask[:, 6, :]],
                  level=[[mask[:, 7 + LEVELS * r + lv, :] for lv in range(LEVELS)] for r in range(2)])
    m.keep.update(small=small, eps_ln=small[:, 68:69], eps_norm=small[:, 69:70])
    ident = m.keep["ident"]
    top = m.top
    m.scratch("mod_rows", [2, NMOD])
    craw = m.sb("craw", [P, KD, 2])
    csil = m.sb("csil", [P, KD, 2])
    brow = m.sb("brow", [2, NMOD])
    mod = m.sb("mod", [2, NMOD])
    wa = [m.sb(f"wa{u}", [P, KD, NC]) for u in range(2)]
    small_loaded, c_ready, cols_ready = m.sem("ada_small"), m.sem("ada_c"), m.sem("ada_cols")
    cols_kept, rows_stored = m.sem("ada_cols_kept"), m.sem("ada_rows_stored")
    loaded = [m.sem(f"ada_loaded{u}") for u in range(2)]
    product = [m.sem(f"ada_product{u}") for u in range(2)]
    kept = [m.sem(f"ada_kept{u}") for u in range(2)]
    w = d["w_ada"].rearrange("(k p) (j n) -> j p k n", p=P, n=NC)
    steps = NMOD // NC // 2

    with nc.Block() as block:
        @block.sync
        def _(sp):
            sp.dma_start(craw[:, :, :], d["c_cols"].rearrange("p (k r) -> p k r", r=2)).then_inc(small_loaded, 16)
            sp.dma_start(brow[:, :], d["b_ada"]).then_inc(small_loaded, 16)
            sp.dma_start(mask[:, :, :], d["masks"].rearrange("p (s n) -> p s n", n=P)).then_inc(small_loaded, 16)
            sp.dma_start(small[:, :], d["small"]).then_inc(small_loaded, 16)
            with sp.Fori(0, steps) as i:
                for u in range(2):
                    sp.wait_ge(product[u], i)
                    sp.dma_start(wa[u][:, :, :], one(w, 2 * i + u).rearrange("j p k n -> (j p) k n")).then_inc(loaded[u], 16)
            sp.wait_ge(kept[0], steps)
            sp.wait_ge(kept[1], steps)
            sp.dma_start(d["mod_rows"], mod[:, :]).then_inc(rows_stored, 16)
            sp.wait_ge(rows_stored, 16)

        @block.scalar
        def _(act):
            act.wait_ge(small_loaded, 64)
            nc.scalar.activation(csil[:, :, :], craw[:, :, :], ACT.Silu).then_inc(c_ready, 1)

        @block.tensor
        def _(pe):
            pe.wait_ge(small_loaded, 64)
            pe.wait_ge(c_ready, 1)
            with pe.Fori(0, steps) as i:
                for u in range(2):
                    pe.wait_ge(loaded[u], 16 * i + 16)
                    pe.wait_ge(kept[u], i)
                    for k in range(KD):
                        last = nc.tensor.matmul(m.bank(u)[0:2, :], csil[:, k, :], wa[u][:, k, :],
                                                start=(k == 0), stop=(k == KD - 1))
                    last.then_inc(product[u], 1)
            pe.wait_ge(kept[0], steps)
            pe.wait_ge(kept[1], steps)
            for j in range(6 * KD):
                last = nc.tensor.matmul(m.bank(2)[:, 2 * j:2 * j + 2], mod[:, j * P:(j + 1) * P], ident[0:2, 0:2],
                                        start=True, stop=True)
            last.then_inc(cols_ready, 1)

        @block.vector
        def _(dve):
            dve.wait_ge(small_loaded, 64)
            with dve.Fori(0, steps) as i:
                for u in range(2):
                    dve.wait_ge(product[u], i + 1)
                    here = bass.ds((2 * i + u) * NC, NC)
                    nc.vector.tensor_tensor(mod[:, here], m.bank(u)[0:2, :], brow[:, here], ALU.add).then_inc(kept[u], 1)
            dve.wait_ge(cols_ready, 1)
            nc.vector.tensor_copy(modT[:, :, :], m.bank(2, 12 * KD).rearrange("p (j r) -> p j r", r=2)).then_inc(cols_kept, 1)
            dve.wait_ge(cols_kept, 1)
            for part in (1, 4):
                nc.vector.tensor_scalar(modT[:, part * KD:(part + 1) * KD, :], modT[:, part * KD:(part + 1) * KD, :],
                                        1.0, None, ALU.add).then_inc(cols_kept, 1)
    m.top = top


def normed_transposed(m):
    nc, d, ident, modT = m.nc, m.dram, m.keep["ident"], m.keep["modT"]
    m.base = m.top
    hT = m.keep["hT"] = m.sb("hT", [P, KD, TOK])
    top = m.top
    RING = 4
    xt = [m.sb(f"xt{u}", [P, D]) for u in range(RING)]
    xn = [m.sb(f"xn{u}", [P, D]) for u in range(2)]
    st = m.sb("ln_st", [P, 2, 6])
    mv = [m.sb(f"ln_mv{u}", [P, 2]) for u in range(2)]
    sd = [m.sb(f"ln_sd{u}", [P, 1]) for u in range(2)]
    loaded = [m.sem(f"x_loaded{u}") for u in range(RING)]
    stats, std = m.sem("x_stats"), m.sem("x_std")
    normed = [m.sem(f"x_normed{u}") for u in range(2)]
    turned = [m.sem(f"x_turned{u}") for u in range(2)]
    kept = [m.sem(f"x_kept{u}") for u in range(2)]
    own = m.sem("x_dve_link")
    x = d["tokens"].rearrange("(t p) n -> t p n", p=P)

    with nc.Block() as block:
        @block.sync
        def _(sp):
            for t in range(TT):
                if t >= RING:
                    sp.wait_ge(normed[t % 2], (t - RING) // 2 + 1)
                sp.dma_start(xt[t % RING][:, :], flat(one(x, t))).then_inc(loaded[t % RING], 16)

        @block.vector
        def _(dve):
            link = Link(dve, own)

            def measure(t):
                dve.wait_ge(loaded[t % RING], 16 * (t // RING) + 16)
                for c in range(2):
                    last = nc.vector.bn_stats(st[:, c, :], xt[t % RING][:, c * NC:(c + 1) * NC])
                link(last)
                link(nc.vector.bn_aggr(mv[t % 2][:, :], st[:, :, :].rearrange("p a b -> p (a b)")))
                dve.sem_inc(stats, 1)

            def norm(t):
                u = t % 2
                dve.wait_ge(std, t + 1)
                link(nc.vector.reciprocal(sd[u][:, :], sd[u][:, :]))
                dve.wait_ge(turned[u], t // 2)
                nc.vector.tensor_scalar(xn[u][:, :], xt[t % RING][:, :], mv[u][:, 0:1], sd[u][:, :],
                                        ALU.subtract, ALU.mult).then_inc(normed[u], 1)

            measure(0)
            for t in range(TT):
                if t + 1 < TT:
                    measure(t + 1)
                norm(t)

        @block.tensor
        def _(pe):
            with pe.Fori(0, TT // 2) as i:
                for u in range(2):
                    pe.wait_ge(normed[u], i + 1)
                    pe.wait_ge(kept[u], i)
                    for k in range(KD):
                        last = nc.tensor.transpose(m.bank(2 * u + k // 4)[:, k % 4 * P:(k % 4 + 1) * P],
                                                   xn[u][:, k * P:(k + 1) * P], ident)
                    last.then_inc(turned[u], 1)

        @block.scalar
        def _(act):
            def deviation(t, i, u):
                act.wait_ge(stats, t + 1)
                act.wait_ge(normed[u], i)
                nc.scalar.activation(sd[u][:, :], mv[u][:, 1:2], ACT.Sqrt, bias=m.keep["eps_ln"]).then_inc(std, 1)

            def leave(t, i, u, r):
                act.wait_ge(turned[u], i + 1)
                for k in range(KD):
                    last = nc.scalar.activation(hT[:, k, bass.ds(t * P, P)],
                                                m.bank(2 * u + k // 4)[:, k % 4 * P:(k % 4 + 1) * P], ACT.Identity,
                                                scale=modT[:, KD + k, r:r + 1], bias=modT[:, k, r:r + 1])
                last.then_inc(kept[u], 1)

            deviation(0, 0, 0)
            deviation(1, 0, 1)
            with act.Fori(0, TL // 2) as i:
                for u in range(2):
                    deviation(2 * i + u + 2, i + 1, u)
                    leave(2 * i + u, i, u, 0)
            for u in range(2):
                leave(TL + u, TL // 2, u, 1)
    m.top = top


def delta_inputs(m):
    nc, d, ident, hT = m.nc, m.dram, m.keep["ident"], m.keep["hT"]
    gap = CONV // 2
    wide = TOK + gap
    wt = m.keep["wt"] = m.sb("wt", [P, KD, TAIL])
    m.keep["wt_loaded"] = m.sem("wt_loaded", lasting=True)
    top = m.top
    m.scratch("qT", [H, P, SEQ])
    m.scratch("kT", [H, P, TOK])
    m.scratch("k", [TT, P, HD])
    m.scratch("v", [TT, P, HD])
    cw = m.sb("cw", [P, 3 * H * CONV])
    wm = [m.sb(f"wm{u}", [P, KD, P]) for u in range(2)]
    padded = [m.sb(f"padded{u}", [P, TOK + 3 * gap]) for u in range(2)]
    conv = [m.sb(f"conv{u}", [P, wide]) for u in range(2)]
    act_out = [m.sb(f"silu{u}", [P, wide]) for u in range(2)]
    raw = [m.sb(f"raw{u}", [P, TT, P]) for u in range(2)]
    nrm = [m.sb(f"nrm{u}", [P, TT, P]) for u in range(2)]
    back = [m.sb(f"back{u}", [P, TOK]) for u in range(2)]
    ssq = m.sb("ssq", [P, TT])
    sd = m.sb("ssd", [P, TT])
    cw_loaded, zeroed = m.sem("cw_loaded"), m.sem("pads_zeroed")
    wm_loaded = [m.sem(f"wm_loaded{u}") for u in range(2)]
    tok_stored = [m.sem(f"heads_tok_stored{u}") for u in range(2)]
    ch_stored = [m.sem(f"heads_ch_stored{u}") for u in range(2)]
    proj, evac, conved, silued = m.sem("c_proj"), m.sem("c_evac"), m.sem("c_conved"), m.sem("c_silued")
    turned, kept, summed, rooted = m.sem("c_turned"), m.sem("c_kept"), m.sem("c_summed"), m.sem("c_rooted")
    normed, returned, rekept = m.sem("c_normed"), m.sem("c_returned"), m.sem("c_rekept")
    own = m.sem("c_dve_link")
    PARTS = 3 * H
    QK = 2 * H

    def tiles(c):
        return TL if c < H else TT

    def groups(c):
        return 2 * c if c < H else 3 * c - H

    def tok_count(c, u):
        return 16 * sum(b >= H for b in range(c) if b % 2 == u)

    with nc.Block() as block:
        @block.sync
        def _(sp):
            sp.dma_start(cw[:, :], d["conv_cols"]).then_inc(cw_loaded, 16)
            for c in range(PARTS):
                if c >= 2:
                    sp.wait_ge(proj, c - 1)
                sp.dma_start(wm[c % 2][:, :, :], d["w_in"][:, c * P:(c + 1) * P].rearrange("(k p) n -> p k n", p=P)
                             ).then_inc(wm_loaded[c % 2], 16)
                if c == 1:
                    sp.dma_start(wt[:, :, :], d["w_in"][:, 3 * HD:].rearrange("(k p) n -> p k n", p=P)
                                 ).then_inc(m.keep["wt_loaded"], 16)

        @block.gpsimd
        def _(pool):
            for u in range(2):
                for at in (0, gap + SEQ, 2 * gap + TOK):
                    last = nc.gpsimd.memset(padded[u][:, at:at + gap], 0.0)
            last.then_inc(zeroed, 1)
            for c in range(PARTS):
                u, h = c % 2, c % H
                if c >= H:
                    pool.wait_ge(normed if c < QK else kept, c + 1)
                    src = nrm[u] if c < QK else raw[u]
                    dst = d["k" if c < QK else "v"][:, :, h * P:(h + 1) * P].rearrange("t p n -> p t n")
                    pool.dma_start(dst, src[:, :, :]).then_inc(tok_stored[u], 16)
                if c < QK:
                    pool.wait_ge(rekept, groups(c + 1))
                    pool.dma_start(d["qT" if c < H else "kT"][h], back[u][:, 0:tiles(c) * P]).then_inc(ch_stored[u], 16)
            for u in range(2):
                pool.wait_ge(tok_stored[u], tok_count(PARTS, u))
                pool.wait_ge(ch_stored[u], 16 * (QK // 2))

        @block.tensor
        def _(pe):
            def project(c):
                pe.wait_ge(wm_loaded[c % 2], 16 * (c // 2 + 1))
                pe.wait_ge(evac, c)
                for b, n in ((0, NC), (1, NC), (2, CTX))[:2 if c < H else 3]:
                    for k in range(KD):
                        last = nc.tensor.matmul(m.bank(b, n), wm[c % 2][:, k, :], hT[:, k, b * NC:b * NC + n],
                                                start=(k == 0), stop=(k == KD - 1))
                last.then_inc(proj, 1)

            def turn(c):
                pe.wait_ge(silued, c + 1)
                pe.wait_ge(kept, c)
                for t in range(tiles(c)):
                    at = t * P + (gap if t >= TL else 0)
                    last = nc.tensor.transpose(m.psum[:, 3 * NC + t * P:3 * NC + (t + 1) * P],
                                               act_out[c % 2][:, at:at + P], ident)
                last.then_inc(turned, 1)

            def turn_back(c):
                pe.wait_ge(normed, c + 1)
                for g, t0 in enumerate(range(0, tiles(c), 4)):
                    n = groups(c) + g
                    if n >= 2:
                        pe.wait_ge(rekept, n - 1)
                    for t in range(t0, min(t0 + 4, tiles(c))):
                        last = nc.tensor.transpose(m.bank(6 + n % 2, P, (t - t0) * P), nrm[c % 2][:, t, :], ident)
                    last.then_inc(returned, 1)

            for c in range(PARTS + 1):
                if c < PARTS:
                    project(c)
                if 2 <= c < QK + 2:
                    turn_back(c - 2)
                if c:
                    turn(c - 1)

        @block.scalar
        def _(act):

            for c in range(PARTS + 1):
                if c < PARTS:
                    u = c % 2
                    act.wait_ge(proj, c + 1)
                    if c >= 2:
                        act.wait_ge(conved, c - 1)
                    if c >= H or c < 2:
                        src = m.psum[:, SEQ:TOK] if c >= H else hT[:, 0, SEQ:TOK]
                        nc.scalar.activation(padded[u][:, 2 * gap + SEQ:2 * gap + TOK], src, ACT.Copy)
                    nc.scalar.activation(padded[u][:, gap:gap + SEQ], m.psum[:, 0:SEQ], ACT.Copy).then_inc(evac, 1)
                if c:
                    b, u = c - 1, (c - 1) % 2
                    act.wait_ge(conved, b + 1)
                    if b >= 2:
                        act.wait_ge(turned, b - 1)
                    nc.scalar.activation(act_out[u][:, :], conv[u][:, :], ACT.Silu).then_inc(silued, 1)
                if 2 <= c < QK + 2:
                    b, u = c - 2, (c - 2) % 2
                    if b >= 2:
                        act.wait_ge(ch_stored[u], 16 * (b // 2))
                    for g, t0 in enumerate(range(0, tiles(b), 4)):
                        n = groups(b) + g
                        act.wait_ge(returned, n + 1)
                        w = (min(t0 + 4, tiles(b)) - t0) * P
                        nc.scalar.activation(back[u][:, t0 * P:t0 * P + w], m.bank(6 + n % 2, w), ACT.Copy
                                             ).then_inc(rekept, 1)
                if c:
                    b, u = c - 1, (c - 1) % 2
                    act.wait_ge(turned, b + 1)
                    if 2 <= b < QK + 2:
                        act.wait_ge(normed, b - 1)
                    if b - 2 >= QK:
                        act.wait_ge(tok_stored[u], tok_count(b - 1, u))
                    n = tiles(b)
                    nc.scalar.activation(raw[u][:, 0:n, :], m.psum[:, 3 * NC:3 * NC + n * P].rearrange("p (t n) -> p t n", n=P),
                                         ACT.Copy).then_inc(kept, 1)
                    if b < QK:
                        act.wait_ge(summed, b + 1)
                        nc.scalar.activation(sd[:, :], ssq[:, :], ACT.Sqrt, bias=m.keep["eps_norm"]).then_inc(rooted, 1)

        @block.vector
        def _(dve):
            link = Link(dve, own)
            dve.wait_ge(cw_loaded, 16)
            dve.wait_ge(zeroed, 1)
            for c in range(PARTS):
                if c < PARTS:
                    u = c % 2
                    dve.wait_ge(evac, c + 1)
                    if c >= 2:
                        dve.wait_ge(silued, c - 1)
                    y = conv[u][:, :]
                    link(nc.vector.tensor_scalar(y, padded[u][:, 0:wide], cw[:, c * CONV:c * CONV + 1], None, ALU.mult))
                    for j in range(1, CONV):
                        ins = nc.vector.scalar_tensor_tensor(y, padded[u][:, j:j + wide], cw[:, c * CONV + j:c * CONV + j + 1],
                                                             y, ALU.mult, ALU.add)
                        if j < CONV - 1:
                            link(ins)
                    ins.then_inc(conved, 1)
                if 1 <= c <= QK:
                    b, u = c - 1, (c - 1) % 2
                    n = tiles(b)
                    dve.wait_ge(kept, b + 1)
                    if b >= 2:
                        dve.wait_ge(returned, groups(b - 1))
                        if b - 2 >= H:
                            dve.wait_ge(tok_stored[u], tok_count(b - 1, u))
                    link(nc.vector.tensor_tensor(nrm[u][:, 0:n, :], raw[u][:, 0:n, :], raw[u][:, 0:n, :], ALU.mult))
                    if n < TT and b == 0:
                        link(nc.vector.memset(ssq[:, TL:TT], 1.0))
                    if b:
                        dve.wait_ge(rooted, b)
                    nc.vector.tensor_reduce(ssq[:, 0:n], nrm[u][:, 0:n, :], AX, ALU.add).then_inc(summed, 1)
                    dve.wait_ge(rooted, b + 1)
                    link(nc.vector.reciprocal(sd[:, :], sd[:, :]))
                    if b < H:
                        link(nc.vector.tensor_scalar(sd[:, :], sd[:, :], float(P) ** -0.5, None, ALU.mult))
                    nc.vector.tensor_tensor(nrm[u][:, 0:n, :], raw[u][:, 0:n, :], sd[:, 0:n].unsqueeze(2).to_broadcast([P, n, P]),
                                            ALU.mult).then_inc(normed, 1)
    m.top = top


def token_inputs(m):
    nc, d, ident, hT, wt = m.nc, m.dram, m.keep["ident"], m.keep["hT"], m.keep["wt"]
    top, m.limit = m.top, m.high
    dkT = m.keep["dkT"] = m.nc.alloc_sbuf_tensor_at("dkT", [P, H, TOK], F32, offset=m.high)
    dv = m.keep["dv"] = m.nc.alloc_sbuf_tensor_at("dv", [P, TT, HD], F32, offset=m.high + 4 * H * TOK)
    gates = m.keep["gates"] = m.nc.alloc_sbuf_tensor_at("gates", [P, TT, 16], F32, offset=m.high + 4 * (H * TOK + TT * HD))
    m.scratch("z", [TL, P, HD])
    m.scratch("dqT", [TL, P, HD])
    lhs = [m.sb(f"lhs{u}", [P, KD, P]) for u in range(2)]
    rope = m.sb("rope", [P, TL, 2, DK])
    qs = [m.sb(f"rope_{n}", [P, HD]) for n in ("qcos", "qsin", "q")]
    ks = [m.sb(f"rope_{n}", [P, HD]) for n in ("kcos", "ksin", "k")]
    zst = [m.sb(f"zst{u}", [P, HD]) for u in range(2)]
    qst = [m.sb(f"qst{u}", [P, HD]) for u in range(2)]
    rope_loaded, lhs_ready = m.sem("rope_loaded"), m.sem("d_lhs_ready")
    qk_proj, rest_kept = m.sem("d_qk_proj"), m.sem("d_rest_kept")
    qk_read, roped, turned, turned_kept = m.sem("d_qk_read"), m.sem("d_roped"), m.sem("d_turned"), m.sem("d_turned_kept")
    rest_proj = [m.sem(f"d_rest_proj{u}") for u in range(2)]
    z_stored = [m.sem(f"z_stored{u}") for u in range(2)]
    q_stored = [m.sem(f"q_stored{u}") for u in range(2)]
    own = m.sem("d_dve_link")
    Z, G, Q, K, V = 0, HD, HD + 16, 2 * HD + 16, 3 * HD + 16

    def tiles(eng, body):
        with eng.Fori(0, TL // 2) as i:
            for u in range(2):
                body(i, u, True)
        for u in range(2):
            body(TL // 2, u, False)

    with nc.Block() as block:
        @block.sync
        def _(sp):
            sp.dma_start(rope[:, :, :, :], d["rope"].rearrange("(t p) (f n) -> p t f n", p=P, f=2)).then_inc(rope_loaded, 16)
            with sp.Fori(0, TL // 2) as i:
                for u in range(2):
                    sp.wait_ge(rest_kept, 2 * i + u + 1)
                    sp.dma_start(flat(one(d["z"], 2 * i + u)), zst[u][:, :]).then_inc(z_stored[u], 16)
                    sp.wait_ge(turned_kept, 2 * i + u + 1)
                    sp.dma_start(flat(one(d["dqT"], 2 * i + u)), qst[u][:, :]).then_inc(q_stored[u], 16)
            for u in range(2):
                sp.wait_ge(z_stored[u], 16 * TL // 2)
                sp.wait_ge(q_stored[u], 16 * TL // 2)

        @block.gpsimd
        def _(pool):
            def body(i, u, latent):
                pool.wait_ge(rest_proj[u], i)
                nc.gpsimd.tensor_copy(lhs[u][:, :, :], hT[:, :, bass.ds((2 * i + u) * P, P)]).then_inc(lhs_ready, 1)
            tiles(pool, body)

        @block.tensor
        def _(pe):
            def group(b, u, at, n):
                for k in range(KD):
                    last = nc.tensor.matmul(m.bank(b, n), lhs[u][:, k, :], wt[:, k, at:at + n],
                                            start=(k == 0), stop=(k == KD - 1))
                return last

            def body(i, u, latent):
                t = 2 * i + u
                pe.wait_ge(lhs_ready, t + 1)
                pe.wait_ge(qk_read, t)
                if latent:
                    group(2, u, Q, HD)
                group(3, u, K, HD).then_inc(qk_proj, 1)
                pe.wait_ge(rest_kept, t)
                if latent:
                    group(0, u, Z, HD)
                group(1, u, V, HD)
                group(4, u, G, 16).then_inc(rest_proj[u], 1)
                pe.wait_ge(roped, t + 1)
                pe.wait_ge(turned_kept, t)
                for b, src in ((5, qs[2]), (6, ks[2])):
                    if latent or b == 6:
                        for h in range(H):
                            last = nc.tensor.transpose(m.bank(b, P, h * P), src[:, h * P:(h + 1) * P], ident)
                last.then_inc(turned, 1)

            pe.wait_ge(m.keep["wt_loaded"], 16)
            tiles(pe, body)

        @block.scalar
        def _(act):
            def body(i, u, latent):
                t = 2 * i + u
                act.wait_ge(rest_proj[u], i + 1)
                if latent:
                    act.wait_ge(z_stored[u], 16 * i)
                    nc.scalar.activation(zst[u][:, :], m.bank(0), ACT.Copy)
                nc.scalar.activation(cols(dv[:, bass.ds(t, 1), :]), m.bank(1), ACT.Copy)
                nc.scalar.activation(cols(gates[:, bass.ds(t, 1), :]), m.bank(4, 16), ACT.Copy).then_inc(rest_kept, 1)
                act.wait_ge(turned, t + 1)
                if latent:
                    act.wait_ge(q_stored[u], 16 * i)
                    nc.scalar.activation(qst[u][:, :], m.bank(5), ACT.Copy)
                nc.scalar.activation(dkT[:, :, bass.ds(t * P, P)], m.bank(6).rearrange("p (h n) -> p h n", h=H),
                                     ACT.Copy).then_inc(turned_kept, 1)
            tiles(act, body)

        @block.vector
        def _(dve):
            def heads(ap):
                return ap.rearrange("p (h n) -> p h n", n=DK)

            def rotate(out, c, s):
                o, c, s = (x[:, :].rearrange("p (h a n) -> p h a n", a=2, n=16) for x in (out, c, s))
                nc.vector.tensor_tensor(o[:, :, 0, :], c[:, :, 0, :], s[:, :, 1, :], ALU.subtract)
                return nc.vector.tensor_tensor(o[:, :, 1, :], c[:, :, 1, :], s[:, :, 0, :], ALU.add)

            dve.wait_ge(rope_loaded, 16)
            with dve.Fori(0, TL // 2) as i:
                for u in range(2):
                    t = 2 * i + u
                    dve.wait_ge(qk_proj, t + 1)
                    for b, (c, s, _) in ((2, qs), (3, ks)):
                        for f, x in enumerate((c, s)):
                            table = rope[:, bass.ds(t, 1), f, :].to_broadcast([P, 2 * H, DK])
                            last = nc.vector.tensor_tensor(heads(x[:, :]), heads(m.bank(b)), table, ALU.mult)
                    last.then_inc(qk_read, 1)
                    dve.wait_ge(qk_read, t + 1)
                    dve.wait_ge(turned, t)
                    rotate(qs[2], qs[0], qs[1])
                    rotate(ks[2], ks[0], ks[1]).then_inc(roped, 1)
                    dve.wait_ge(roped, t + 1)
            for u in range(2):
                t = TL + u
                dve.wait_ge(qk_proj, t + 1)
                dve.wait_ge(turned, t)
                nc.vector.tensor_copy(ks[2][:, :], m.bank(3)).then_inc(roped, 1)
                dve.wait_ge(roped, t + 1)
                dve.sem_inc(qk_read, 1)
    m.top = top


class Events:

    def __init__(self, m, label, names):
        self.names = names.split()
        self.sems = [m.sem(f"{label}_{way}") for way in ("forward", "reverse")]

    def at(self, name, s):
        return s * len(self.names) + self.names.index(name) + 1

    def done(self, ins, name, r):
        assert name in self.names
        ins.then_inc(self.sems[r], 1)

    def wait(self, eng, name, r, s):
        eng.wait_ge(self.sems[r], self.at(name, s))

    def wait_last(self, eng, name, r, s):
        if isinstance(s, int) and s == 0:
            return
        eng.wait_ge(self.sems[r], self.at(name, s - 1))


GATE_KINDS = 7
G_G, G_BETA, G_NGC, G_NEGC, G_EGC, G_ETOT, G_TAIL = range(GATE_KINDS)


def delta_gates(m):
    nc, d = m.nc, m.dram
    gates, tri, ones = m.keep["gates"], m.keep["tri"], m.keep["ones"]
    m.top = m.base
    G = m.keep["G"] = m.sb("G", [P, 2, TT, GATE_KINDS, H])
    top = m.top
    rg = m.sb("rg", [P, 2, 2, H])
    a = m.sb("ga", [P, 2, TT, H])
    b = m.sb("gb", [P, 2, TT, H])
    e = m.sb("ge", [P, 2, TT, H])
    gc = m.sb("ggc", [P, 2, 2, TT, H])
    loaded, dve_did, act_did, sums = m.sem("g_loaded"), m.sem("g_dve"), m.sem("g_act"), m.sem("g_sums")

    def gate(raw, r):
        return raw.rearrange("p t (k r h) -> p t k r h", k=2, r=2)[:, :, :, r, :]

    with nc.Block() as block:
        @block.sync
        def _(sp):
            sp.dma_start(rg[:, :, :, :], d["rep_gates"].rearrange("p (w r h) -> p w r h", w=2, r=2)).then_inc(loaded, 16)

        @block.vector
        def _(dve):
            link = Link(dve, dve_did)
            cp = nc.vector.tensor_copy
            dve.wait_ge(loaded, 16)
            for k, dst in ((0, b), (1, a)):
                cp(dst[:, 0, TC:TT, :], gate(gates, 0)[:, 0:TL, k, :])
                cp(dst[:, 0, 0:TC, :], gate(gates, 0)[:, TL:TT, k, :])
                for s in range(TT):
                    last = cp(dst[:, 1, s, :], gate(gates, 1)[:, TT - 1 - s, k, :])
            link(last)
            link(nc.vector.tensor_tensor(a[:, :, :, :], a[:, :, :, :], rg[:, 0, :, :].unsqueeze(2).to_broadcast([P, 2, TT, H]),
                                         ALU.add))
            link(nc.vector.tensor_scalar(e[:, :, :, :], a[:, :, :, :], -1.0, None, ALU.mult))
            link(nc.vector.tensor_tensor(e[:, :, :, :], e[:, :, :, :], a[:, :, :, :], ALU.min))
            dve.wait_ge(act_did, 4)
            nc.vector.tensor_scalar(a[:, :, :, :], a[:, :, :, :], 0.0, None, ALU.max)
            link(nc.vector.tensor_copy(G[:, :, :, G_BETA, :], b[:, :, :, :]))
            link(nc.vector.tensor_tensor(a[:, :, :, :], a[:, :, :, :], e[:, :, :, :], ALU.add))
            link(nc.vector.tensor_tensor(a[:, :, :, :], a[:, :, :, :], rg[:, 1, :, :].unsqueeze(2).to_broadcast([P, 2, TT, H]),
                                         ALU.mult))
            link(nc.vector.tensor_scalar(a[:, :, :, :], a[:, :, :, :], -1.0, None, ALU.mult))
            nc.vector.tensor_copy(G[:, :, :, G_G, :], a[:, :, :, :])
            dve.wait_ge(sums, 1)
            link(nc.vector.tensor_copy(gc[:, :, :, :, :], m.bank(0, 4 * TT * H).rearrange("p (w r t h) -> p w r t h", w=2, r=2, h=H)))
            link(nc.vector.tensor_scalar(G[:, :, :, G_NGC, :], gc[:, 0], -1.0, None, ALU.mult))
            link(nc.vector.tensor_tensor(e[:, :, :, :], gc[:, 1], gc[:, 0], ALU.subtract))
            dve.wait_ge(act_did, 7)
            nc.vector.tensor_scalar(G[:, :, :, G_NEGC, :], G[:, :, :, G_EGC, :], -1.0, None, ALU.mult)

        @block.scalar
        def _(act):
            link = Link(act, act_did)
            act.wait_ge(dve_did, 4)
            link(nc.scalar.activation(e[:, :, :, :], e[:, :, :, :], ACT.Exp))
            link(nc.scalar.activation(rg[:, 1, :, :], rg[:, 1, :, :], ACT.Exp))
            link(nc.scalar.activation(e[:, :, :, :], e[:, :, :, :], ACT.Ln, bias=1.0))
            link(nc.scalar.activation(b[:, :, :, :], b[:, :, :, :], ACT.Sigmoid))
            act.wait_ge(dve_did, 11)
            link(nc.scalar.activation(G[:, :, :, G_EGC, :], gc[:, 0], ACT.Exp))
            link(nc.scalar.activation(G[:, :, :, G_ETOT, :], gc[:, 1], ACT.Exp))
            link(nc.scalar.activation(G[:, :, :, G_TAIL, :], e[:, :, :, :], ACT.Exp))

        @block.tensor
        def _(pe):
            pe.wait_ge(dve_did, 8)
            n = TT * H
            for w in range(2):
                for r in range(2):
                    last = nc.tensor.matmul(m.bank(0, n, (2 * w + r) * n), ones if w else tri[r],
                                            a[:, r].rearrange("p t h -> p (t h)"), start=True, stop=True)
            last.then_inc(sums, 1)
    m.top = top


def delta_rule(m):
    nc, d = m.nc, m.dram
    BF = mybir.dt.bfloat16
    G, ident, ones, tri, level, neg = (m.keep[n] for n in ("G", "ident", "ones", "tri", "level", "neg"))
    top = m.top
    R2 = range(2)
    m.scratch("o", [2, TT, P, HD])
    W = [P, H, P]
    Q32 = P // 4

    def both(name, shape=W, dt=F32):
        return [m.sb(f"{name}{r}", shape, dt) for r in R2]

    def twice(name):
        return [[m.sb(f"{name}{r}{u}", W) for u in R2] for r in R2]

    kT, qT, kt, vt = twice("e_kT"), twice("e_qT"), twice("e_k"), twice("e_v")
    TTf, attn = twice("e_TT"), twice("e_attn")
    am = twice("e_am")
    tg, dec, at = both("e_tg"), both("e_dec"), both("e_at")
    Tf, pf, R, vn, vn2, osb, S = (both("e_" + n) for n in ("T", "pf", "R", "vn", "vn2", "o", "S"))
    Tc, TTc, pc = (both("e_" + n, [P, H, Q32]) for n in ("Tc", "TTc", "pc"))
    identc = m.sb("identc", [P, Q32])
    quad = m.sb("quad", [P, P])
    nego = m.sb("nego", [P, 2, H, P], BF)
    identb = m.sb("identb", [P, P], BF)
    quad_loaded = m.sem("quad_loaded")
    A, B, C, Sb = (lambda r: r), (lambda r: 2 + r), (lambda r: 4 + r), (lambda r: 6 + r)

    loaded = [[m.sem(f"e_loaded{r}{u}") for u in R2] for r in R2]
    stored = [m.sem(f"o_stored{r}") for r in R2]
    own, ready = m.sem("e_dve_link"), m.sem("e_ready")
    pool_prep = Events(m, "e_pool_prep", "TG " + " ".join(f"AM{lv}" for lv in range(LEVELS)))
    pe_prep = Events(m, "e_pe_prep", "RB KK P0 P1 X1 P2 X2 P3 X3 P4 X4 P5 X5 Y5 KQ P6 Y6")
    act_prep = Events(m, "e_act_prep", "dec P1 P2 P3 P4 P5 P6")
    dve_prep = Events(m, "e_dve_prep", "AT Tc0 T0 Tc1 T1 Tc2 T2 Tc3 T3 Tc4 T4 Tf T5 attn TT")
    pe_scan = Events(m, "e_pe_scan", "KS QS TR AV KV")
    act_scan = Events(m, "e_act_scan", "QS vn2")
    dve_scan = Events(m, "e_dve_scan", "R vn S o")

    def gs(r, s, kind, h=None):
        g = G[:, r, bass.ds(s, 1), kind, :].rearrange("p t h -> p (t h)")
        return g if h is None else g[:, h:h + 1]

    def heads(b, n=P):
        return m.bank(b, H * n).rearrange("p (h n) -> p h n", h=H)

    def halves(ap, b, later):
        v = ap.rearrange("p (g t n) -> p g t n", t=2, n=b)
        return v[:, :, int(later), :]

    def halves_h(ap, b, later):
        v = ap.rearrange("p h (g t n) -> p h g t n", t=2, n=b)
        return v[:, :, :, int(later), :]

    def rounds(eng, order, stages, link=None, links=0):
        def run(s_scan, s_prep):
            for name in order.split():
                kind, s = ("scan", s_scan) if name.startswith("*") else ("prep", s_prep)
                if s is not None:
                    for r in R2:
                        stages[kind, name.lstrip("*")](r, *s)

        link = link or Link(eng, None)
        run(None, (0, 0))
        run((0, 0), (1, 1))
        run((1, 1), (2, 0))
        with link.loop(TT // 2 - 2, 2 * links) as i:
            run((2 * i + 2, 0), (2 * i + 3, 1))
            run((2 * i + 3, 1), (2 * i + 4, 0))
        run((TT - 2, 0), (TT - 1, 1))
        run((TT - 1, 1), None)

    with nc.Block() as block:
        @block.sync
        def _(sp):
            sp.dma_start(quad[:, :], d["quad"][:, 0:P]).then_inc(quad_loaded, 16)
            sp.dma_start(identc[:, :], d["quad"][:, P:P + Q32]).then_inc(quad_loaded, 16)

            def load(r, u, q_src, t, s):
                span = bass.ds(t * P, P)
                for h_src, dst in ((d["kT"], kT), (q_src, qT)):
                    sp.dma_start(dst[r][u][:, :, :], h_src[:, :, span].rearrange("h p n -> p h n")).then_inc(loaded[r][u], 16)
                for src, dst in ((d["k"], kt), (d["v"], vt)):
                    sp.dma_start(dst[r][u][:, :, :], flat(one(src, t)).rearrange("p (h n) -> p h n", h=H)
                                 ).then_inc(loaded[r][u], 16)

            def store(r, s):
                dve_scan.wait(sp, "o", r, s)
                sp.dma_start(flat(one(d["o"][r], s)), osb[r][:, :, :].rearrange("p h n -> p (h n)")).then_inc(stored[r], 16)

            for s in R2:
                for r in R2:
                    load(r, s, d["kT"], TL + s if r == 0 else TT - 1 - s, s)
            with sp.Fori(0, TL // 2) as i:
                mirrored = [i * -2 + (TL - 1 - u) for u in R2]
                for u in R2:
                    s = 2 * i + u
                    for r in R2:
                        pe_scan.wait(sp, "KV", r, s)
                        load(r, u, d["qT"], s if r == 0 else mirrored[u], s)
                        store(r, s)
            for s in (TL, TL + 1):
                for r in R2:
                    store(r, s)
            for r in R2:
                sp.wait_ge(stored[r], 16 * TT)

        @block.gpsimd
        def _(pool):
            def TG(r, s, u):
                pe_prep.wait_last(pool, "RB", r, s)
                ins = nc.gpsimd.tensor_tensor(tg[r][:, :, :], tri[r].unsqueeze(1).to_broadcast(W),
                                              gs(r, s, G_G).unsqueeze(2).to_broadcast(W), ALU.mult)
                pool_prep.done(ins, "TG", r)

            def masked(lv):
                def AM(r, s, u):
                    if lv == 0:
                        dve_prep.wait(pool, "AT", r, s)
                    if lv < 2:
                        pe_prep.wait_last(pool, "P6" if lv == 0 else "P5", r, s)
                    else:
                        pe_prep.wait(pool, f"P{lv - 2}", r, s)
                    ins = nc.gpsimd.tensor_tensor(am[r][lv % 2][:, :, :], at[r][:, :, :],
                                                  level[r][lv].unsqueeze(1).to_broadcast(W), ALU.mult)
                    pool_prep.done(ins, f"AM{lv}", r)
                return AM

            stages = {("prep", "TG"): TG} | {("prep", f"AM{lv}"): masked(lv) for lv in range(LEVELS)}
            rounds(pool, "TG " + " ".join(f"AM{lv}" for lv in range(LEVELS)), stages)

        @block.tensor
        def _(pe):
            mm = nc.tensor.matmul

            def each(out, lhsT, rhs):
                for h in range(H):
                    last = mm(out(h), lhsT(h), rhs(h), start=True, stop=True)
                return last

            def RB(r, s, u):
                pool_prep.wait(pe, "TG", r, s)
                dve_prep.wait_last(pe, "TT", r, s)
                mm(m.bank(A(r)), identb[:, :], nego[:, r, :, :].rearrange("p h n -> p (h n)"), start=True, stop=False)
                pe_prep.done(mm(m.bank(A(r)), ones, tg[r][:, :, :].rearrange("p h n -> p (h n)"), start=False, stop=True),
                             "RB", r)

            def KK(r, s, u):
                pe.wait_ge(loaded[r][u], (s - u) * 32 + 64)
                dve_prep.wait_last(pe, "T5", r, s)
                k = kT[r][u]
                pe_prep.done(each(lambda h: heads(B(r))[:, h, :], lambda h: k[:, h, :], lambda h: k[:, h, :]), "KK", r)

            def KQ(r, s, u):
                dve_scan.wait_last(pe, "o", r, s)
                pe_prep.done(each(lambda h: heads(C(r))[:, h, :], lambda h: kT[r][u][:, h, :], lambda h: qT[r][u][:, h, :]),
                             "KQ", r)

            def product(lv):
                def PL(r, s, u):
                    pool_prep.wait(pe, f"AM{lv}", r, s)
                    a = am[r][lv % 2]
                    if lv == 0:
                        act_prep.wait(pe, "dec", r, s)
                        last = each(lambda h: heads(A(r), Q32)[:, h, :], lambda h: a[:, h, :], lambda h: identc[:, :])
                    elif lv < 5:
                        dve_prep.wait(pe, f"Tc{lv - 1}", r, s)
                        last = each(lambda h: heads(A(r), Q32)[:, h, :], lambda h: a[:, h, :], lambda h: Tc[r][:, h, :])
                    else:
                        dve_prep.wait(pe, "Tf" if lv == 5 else "T5", r, s)
                        last = each(lambda h: heads(A(r))[:, h, :], lambda h: a[:, h, :], lambda h: Tf[r][:, h, :])
                    pe_prep.done(last, f"P{lv}", r)
                return PL

            def left(lv):
                def XL(r, s, u):
                    act_prep.wait(pe, f"P{lv}", r, s)
                    dve_prep.wait(pe, f"T{lv - 1}", r, s)
                    if lv < 5:
                        last = each(lambda h: heads(B(r), Q32)[:, h, :], lambda h: TTf[r][u][:, h, :], lambda h: pc[r][:, h, :])
                    else:
                        last = each(lambda h: heads(B(r), P // 2)[:, h, :], lambda h: TTf[r][u][:, h, :],
                                    lambda h: halves(pf[r][:, h, :], 32, r == 1))
                    pe_prep.done(last, f"X{lv}", r)
                return XL

            def right(lv):
                def YL(r, s, u):
                    act_prep.wait(pe, f"P{lv}", r, s)
                    last = each(lambda h: heads(A(r), P // 2)[:, h, :], lambda h: pf[r][:, h, :],
                                lambda h: halves(TTf[r][u][:, h, :], 1 << lv, r == 0))
                    pe_prep.done(last, f"Y{lv}", r)
                return YL

            def KS(r, s, u):
                dve_scan.wait_last(pe, "S", r, s)
                pe_scan.done(each(lambda h: heads(Sb(r))[:, h, :], lambda h: kT[r][u][:, h, :], lambda h: S[r][:, h, :]), "KS", r)

            def QS(r, s, u):
                dve_prep.wait(pe, "attn", r, s)
                pe_scan.done(each(lambda h: heads(C(r))[:, h, :], lambda h: qT[r][u][:, h, :], lambda h: S[r][:, h, :]), "QS", r)

            def TR(r, s, u):
                dve_scan.wait(pe, "R", r, s)
                dve_prep.wait(pe, "TT", r, s)
                pe_scan.done(each(lambda h: heads(Sb(r))[:, h, :], lambda h: TTf[r][u][:, h, :], lambda h: R[r][:, h, :]), "TR", r)

            def AV(r, s, u):
                dve_scan.wait(pe, "vn", r, s)
                act_scan.wait(pe, "QS", r, s)
                pe_scan.done(each(lambda h: heads(C(r))[:, h, :], lambda h: attn[r][u][:, h, :], lambda h: vn[r][:, h, :]), "AV", r)

            def KV(r, s, u):
                act_scan.wait(pe, "vn2", r, s)
                pe_scan.done(each(lambda h: heads(Sb(r))[:, h, :], lambda h: kt[r][u][:, h, :], lambda h: vn2[r][:, h, :]), "KV", r)

            stages = {("prep", "RB"): RB, ("prep", "KK"): KK, ("prep", "KQ"): KQ, ("prep", "X5"): left(5),
                      ("prep", "Y5"): right(5), ("prep", "Y6"): right(6), ("scan", "KS"): KS, ("scan", "QS"): QS,
                      ("scan", "TR"): TR, ("scan", "AV"): AV, ("scan", "KV"): KV}
            stages |= {("prep", f"P{lv}"): product(lv) for lv in range(LEVELS)}
            stages |= {("prep", f"X{lv}"): left(lv) for lv in range(1, 5)}
            pe.wait_ge(ready, 1)
            pe.wait_ge(quad_loaded, 32)
            rounds(pe, "RB KK *KS *QS P0 P1 X1 *TR P2 X2 P3 X3 *AV *KV P4 X4 P5 X5 Y5 KQ P6 Y6", stages)

        @block.scalar
        def _(act):
            def dec_(r, s, u):
                pe_prep.wait(act, "RB", r, s)
                dve_prep.wait_last(act, "attn", r, s)
                for h in range(H):
                    last = nc.scalar.activation(dec[r][:, h, :], heads(A(r))[:, h, :], ACT.Exp, bias=gs(r, s, G_NGC, h))
                act_prep.done(last, "dec", r)

            def copy(lv):
                def CP(r, s, u):
                    pe_prep.wait(act, f"P{lv}", r, s)
                    if lv == 1:
                        pe_prep.wait_last(act, "X4", r, s)
                    elif lv == 5:
                        pe_prep.wait_last(act, "Y6", r, s)
                    src, dst = (heads(A(r), Q32), pc[r]) if lv < 5 else (heads(A(r)), pf[r])
                    act_prep.done(nc.scalar.activation(dst[:, :, :], src, ACT.Copy), f"P{lv}", r)
                return CP

            def QS(r, s, u):
                pe_scan.wait(act, "QS", r, s)
                act.wait_ge(stored[r], s * 16)
                for h in range(H):
                    last = nc.scalar.activation(osb[r][:, h, :], heads(C(r))[:, h, :], ACT.Copy, scale=gs(r, s, G_EGC, h))
                act_scan.done(last, "QS", r)

            def vn2_(r, s, u):
                dve_scan.wait(act, "vn", r, s)
                pe_scan.wait_last(act, "KV", r, s)
                for h in range(H):
                    last = nc.scalar.activation(vn2[r][:, h, :], vn[r][:, h, :], ACT.Copy, scale=gs(r, s, G_TAIL, h))
                act_scan.done(last, "vn2", r)

            stages = {("prep", "dec"): dec_, ("scan", "QS"): QS, ("scan", "vn2"): vn2_}
            stages |= {("prep", f"P{lv}"): copy(lv) for lv in range(1, LEVELS)}
            rounds(act, "dec *QS P1 *vn2 P2 P3 P4 P5 P6", stages)

        @block.vector
        def _(dve):
            link = Link(dve, own)
            tt, cp, stt = nc.vector.tensor_tensor, nc.vector.tensor_copy, nc.vector.scalar_tensor_tensor
            cp(nego[:, 0, :, :], neg[0].unsqueeze(1).to_broadcast(W))
            cp(nego[:, 1, :, :], neg[1].unsqueeze(1).to_broadcast(W))
            for r in R2:
                nc.vector.memset(S[r][:, :, :], 0.0)
            cp(identb[:, :], ident).then_inc(ready, 1)
            dve.wait_ge(quad_loaded, 32)

            def AT(r, s, u):
                pe_prep.wait(dve, "KK", r, s)
                act_prep.wait(dve, "dec", r, s)
                pool_prep.wait_last(dve, "AM6", r, s)
                for h in range(H):
                    last = stt(at[r][:, h, :], heads(B(r))[:, h, :], gs(r, s, G_BETA, h), dec[r][:, h, :], ALU.mult, ALU.mult)
                dve_prep.done(last, "AT", r)

            def spread(dst, src):
                return tt(dst[:, :, :].rearrange("p h (q n) -> p h q n", q=4), src[:, :, :].unsqueeze(2).to_broadcast([P, H, 4, Q32]),
                          quad[:, :].rearrange("p (q n) -> p q n", q=4).unsqueeze(1).to_broadcast([P, H, 4, Q32]), ALU.mult)

            def doubled(lv):
                def TL_(r, s, u):
                    if lv == 0:
                        pe_prep.wait(dve, "P0", r, s)
                        new = tt(Tc[r][:, :, :], identc[:, :].unsqueeze(1).to_broadcast([P, H, Q32]), heads(A(r), Q32), ALU.subtract)
                        dve_prep.done(new, "Tc0", r)
                    else:
                        pe_prep.wait(dve, f"X{lv}", r, s)
                        dve_prep.done(tt(Tc[r][:, :, :], Tc[r][:, :, :], heads(B(r), Q32), ALU.subtract), f"Tc{lv}", r)
                    dve_prep.wait(dve, f"Tc{lv}", r, s)
                    link(nc.vector.transpose(TTc[r][:, :, :].rearrange("p h n -> p (h n)"),
                                             Tc[r][:, :, :].rearrange("p h n -> p (h n)")))
                    if lv == 0 and not (isinstance(s, int) and s < 2):
                        pe_scan.wait(dve, "TR", r, s - 2)
                    dve_prep.done(spread(TTf[r][u], TTc[r]), f"T{lv}", r)
                return TL_

            def Tf_(r, s, u):
                dve_prep.done(spread(Tf[r], Tc[r]), "Tf", r)

            def T5(r, s, u):
                pe_prep.wait(dve, "Y5", r, s)
                dve_prep.wait(dve, "Tf", r, s)
                for dst, b, later in ((Tf[r], B(r), r == 1), (TTf[r][u], A(r), r == 0)):
                    for h in range(H):
                        v = halves(dst[:, h, :], 32, later)
                        last = tt(v, v, m.bank(b, P // 2, h * P // 2).rearrange("p (g n) -> p g n", g=2), ALU.subtract)
                dve_prep.done(last, "T5", r)

            def TT_(r, s, u):
                pe_prep.wait(dve, "Y6", r, s)
                v = halves_h(TTf[r][u][:, :, :], 64, r == 0).rearrange("p h g n -> p h (g n)")
                dve_prep.done(tt(v, v, heads(A(r), P // 2), ALU.subtract), "TT", r)

            def attn_(r, s, u):
                pe_prep.wait(dve, "KQ", r, s)
                if not (isinstance(s, int) and s < 2):
                    pe_scan.wait(dve, "AV", r, s - 2)
                dve_prep.done(tt(attn[r][u][:, :, :], heads(C(r)), dec[r][:, :, :], ALU.mult), "attn", r)

            def R_(r, s, u):
                pe_scan.wait(dve, "KS", r, s)
                pe_scan.wait_last(dve, "TR", r, s)
                for h in range(H):
                    last = stt(R[r][:, h, :], heads(Sb(r))[:, h, :], gs(r, s, G_NEGC, h), vt[r][u][:, h, :], ALU.mult, ALU.add)
                dve_scan.done(last, "R", r)

            def vn_(r, s, u):
                pe_scan.wait(dve, "TR", r, s)
                dve_scan.done(tt(vn[r][:, :, :], heads(Sb(r)), gs(r, s, G_BETA).unsqueeze(2).to_broadcast(W), ALU.mult), "vn", r)

            def S_(r, s, u):
                pe_scan.wait(dve, "KV", r, s)
                for h in range(H):
                    last = stt(S[r][:, h, :], S[r][:, h, :], gs(r, s, G_ETOT, h), heads(Sb(r))[:, h, :], ALU.mult, ALU.add)
                dve_scan.done(last, "S", r)

            def o_(r, s, u):
                pe_scan.wait(dve, "AV", r, s)
                dve_scan.done(tt(osb[r][:, :, :], osb[r][:, :, :], heads(C(r)), ALU.add), "o", r)

            stages = {("prep", "AT"): AT, ("prep", "Tf"): Tf_, ("prep", "T5"): T5, ("prep", "TT"): TT_, ("prep", "attn"): attn_,
                      ("scan", "R"): R_, ("scan", "vn"): vn_, ("scan", "S"): S_, ("scan", "o"): o_}
            stages |= {("prep", f"T{lv}"): doubled(lv) for lv in range(5)}
            rounds(dve, "AT *R T0 T1 *vn T2 T3 *S *o T4 Tf T5 attn TT", stages, link, 2 * 5)
    m.top = top


def attention(m):
    nc, d, ident = m.nc, m.dram, m.keep["ident"]
    dkT, dv = m.keep["dkT"], m.keep["dv"]
    top = m.top
    m.scratch("od", [TL, P, HD])
    SC = float(DK) ** -0.5
    lamr = m.sb("lamr", [P, 4, DK])
    lprod = m.sb("lprod", [P, 2, DK])
    lsum = m.sb("lsum", [P, 2])
    nlam = m.sb("nlam", [P, 1])
    qT = [m.sb(f"f_qT{u}", [P, H, P]) for u in range(2)]
    E = [[m.sb(f"f_E{p}{c}", [P, TOK]) for c in range(2)] for p in range(2)]
    A = [m.sb(f"f_A{p}", [P, TOK]) for p in range(2)]
    AT = [m.sb(f"f_AT{p}", [P, TT, P]) for p in range(2)]
    mx = [[m.sb(f"f_mx{p}{c}", [P, 1]) for c in range(2)] for p in range(2)]
    rs = [[m.sb(f"f_rs{p}{c}", [P, 1]) for c in range(2)] for p in range(2)]
    cf = m.sb("f_cf", [P, 1])
    r1 = [m.sb(f"f_r1{u}", [P, H]) for u in range(2)]
    ob = [m.sb(f"f_o{u}", [P, H, P]) for u in range(2)]
    lam_loaded, dve_lam, act_lam = m.sem("lam_loaded"), m.sem("lam_dve"), m.sem("lam_act")
    q_loaded = [m.sem(f"f_q_loaded{u}") for u in range(2)]
    stored = [m.sem(f"f_stored{u}") for u in range(2)]
    shared = m.sem("f_shared_bank")
    scored, maxed = m.sem("f_scored"), m.sem("f_maxed")
    exped = [m.sem(f"f_exped{c}") for c in range(2)]
    mixed, summed, tile_kept = m.sem("f_mixed"), m.sem("f_summed"), m.sem("f_tile_kept")
    turned = [m.sem(f"f_turned{p}") for p in range(2)]
    kept = [m.sem(f"f_kept{b}") for b in range(2)]
    own = m.sem("f_dve_link")
    GROUPS = [(0, 4), (4, 4), (8, 2)]

    def tiles(eng, body, link=None, links=0):
        link = link or Link(eng, None)
        with link.loop(TL // 2 - 1, 2 * links) as i:
            for u in range(2):
                body(2 * i + u, i, u, False)
        body(TL - 2, TL // 2 - 1, 0, False)
        body(TL - 1, TL // 2 - 1, 1, True)

    with nc.Block() as block:
        @block.sync
        def _(sp):
            sp.dma_start(lamr[:, :, :], d["rep_lambda"].rearrange("p (a n) -> p a n", n=DK)).then_inc(lam_loaded, 16)

            def load(t, i, u):
                sp.dma_start(qT[u][:, :, :], flat(one(d["dqT"], t)).rearrange("p (h n) -> p h n", h=H)).then_inc(q_loaded[u], 16)

            def store(t, u):
                sp.wait_ge(tile_kept, t + 1)
                sp.dma_start(flat(one(d["od"], t)), ob[u][:, :, :].rearrange("p h n -> p (h n)")).then_inc(stored[u], 16)

            load(0, 0, 0)
            load(1, 0, 1)
            with sp.Fori(0, TL // 2 - 1) as i:
                for u in range(2):
                    t = 2 * i + u
                    store(t, u)
                    load(t + 2, i, u)
            for t in (TL - 2, TL - 1):
                store(t, t % 2)
            for u in range(2):
                sp.wait_ge(stored[u], 16 * (TL // 2))

        @block.tensor
        def _(pe):
            def score(n, u, h):
                def piece(c, at, key, w):
                    rows = slice(c * DK, (c + 1) * DK)
                    return nc.tensor.matmul(m.psum[:, at:at + w], qT[u][rows, h, :], dkT[rows, h, key:key + w],
                                            start=True, stop=True)

                pe.wait_ge(exped[0], n)
                piece(0, 0, 0, NC)
                piece(0, NC, NC, NC)
                pe.wait_ge(exped[1], n)
                piece(0, 2 * NC, 2 * NC, CTX).then_inc(shared, 1)
                piece(1, 3 * NC, CTX, NC)
                piece(1, 4 * NC, CTX + NC, NC)
                pe.wait_ge(shared, n + 1)
                piece(1, TOK, 0, CTX).then_inc(scored, 1)

            def apply(n, h):
                pe.wait_ge(mixed, n + 1)
                for g, (t0, w) in enumerate(GROUPS):
                    pe.wait_ge(kept[g % 2], n if g == 1 else 2 * n + g // 2)
                    for t in range(t0, t0 + w):
                        last = nc.tensor.transpose(m.bank(5 + g % 2, P, (t - t0) * P), A[h % 2][:, t * P:(t + 1) * P], ident)
                    last.then_inc(turned[h % 2], 1)
                pe.wait_ge(kept[0], 2 * n + 2)
                pe.wait_ge(kept[1], n + 1)
                for t in range(TT):
                    last = nc.tensor.matmul(m.bank(7, P, h * P), AT[h % 2][:, t, :], dv[:, t, h * P:(h + 1) * P],
                                            start=(t == 0), stop=(t == TT - 1))
                last.then_inc(summed, 1)

            def body(t, i, u, final):
                for h in range(H):
                    n = t * H + h
                    if h < H - 1:
                        score(n + 1, u, h + 1)
                    elif not final:
                        pe.wait_ge(q_loaded[1 - u], 16 * (i + u) + 16)
                        score(n + 1, 1 - u, 0)
                    if h == 0:
                        pe.wait_ge(tile_kept, t)
                    apply(n, h)

            pe.wait_ge(q_loaded[0], 16)
            score(0, 0, 0)
            tiles(pe, body)

        @block.scalar
        def _(act):
            act.wait_ge(dve_lam, 2)
            nc.scalar.activation(lsum[:, :], lsum[:, :], ACT.Exp).then_inc(act_lam, 1)

            def exps(n, h):
                for c in range(2):
                    act.wait_ge(maxed, n + 1)
                    nc.scalar.activation(E[h % 2][c][:, :], m.psum[:, c * TOK:(c + 1) * TOK], ACT.Exp, bias=mx[h % 2][c][:, :],
                                         scale=SC, accum_out=rs[h % 2][c][:, :]).then_inc(exped[c], 1)

            def keep(t, h):
                for g, (t0, w) in enumerate(GROUPS):
                    act.wait_ge(turned[h % 2], 3 * (t * (H // 2) + h // 2) + g + 1)
                    nc.scalar.activation(AT[h % 2][:, t0:t0 + w, :].rearrange("p t n -> p (t n)"), m.bank(5 + g % 2, w * P), ACT.Copy
                                         ).then_inc(kept[g % 2], 1)

            def body(t, i, u, final):
                for h in range(H):
                    n = t * H + h
                    keep(t, h)
                    if h < H - 1 or not final:
                        exps(n + 1, (h + 1) % H)

            exps(0, 0)
            tiles(act, body)

        @block.vector
        def _(dve):
            link = Link(dve, own)
            dve.wait_ge(lam_loaded, 16)
            for w in range(2):
                last = nc.vector.tensor_tensor(lprod[:, w, :], lamr[:, 2 * w, :], lamr[:, 2 * w + 1, :], ALU.mult)
            last.then_inc(dve_lam, 1)
            dve.wait_ge(dve_lam, 1)
            nc.vector.tensor_reduce(lsum[:, :], lprod[:, :, :], AX, ALU.add).then_inc(dve_lam, 1)
            dve.wait_ge(act_lam, 1)
            link(nc.vector.tensor_tensor(nlam[:, :], lsum[:, 1:2], lsum[:, 0:1], ALU.subtract))
            link(nc.vector.tensor_scalar(nlam[:, :], nlam[:, :], -LAM_INIT, None, ALU.add))

            def maxes(n, h):
                for c in range(2):
                    dve.wait_ge(scored, n + 1)
                    link(nc.vector.tensor_reduce(mx[h % 2][c][:, :], m.psum[:, c * TOK:(c + 1) * TOK], AX, ALU.max))
                    last = nc.vector.tensor_scalar(mx[h % 2][c][:, :], mx[h % 2][c][:, :], -SC, None, ALU.mult)
                last.then_inc(maxed, 1)

            def mix(t, n, h, u):
                dve.wait_ge(exped[1], n + 1)
                nc.vector.reciprocal(r1[u][:, h:h + 1], rs[h % 2][0][:, :])
                link(nc.vector.reciprocal(cf[:, :], rs[h % 2][1][:, :]))
                link(nc.vector.scalar_tensor_tensor(cf[:, :], rs[h % 2][0][:, :], nlam[:, :], cf[:, :], ALU.mult, ALU.mult))
                dve.wait_ge(turned[h % 2], 3 * (t * (H // 2) + h // 2))
                nc.vector.scalar_tensor_tensor(A[h % 2][:, :], E[h % 2][1][:, :], cf[:, :], E[h % 2][0][:, :], ALU.mult, ALU.add
                                               ).then_inc(mixed, 1)

            def body(t, i, u, final):
                for h in range(H):
                    n = t * H + h
                    mix(t, n, h, u)
                    if h < H - 1 or not final:
                        maxes(n + 1, (h + 1) % H)
                dve.wait_ge(summed, H * t + H)
                dve.wait_ge(stored[u], 16 * i)
                nc.vector.tensor_tensor(ob[u][:, :, :], m.bank(7).rearrange("p (h n) -> p h n", h=H),
                                        r1[u][:, :].unsqueeze(2).to_broadcast([P, H, P]), ALU.mult).then_inc(tile_kept, 1)

            maxes(0, 0)
            tiles(dve, body, link, 4 * H)
    m.top = top


def mixed_output(m):
    nc, d, ident = m.nc, m.dram, m.keep["ident"]
    m.top, m.limit = m.base, 229312
    lg = m.keep["lg"] = m.sb("lg", [P, TL, NG + NE])
    m.after = m.top
    rep_mod = m.keep["rep_mod"] = m.sb("rep_mod", [P, D])
    rep_ln = m.keep["rep_ln"] = m.sb("rep_ln", [P, 2, D])
    m.keep["rows_loaded"] = m.sem("rows_loaded", lasting=True)
    yo = m.keep["yo"] = m.sb("yo", [P, TL, D])
    w_route = m.keep["w_route"] = m.sb("w_route", [P, KD, NG + NE])
    top = m.top
    w_out = m.sb("w_out", [P, KD, D])
    nw = m.sb("nw", [P, 2, P])
    of = [m.sb(f"g_of{u}", [P, HD]) for u in range(2)]
    orv = [m.sb(f"g_or{u}", [P, HD]) for u in range(2)]
    zt = [m.sb(f"g_z{u}", [P, HD]) for u in range(2)]
    Y = [m.sb(f"g_Y{u}", [P, 2 * H, P]) for u in range(2)]
    sq = m.sb("g_sq", [P, 2 * H, P])
    ms = [m.sb(f"g_ms{u}", [P, 2 * H]) for u in range(2)]
    yT = [m.sb(f"g_yT{u}", [P, KD, P]) for u in range(2)]
    w_loaded = m.sem("g_w_loaded")
    loaded = [m.sem(f"g_loaded{u}") for u in range(2)]
    gated, summed, rooted, normed = m.sem("g_gated"), m.sem("g_summed"), m.sem("g_rooted"), m.sem("g_normed")
    turned, projected = m.sem("g_turned"), m.sem("g_projected")
    left = [m.sem(f"g_left{u}") for u in range(2)]
    kept = [m.sem(f"g_kept{u}") for u in range(2)]
    own = m.sem("g_dve_link")

    with nc.Block() as block:
        @block.sync
        def _(sp):
            sp.dma_start(nw[:, :, :], d["rep_norm"].rearrange("p (w n) -> p w n", w=2)).then_inc(w_loaded, 16)
            sp.dma_start(w_out[:, :, :], d["w_out"].rearrange("(k p) n -> p k n", p=P)).then_inc(w_loaded, 16)
            with sp.Fori(0, TL // 2) as i:
                for u in range(2):
                    t = 2 * i + u
                    back = i * -2 + (TT - 1 - u)
                    sp.wait_ge(kept[u], i)
                    sp.dma_start(of[u][:, :], flat(one(d["o"][0], t + TC))).then_inc(loaded[u], 16)
                    sp.dma_start(orv[u][:, :], flat(one(d["o"][1], back))).then_inc(loaded[u], 16)
                    sp.dma_start(zt[u][:, :], flat(one(d["z"], t))).then_inc(loaded[u], 16)
                    sp.dma_start(Y[u][:, H:, :], flat(one(d["od"], t)).rearrange("p (h n) -> p h n", h=H)).then_inc(loaded[u], 16)
            sp.dma_start(rep_ln[:, :, :], d["rep_ln"].rearrange("p (w n) -> p w n", w=4)[:, 0:2, :]).then_inc(m.keep["rows_loaded"], 16)
            sp.dma_start(rep_mod[:, :], d["mod_rows"][0:1, 2 * D:3 * D].to_broadcast([P, D])).then_inc(m.keep["rows_loaded"], 16)
            sp.dma_start(w_route[:, :, :], d["w_route"].rearrange("(k p) n -> p k n", p=P)).then_inc(m.keep["rows_loaded"], 16)

        @block.scalar
        def _(act):
            def gate(t, i, u):
                act.wait_ge(loaded[u], 64 * i + 64)
                nc.scalar.activation(zt[u][:, :], zt[u][:, :], ACT.Silu).then_inc(gated, 1)
                act.wait_ge(summed, t + 1)
                nc.scalar.activation(ms[u][:, :], ms[u][:, :], ACT.Sqrt, bias=m.keep["eps_norm"], scale=1.0 / P).then_inc(rooted, 1)

            def keep(t, u):
                act.wait_ge(turned, t + 1)
                nc.scalar.activation(yT[u][:, :, :].rearrange("p k n -> p (k n)"), m.psum[:, 2 * u * NC:2 * u * NC + D], ACT.Copy
                                     ).then_inc(kept[u], 1)

            def leave(t, u):
                act.wait_ge(projected, t + 1)
                nc.scalar.activation(cols(yo[:, bass.ds(t, 1), :]), m.psum[:, (4 + 2 * u) * NC:(6 + 2 * u) * NC], ACT.Copy
                                     ).then_inc(left[u], 1)

            gate(0, 0, 0)
            gate(1, 0, 1)
            keep(0, 0)
            with act.Fori(0, TL // 2 - 1) as i:
                for u in range(2):
                    keep(2 * i + 1 + u, 1 - u)
                    gate(2 * i + 2 + u, i + 1, u)
                    leave(2 * i + u, u)
            keep(TL - 1, 1)
            leave(TL - 2, 0)
            leave(TL - 1, 1)

        @block.vector
        def _(dve):
            link = Link(dve, own)
            tt = nc.vector.tensor_tensor
            W8 = [P, 2 * H, P]
            dve.wait_ge(w_loaded, 32)
            link(nc.vector.tensor_scalar(nw[:, 1, :], nw[:, 1, :], 1.0 - LAM_INIT, None, ALU.mult))
            with link.loop(TL // 2, 2 * 5) as i:
                for u in range(2):
                    t = 2 * i + u
                    dve.wait_ge(loaded[u], 64 * i + 64)
                    link(tt(Y[u][:, 0:H, :].rearrange("p h n -> p (h n)"), of[u][:, :], orv[u][:, :], ALU.add))
                    link(tt(sq[:, :, :], Y[u][:, :, :], Y[u][:, :, :], ALU.mult))
                    nc.vector.tensor_reduce(ms[u][:, :], sq[:, :, :], AX, ALU.add).then_inc(summed, 1)
                    dve.wait_ge(rooted, t + 1)
                    link(nc.vector.reciprocal(ms[u][:, :], ms[u][:, :]))
                    link(tt(Y[u][:, :, :], Y[u][:, :, :], ms[u][:, :].unsqueeze(2).to_broadcast(W8), ALU.mult))
                    nc.vector.tensor_tensor(Y[u][:, 0:H, :], Y[u][:, 0:H, :], nw[:, 0, :].unsqueeze(1).to_broadcast([P, H, P]), ALU.mult)
                    link(tt(Y[u][:, H:, :], Y[u][:, H:, :], nw[:, 1, :].unsqueeze(1).to_broadcast([P, H, P]), ALU.mult))
                    dve.wait_ge(gated, t + 1)
                    tt(Y[u][:, 0:H, :].rearrange("p h n -> p (h n)"), Y[u][:, 0:H, :].rearrange("p h n -> p (h n)"), zt[u][:, :],
                       ALU.mult).then_inc(normed, 1)

        @block.tensor
        def _(pe):
            def turn(t, i, u):
                pe.wait_ge(normed, t + 1)
                pe.wait_ge(kept[u], i)
                for k in range(KD):
                    last = nc.tensor.transpose(m.psum[:, 2 * u * NC + k * P:2 * u * NC + (k + 1) * P], Y[u][:, k, :], ident)
                last.then_inc(turned, 1)

            def project(i, u):
                pe.wait_ge(kept[u], i + 1)
                pe.wait_ge(left[u], i)
                for c in range(2):
                    for k in range(KD):
                        last = nc.tensor.matmul(m.bank(4 + 2 * u + c), yT[u][:, k, :], w_out[:, k, c * NC:(c + 1) * NC],
                                                start=(k == 0), stop=(k == KD - 1))
                last.then_inc(projected, 1)

            pe.wait_ge(w_loaded, 32)
            turn(0, 0, 0)
            with pe.Fori(0, TL // 2 - 1) as i:
                turn(2 * i + 1, i, 1)
                project(i, 0)
                turn(2 * i + 2, i + 1, 0)
                project(i, 1)
            turn(TL - 1, TL // 2 - 1, 1)
            project(TL // 2 - 1, 0)
            project(TL // 2 - 1, 1)
    m.top = top


def layer_norm_stats(nc, dve, link, st, mv, src, plain=False):
    for c in range(2):
        last = nc.vector.bn_stats(st[:, c, :], src[:, c * NC:(c + 1) * NC])
    link(last, plain=plain)
    link(nc.vector.bn_aggr(mv[:, :], st[:, :, :].rearrange("p a b -> p (a b)")))


def residual_and_logits(m):
    nc, d, ident, modT = m.nc, m.dram, m.keep["ident"], m.keep["modT"]
    rep_mod, rep_ln, yo, lg = (m.keep[n] for n in ("rep_mod", "rep_ln", "yo", "lg"))
    w_route = m.keep["w_route"]
    m.scratch("x1", [TL, P, D])
    m.scratch("xn2", [SEQ, D])
    m.scratch("token_of", [(BLOCKS + 2) * P, 1], I32)
    st = m.sb("h_st", [P, 2, 6])
    mv = [[m.sb(f"h_mv{w}{u}", [P, 2]) for u in range(2)] for w in range(2)]
    sd = [[m.sb(f"h_sd{w}{u}", [P, 1]) for u in range(2)] for w in range(2)]
    xt = [m.sb(f"h_x{u}", [P, D]) for u in range(2)]
    x1 = [m.sb(f"h_x1{u}", [P, D]) for u in range(2)]
    xn = [m.sb(f"h_xn{u}", [P, D]) for u in range(2)]
    h2T = [m.sb(f"h_h2T{u}", [P, KD, P]) for u in range(2)]
    none = m.sb("h_none", [P, BLOCKS + 2], I32)
    loaded = [m.sem(f"h_loaded{u}") for u in range(2)]
    x1_stored = [m.sem(f"h_x1_stored{u}") for u in range(2)]
    xn_stored = [m.sem(f"h_xn_stored{u}") for u in range(2)]
    scaled, shaped, normed = m.sem("h_scaled"), m.sem("h_shaped"), m.sem("h_normed")
    stats, std = ([m.sem(f"h_{n}{w}") for w in range(2)] for n in ("stats", "std"))
    added, routed, biased = m.sem("h_added"), m.sem("h_routed"), m.sem("h_logits_kept")
    turned = [m.sem(f"h_turned{u}") for u in range(2)]
    kept = [m.sem(f"h_kept{u}") for u in range(2)]
    cleared, clear_stored, own = m.sem("h_cleared"), m.sem("h_clear_stored"), m.sem("h_dve_link")
    x = d["tokens"].rearrange("(t p) n -> t p n", p=P)
    xn2 = d["xn2"].rearrange("(t p) n -> t p n", p=P)

    with nc.Block() as block:
        @block.sync
        def _(sp):
            def load(t, u):
                sp.dma_start(xt[u][:, :], flat(one(x, t))).then_inc(loaded[u], 16)

            def store(t, u):
                sp.wait_ge(shaped, t + 1)
                sp.dma_start(flat(one(d["x1"], t)), x1[u][:, :]).then_inc(x1_stored[u], 16)
                sp.wait_ge(normed, t + 1)
                sp.dma_start(flat(one(xn2, t)), xn[u][:, :]).then_inc(xn_stored[u], 16)

            sp.wait_ge(cleared, 1)
            sp.dma_start(d["token_of"].rearrange("(p b) a -> p (b a)", p=P), none[:, :]).then_inc(clear_stored, 16)
            for u in range(2):
                load(u, u)
            with sp.Fori(0, TL // 2 - 1) as i:
                for u in range(2):
                    sp.wait_ge(added, 2 * i + u + 1)
                    load(2 * i + u + 2, u)
                    store(2 * i + u, u)
            for u in range(2):
                store(TL - 2 + u, u)
            for u in range(2):
                sp.wait_ge(x1_stored[u], 16 * (TL // 2))
                sp.wait_ge(xn_stored[u], 16 * (TL // 2))
            sp.wait_ge(clear_stored, 16)

        @block.gpsimd
        def _(pool):
            nc.gpsimd.memset(none[:, :], 0).then_inc(cleared, 1)
            pool.wait_ge(m.keep["rows_loaded"], 48)
            with pool.Fori(0, TL) as t:
                y = cols(yo[:, bass.ds(t, 1), :])
                nc.gpsimd.tensor_tensor(y, y, rep_mod[:, :], ALU.mult).then_inc(scaled, 1)

        @block.vector
        def _(dve):
            link = Link(dve, own)
            tt = nc.vector.tensor_tensor
            dve.wait_ge(m.keep["rows_loaded"], 48)

            def add(t, i, u):
                dve.wait_ge(scaled, t + 1)
                dve.wait_ge(loaded[u], 16 * i + 16)
                dve.wait_ge(x1_stored[u], 16 * i)
                nc.vector.scalar_tensor_tensor(x1[u][:, :], xt[u][:, :], ALPHA, cols(yo[:, bass.ds(t, 1), :]), ALU.mult, ALU.add
                                               ).then_inc(added, 1)
                dve.wait_ge(added, t + 1)
                layer_norm_stats(nc, dve, link, st, mv[0][u], x1[u], plain=True)
                dve.sem_inc(stats[0], 1)

            def norm(t, u):
                dve.wait_ge(std[0], t + 1)
                link(nc.vector.reciprocal(sd[0][u][:, :], sd[0][u][:, :]))
                link(nc.vector.tensor_scalar(x1[u][:, :], x1[u][:, :], mv[0][u][:, 0:1], sd[0][u][:, :], ALU.subtract, ALU.mult))
                link(tt(x1[u][:, :], x1[u][:, :], rep_ln[:, 0, :], ALU.mult))
                tt(x1[u][:, :], x1[u][:, :], rep_ln[:, 1, :], ALU.add).then_inc(shaped, 1)
                dve.wait_ge(shaped, t + 1)
                layer_norm_stats(nc, dve, link, st, mv[1][u], x1[u], plain=True)
                dve.sem_inc(stats[1], 1)

            def norm_again(t, i, u):
                dve.wait_ge(std[1], t + 1)
                link(nc.vector.reciprocal(sd[1][u][:, :], sd[1][u][:, :]))
                dve.wait_ge(turned[u], i)
                dve.wait_ge(xn_stored[u], 16 * i)
                link(nc.vector.tensor_scalar(xn[u][:, :], x1[u][:, :], mv[1][u][:, 0:1], sd[1][u][:, :], ALU.subtract, ALU.mult))
                dve.sem_inc(normed, 1)

            add(0, 0, 0)
            add(1, 0, 1)
            norm(0, 0)
            with link.loop(TL // 2 - 1, 2 * 11) as i:
                for u in range(2):
                    norm_again(2 * i + u, i, u)
                    norm(2 * i + u + 1, 1 - u)
                    add(2 * i + u + 2, i + 1, u)
            norm_again(TL - 2, TL // 2 - 1, 0)
            norm(TL - 1, 1)
            norm_again(TL - 1, TL // 2 - 1, 1)

        @block.scalar
        def _(act):
            def deviation(w, t, u):
                act.wait_ge(stats[w], t + 1)
                nc.scalar.activation(sd[w][u][:, :], mv[w][u][:, 1:2], ACT.Sqrt, bias=m.keep["eps_ln"]).then_inc(std[w], 1)

            def leave(t, i, u):
                act.wait_ge(turned[u], i + 1)
                for k in range(KD):
                    last = nc.scalar.activation(h2T[u][:, k, :], m.bank(2 * u + k // 4)[:, k % 4 * P:(k % 4 + 1) * P], ACT.Identity,
                                                scale=modT[:, 4 * KD + k, 0:1], bias=modT[:, 3 * KD + k, 0:1])
                last.then_inc(kept[u], 1)
                act.wait_ge(routed, t + 1)
                nc.scalar.activation(cols(lg[:, bass.ds(t, 1), :]), m.bank(4, NG + NE), ACT.Copy).then_inc(biased, 1)

            deviation(0, 0, 0)
            deviation(0, 1, 1)
            deviation(1, 0, 0)
            with act.Fori(0, TL // 2 - 1) as i:
                for u in range(2):
                    deviation(1, 2 * i + u + 1, 1 - u)
                    deviation(0, 2 * i + u + 2, u)
                    leave(2 * i + u, i, u)
            deviation(1, TL - 1, 1)
            leave(TL - 2, TL // 2 - 1, 0)
            leave(TL - 1, TL // 2 - 1, 1)

        @block.tensor
        def _(pe):
            pe.wait_ge(m.keep["rows_loaded"], 48)
            with pe.Fori(0, TL // 2) as i:
                for u in range(2):
                    t = 2 * i + u
                    pe.wait_ge(normed, t + 1)
                    pe.wait_ge(kept[u], i)
                    for k in range(KD):
                        last = nc.tensor.transpose(m.bank(2 * u + k // 4)[:, k % 4 * P:(k % 4 + 1) * P],
                                                   xn[u][:, k * P:(k + 1) * P], ident)
                    last.then_inc(turned[u], 1)
                    pe.wait_ge(kept[u], i + 1)
                    pe.wait_ge(biased, t)
                    for k in range(KD):
                        last = nc.tensor.matmul(m.bank(4, NG + NE), h2T[u][:, k, :], w_route[:, k, :], start=(k == 0), stop=(k == KD - 1))
                    last.then_inc(routed, 1)
    m.top = m.after


def load_expert(m, sp, place, u, used):
    plan = m.keep["plan"]
    e = sp.value_load(plan[0:1, bass.ds(place + PLAN_EXPERT, 1)], min_val=0, max_val=NE - 1)
    if used:
        end = sp.value_load(plan[0:1, bass.ds(place + (PLAN_END - 2), 1)], min_val=1, max_val=BLOCKS)
    for n, W in m.keep["weights"].items():
        if used:
            sp.wait_ge(used[n], end)
        src = m.dram[f"w_{n}"].rearrange("e (k p) n -> e p k n", p=P)
        sp.dma_start(W[:, u, :, :], one(src, e).rearrange("e p k n -> (e p) k n")).then_inc(m.keep["weights_loaded"][n][u], 16)


def routing(m):
    nc, d, small, ones, before, lg = m.nc, m.dram, m.keep["small"], m.keep["ones"], m.keep["before"], m.keep["lg"]
    gate = m.keep["gate"] = m.sb("gate", [P, 2, TL])
    row = m.keep["row"] = m.sb("row", [P, 2, TL], I32)
    plan = m.keep["plan"] = m.sb("plan", [P, PLAN], I32)
    tok = m.keep["tok"] = m.sb("tok", [P, BLOCKS + 2], I32)
    weights_at = m.top
    weights = m.keep["weights"] = {"gate": m.sb("w_gate", [P, 2, KD, DE]), "up": m.sb("w_up", [P, 2, KD, DE]),
                                   "down": m.sb("w_down", [P, 2, DE // P, D])}
    m.keep["rests"] = {n: nc.alloc_sbuf_tensor_at(f"rest_{n}", w.shape, F32R, offset=weights_at + at * 8 * KD * DE)
                       for at, (n, w) in enumerate(weights.items())}
    weights_loaded = m.keep["weights_loaded"] = {n: [m.sem(f"w_{n}_loaded{u}", lasting=True) for u in range(2)] for n in weights}
    top = m.top
    T8 = [P, TL]
    names = "gmax gsum pg best tie m1 m2 e2 den".split()
    v = {n: m.sb("r_" + n, T8) for n in names}
    rb = m.sb("r_bias", [P, NG + NE])
    oh = m.sb("r_group", [P, TL, NG])
    eg = m.sb("r_eg", [P, TL, NG])
    pick = m.sb("r_pick", [P, TL, NG, EG])
    li = m.sb("r_li", [P, TL, EG])
    ohs = [m.sb(f"r_first{j}", [P, TL, EG]) for j in range(2)]
    E = [m.sb(f"r_E{j}", [P, TL, NE]) for j in range(2)]
    M = m.sb("r_M", [P, TL, NE])
    rank = m.sb("r_rank", [P, TL, NE])
    cnt = m.sb("r_cnt", [P, NE])
    nblk = m.sb("r_nblk", [P, NE])
    ends = m.sb("r_ends", [P, NE])
    base = m.sb("r_base", [P, NE])
    onesr = m.sb("r_ones", [P, NE])
    over = m.sb("r_over", [P, NE, EG])
    own_of = m.sb("r_own", [P, BLOCKS, NE])
    some = m.sb("r_some", [P, NE])
    nth = m.sb("r_nth", [P, NE])
    upto = m.sb("r_upto", [P, NE, NE])
    last_ = m.sb("r_last", [P, 1])
    planf = m.sb("r_planf", [P, PLAN])
    rowf = m.sb("r_rowf", [P, 2, TL])
    ids = m.sb("r_ids", [P, TL], I32)
    loaded, dve_did, act_did, counted = m.sem("r_loaded"), m.sem("r_dve"), m.sem("r_act"), m.sem("r_counted")
    planned = m.sem("r_planned")
    rows_ready, chosen, scattered, tok_loaded = m.sem("r_rows_ready"), m.sem("r_chosen"), m.sem("r_scattered"), m.sem("r_tok_loaded")
    desc = {NG: small[:, 0:4], EG: small[:, 4:12]}

    with nc.Block() as block:
        @block.sync
        def _(sp):
            sp.dma_start(ids[:, :], d["ids"]).then_inc(loaded, 16)
            sp.dma_start(rb[:, :], d["rep_route"]).then_inc(loaded, 16)
            sp.wait_ge(planned, 1)
            load_expert(m, sp, 0, 0, None)
            load_expert(m, sp, 1, 1, None)

        @block.gpsimd
        def _(pool):
            pool.wait_ge(loaded, 32)
            pool.wait_ge(rows_ready, 1)
            for j in range(2):
                for t in range(TL):
                    pool.indirect_dma_start(out=d["token_of"], out_offset=bass.IndirectOffsetOnAxis(ap=row[:, j, t:t + 1], axis=0),
                                            in_=ids[:, t:t + 1], in_offset=None).then_inc(scattered, 16)

        @block.vector
        def _(dve):
            link = Link(dve, dve_did)
            tt, ts, red = nc.vector.tensor_tensor, nc.vector.tensor_scalar, nc.vector.tensor_reduce

            def wide(ap, n):
                return ap.unsqueeze(2).to_broadcast([P, TL, n])

            def first_of(out, values, top_, n):
                link(tt(out, values, wide(top_[:, :], n), ALU.is_equal))
                link(tt(out, out, desc[n].unsqueeze(1).to_broadcast([P, TL, n]), ALU.mult))
                link(red(v["tie"][:, :], out, AX, ALU.max))
                link(tt(out, out, wide(v["tie"][:, :], n), ALU.is_equal))

            dve.wait_ge(loaded, 32)
            link(tt(lg[:, :, :], lg[:, :, :], rb[:, :].unsqueeze(1).to_broadcast([P, TL, NG + NE]), ALU.add))
            g, e = lg[:, :, 0:NG], lg[:, :, NG:]
            link(red(v["gmax"][:, :], g, AX, ALU.max))
            link(tt(eg[:, :, :], g, wide(v["gmax"][:, :], NG), ALU.subtract))
            dve.sem_inc(chosen, 1)
            first_of(oh[:, :, :], g, v["gmax"], NG)
            link(tt(pick[:, :, :, :], e.rearrange("p t (g e) -> p t g e", g=NG),
                    oh[:, :, :].unsqueeze(3).to_broadcast([P, TL, NG, EG]), ALU.mult))
            link(red(li[:, :, :], pick[:, :, :, :].rearrange("p t g e -> p t e g"), AX, ALU.add))
            link(red(v["m1"][:, :], li[:, :, :], AX, ALU.max))
            first_of(ohs[0][:, :, :], li[:, :, :], v["m1"], EG)
            link(nc.vector.scalar_tensor_tensor(li[:, :, :], ohs[0][:, :, :], -BIG, li[:, :, :], ALU.mult, ALU.add))
            link(red(v["m2"][:, :], li[:, :, :], AX, ALU.max))
            first_of(ohs[1][:, :, :], li[:, :, :], v["m2"], EG)
            link(tt(v["e2"][:, :], v["m2"][:, :], v["m1"][:, :], ALU.subtract))
            dve.sem_inc(chosen, 1)
            for j in range(2):
                last = tt(E[j][:, :, :].rearrange("p t (g e) -> p t g e", g=NG), oh[:, :, :].unsqueeze(3).to_broadcast([P, TL, NG, EG]),
                          ohs[j][:, :, :].unsqueeze(2).to_broadcast([P, TL, NG, EG]), ALU.mult)
            link(last)
            link(tt(M[:, :, :], E[0][:, :, :], E[1][:, :, :], ALU.add))
            dve.sem_inc(chosen, 1)
            dve.wait_ge(act_did, 2)
            link(red(v["gsum"][:, :], eg[:, :, :], AX, ALU.add))
            link(ts(v["den"][:, :], v["e2"][:, :], 1.0, None, ALU.add))
            link(tt(v["den"][:, :], v["den"][:, :], v["gsum"][:, :], ALU.mult))
            link(nc.vector.reciprocal(gate[:, 0, :], v["den"][:, :]))
            link(tt(gate[:, 1, :], gate[:, 0, :], v["e2"][:, :], ALU.mult))
            dve.wait_ge(counted, 1)
            nc.vector.tensor_copy(rank[:, :, :], m.bank(0, TL * NE).rearrange("p (t e) -> p t e", e=NE))
            nc.vector.memset(onesr[:, :], 1.0)
            link(nc.vector.tensor_copy(cnt[:, :], m.bank(1, NE)))
            link(tt(over[:, :, :], cnt[:, :].unsqueeze(2).to_broadcast([P, NE, EG]), small[:, 12:20].unsqueeze(1).to_broadcast([P, NE, EG]),
                    ALU.is_gt))
            link(red(nblk[:, :], over[:, :, :], AX, ALU.add))
            link(nc.vector.tensor_tensor_scan(ends[:, :], onesr[:, :], nblk[:, :], 0.0, ALU.mult, ALU.add))
            link(tt(base[:, :], ends[:, :], nblk[:, :], ALU.subtract))
            link(ts(base[:, :], base[:, :], float(P), None, ALU.mult))
            link(tt(rank[:, :, :], rank[:, :, :], base[:, :].unsqueeze(1).to_broadcast([P, TL, NE]), ALU.add))
            for j in range(2):
                link(tt(M[:, :, :], E[j][:, :, :], rank[:, :, :], ALU.mult))
                link(red(rowf[:, j, :], M[:, :, :], AX, ALU.add))
            nc.vector.tensor_copy(row[:, :, :], rowf[:, :, :]).then_inc(rows_ready, 1)
            link(ts(some[:, :], nblk[:, :], 1.0, None, ALU.min))
            link(nc.vector.tensor_tensor_scan(nth[:, :], onesr[:, :], some[:, :], 0.0, ALU.mult, ALU.add))
            place = small[:, 20:20 + NE].unsqueeze(2).to_broadcast([P, NE, NE])
            link(tt(upto[:, :, :], nth[:, :].unsqueeze(1).to_broadcast([P, NE, NE]), place, ALU.is_le))
            link(red(planf[:, PLAN_EXPERT:PLAN_EXPERT + NE], upto[:, :, :], AX, ALU.add))
            link(ts(planf[:, PLAN_EXPERT:PLAN_EXPERT + NE], planf[:, PLAN_EXPERT:PLAN_EXPERT + NE], float(NE - 1), None, ALU.min))
            place = small[:, 21:21 + NE].unsqueeze(2).to_broadcast([P, NE, NE])
            link(tt(upto[:, :, :], nth[:, :].unsqueeze(1).to_broadcast([P, NE, NE]), place, ALU.is_le))
            link(tt(upto[:, :, :], upto[:, :, :], nblk[:, :].unsqueeze(1).to_broadcast([P, NE, NE]), ALU.mult))
            link(red(planf[:, PLAN_END:PLAN_END + NE], upto[:, :, :], AX, ALU.add))
            link(tt(own_of[:, :, :], ends[:, :].unsqueeze(1).to_broadcast([P, BLOCKS, NE]),
                    small[:, 20:20 + BLOCKS].unsqueeze(2).to_broadcast([P, BLOCKS, NE]), ALU.is_le))
            link(tt(own_of[:, :, :], own_of[:, :, :], some[:, :].unsqueeze(1).to_broadcast([P, BLOCKS, NE]), ALU.mult))
            rank_of = planf[:, PLAN_RANK:PLAN_RANK + BLOCKS]
            link(red(rank_of, own_of[:, :, :], AX, ALU.add))
            link(ts(last_[:, :], nth[:, NE - 1:NE], -1.0, None, ALU.add))
            link(tt(rank_of, rank_of, last_[:, :].to_broadcast([P, BLOCKS]), ALU.min))
            link(nc.vector.tensor_copy(planf[:, PLAN_BLOCKS:PLAN_BLOCKS + 1], ends[:, NE - 1:NE]))
            link(nc.vector.tensor_copy(planf[:, PLAN_EXPERTS:], nth[:, NE - 1:NE]))
            nc.vector.tensor_copy(plan[:, :], planf[:, :]).then_inc(planned, 1)

        @block.scalar
        def _(act):
            act.wait_ge(chosen, 1)
            nc.scalar.activation(eg[:, :, :], eg[:, :, :], ACT.Exp).then_inc(act_did, 1)
            act.wait_ge(chosen, 2)
            nc.scalar.activation(v["e2"][:, :], v["e2"][:, :], ACT.Exp).then_inc(act_did, 1)
            act.wait_ge(scattered, 16 * 2 * TL)
            act.dma_start(tok[:, :], d["token_of"].rearrange("(b p) a -> p (b a)", p=P),
                          allow_slow_non_contiguous=True).then_inc(tok_loaded, 16)
            act.wait_ge(tok_loaded, 16)

        @block.tensor
        def _(pe):
            pe.wait_ge(chosen, 3)
            for t in range(TL):
                for b in range(t):
                    nc.tensor.matmul(m.bank(0, NE, t * NE), ones, M[:, b, :], start=(b == 0), stop=False)
                nc.tensor.matmul(m.bank(0, NE, t * NE), before, M[:, t, :], start=(t == 0), stop=True)
            for t in range(TL):
                last = nc.tensor.matmul(m.bank(1, NE), ones, M[:, t, :], start=(t == 0), stop=(t == TL - 1))
            last.then_inc(counted, 1)
    m.top = top


def experts(m):
    nc, d, ident, modT, plan, tok = m.nc, m.dram, m.keep["ident"], m.keep["modT"], m.keep["plan"], m.keep["tok"]
    top = m.top
    m.scratch("yb", [BLOCKS * P, D])
    KE, HALF = DE // P, DE // 2
    CH = 4
    W, rests, loads = m.keep["weights"], m.keep["rests"], m.keep["weights_loaded"]
    heads = {"gate": m.sb("head_gate", [P, KD, DE], F32R), "up": m.sb("head_up", [P, KD, DE], F32R),
             "down": m.sb("head_down", [P, KE, D], F32R)}
    idx = [m.sb(f"i_idx{u}", [P, 1], I32) for u in range(2)]
    xg = [m.sb(f"i_x{u}", [P, D]) for u in range(2)]
    xm = m.sb("i_xm", [P, KD, P])
    xh, xr = ([m.sb(f"i_x_{n}{u}", [P, KD, P], F32R) for u in range(2)] for n in ("head", "rest"))
    nothing = m.sb("i_nothing", [P, D])
    hs = m.sb("i_silu", [P, DE])
    hh = m.sb("i_h", [P, DE])
    hTh, hTr = (m.sb(f"i_hT_{n}", [P, KE, P], F32R) for n in ("head", "rest"))
    yo = [m.sb(f"i_y{u}", [P, D]) for u in range(2)]
    U2 = range(2)
    used = {n: m.sem(f"i_{n}_used") for n in W}
    first_half = {n: m.sem(f"i_{n}_first_half") for n in ("gate", "up")}
    head, rest = ({n: m.sem(f"i_{n}_{part}") for n in W} for part in ("head", "rest"))
    nothing_ready, nothing_stored = m.sem("i_nothing_ready"), m.sem("i_nothing_stored")
    idx_ready, all_stored = m.sem("i_idx_ready"), m.sem("i_all_stored")
    gathered = [m.sem(f"i_gathered{u}") for u in U2]
    stored = [m.sem(f"i_stored{u}") for u in U2]
    x_turned = [m.sem(f"i_x_turned{u}") for u in U2]
    x_kept = [m.sem(f"i_x_kept{u}") for u in U2]
    x_parts = m.sem("i_x_parts")
    silued, mixed, h_turned, h_head, h_kept, y_kept = (
        m.sem("i_" + n) for n in ("silued", "mixed", "h_turned", "h_head", "h_kept", "y_kept"))
    ybt = d["yb"].rearrange("(b p) n -> b p n", p=P)
    LOW = 2 * SEQ // P

    def blocks(eng, body):
        nb = eng.value_load(plan[0:1, PLAN_BLOCKS:PLAN_BLOCKS + 1], min_val=LOW, max_val=BLOCKS - 1)
        with eng.Fori(0, BLOCKS // 2) as i:
            for u in range(2):
                with eng.If(2 * i + u < nb):
                    body(2 * i + u, i, u)
        return nb

    def place_of(eng, b):
        return eng.value_load(plan[0:1, bass.ds(b + PLAN_RANK, 1)], min_val=0, max_val=NE - 1)

    def ahead(eng, b):
        place, after = place_of(eng, b), place_of(eng, b + 1)

        def run(split, *args):
            with eng.If(place < after):
                split(place + 1, b + 1, *args)
        return run

    def of_half(w, place, n, c):
        step = W[n].shape[2] // CH
        if isinstance(place, int):
            return w[n][:, place, c * step:(c + 1) * step, :].rearrange("p k n -> p (k n)")
        return w[n][:, bass.ds(place & 1, 1), c * step:(c + 1) * step, :].rearrange("p a k n -> p (a k n)")

    def of_head(n, c):
        step = W[n].shape[2] // CH
        return heads[n][:, c * step:(c + 1) * step, :].rearrange("p k n -> p (k n)")

    def take_rest(eng, op, place, n, steps):
        for c in steps:
            eng.wait_ge(head[n], place * CH + c + 1)
            op(of_half(rests, place, n, c), of_half(W, place, n, c), of_head(n, c), ALU.subtract).then_inc(rest[n], 1)

    with nc.Block() as block:
        @block.sync
        def _(sp):
            experts_ = sp.value_load(plan[0:1, PLAN_EXPERTS:PLAN_EXPERTS + 1], min_val=2, max_val=NE)
            nb = sp.value_load(plan[0:1, PLAN_BLOCKS:PLAN_BLOCKS + 1], min_val=LOW, max_val=BLOCKS)
            with sp.Fori(0, NE // 2 - 1) as i:
                for u in range(2):
                    with sp.If(2 * i + u + 2 < experts_):
                        load_expert(m, sp, 2 * i + u + 2, u, used)
            sp.wait_ge(nothing_ready, 1)
            with sp.Fori(0, BLOCKS - LOW) as j:
                with sp.If(nb < j + LOW + 1):
                    sp.dma_start(flat(one(ybt, j + LOW)), nothing[:, :]).then_inc(nothing_stored, 16)
                with sp.If(j + LOW < nb):
                    sp.sem_inc(nothing_stored, 16)
            sp.wait_ge(nothing_stored, 16 * (BLOCKS - LOW))
            sp.sem_inc(all_stored, 1)

        @block.gpsimd
        def _(pool):
            nc.gpsimd.memset(nothing[:, :], 0.0).then_inc(nothing_ready, 1)

            def gather(b, i, u):
                pool.wait_ge(x_turned[u], i)
                nc.gpsimd.tensor_copy(idx[u][:, :], tok[:, bass.ds(b, 1)]).then_inc(idx_ready, 1)
                pool.wait_ge(idx_ready, 2 * b + 1)
                pool.sem_inc(idx_ready, 1)
                pool.indirect_dma_start(out=xg[u][:, :], out_offset=None, in_=d["xn2"],
                                        in_offset=bass.IndirectOffsetOnAxis(ap=idx[u][:, :], axis=0)).then_inc(gathered[u], 16)

            def split(place, b):
                take_rest(pool, nc.gpsimd.tensor_tensor, place, "down", range(CH))

            def body(b, i, u):
                gather(b + 2, i + 1, u)
                ahead(pool, b)(split)

            gather(0, 0, 0)
            gather(1, 0, 1)
            take_rest(pool, nc.gpsimd.tensor_tensor, 0, "down", range(CH))
            blocks(pool, body)

        @block.tensor
        def _(pe):
            def turn(i, u):
                pe.wait_ge(gathered[u], 16 * i + 16)
                pe.wait_ge(x_kept[u], i)
                for k in range(KD):
                    last = nc.tensor.transpose(m.bank(k // 4)[:, k % 4 * P:(k % 4 + 1) * P], xg[u][:, k * P:(k + 1) * P], ident)
                last.then_inc(x_turned[u], 1)

            def product(out, xs, ws, first, final):
                passes = ((xs[0], ws[0]), (xs[1], ws[0]), (xs[0], ws[1]))
                for n, (x, w) in enumerate(passes):
                    last = nc.tensor.matmul(out, x, w, start=(first and n == 0), stop=(final and n == 2))
                return last

            def hidden(bank, n, u, place, half, g):
                here = slice(g * HALF, (g + 1) * HALF)
                for k in range(KD):
                    last = product(m.bank(bank, HALF), (xh[u][:, k, :], xr[u][:, k, :]),
                                   (heads[n][:, k, here], cols(rests[n][:, bass.ds(half, 1), k, here])), k == 0, k == KD - 1)
                last.then_inc(used[n] if g else first_half[n], 1)

            def turn_h(b, g):
                pe.wait_ge(mixed, 2 * b + g + 1)
                pe.wait_ge(h_kept, 2 * b + g)
                for k in (2 * g, 2 * g + 1):
                    last = nc.tensor.transpose(m.bank(4, P, k * P), hh[:, k * P:(k + 1) * P], ident)
                last.then_inc(h_turned, 1)

            def down(b, place, half, g):
                pe.wait_ge(h_kept, 2 * b + g + 1)
                pe.wait_ge(rest["down"], place * CH + 2 * g + 2)
                for k in (2 * g, 2 * g + 1):
                    for c in range(2):
                        here = slice(c * NC, (c + 1) * NC)
                        last = product(m.bank(5 + c), (hTh[:, k, :], hTr[:, k, :]),
                                       (heads["down"][:, k, here], cols(rests["down"][:, bass.ds(half, 1), k, here])), k == 0, k == KE - 1)
                return last

            def body(b, i, u):
                place = place_of(pe, b)
                half = place & 1
                pe.wait_ge(x_kept[u], i + 1)
                pe.wait_ge(silued, 2 * b)
                pe.wait_ge(rest["gate"], place * CH + CH)
                hidden(2, "gate", u, place, half, 0)
                turn(i + u, 1 - u)
                pe.wait_ge(mixed, 2 * b)
                pe.wait_ge(rest["up"], place * CH + CH)
                hidden(3, "up", u, place, half, 0)
                hidden(7, "gate", u, place, half, 1)
                turn_h(b, 0)
                pe.wait_ge(mixed, 2 * b + 1)
                hidden(3, "up", u, place, half, 1)
                pe.wait_ge(y_kept, b)
                down(b, place, half, 0)
                turn_h(b, 1)
                down(b, place, half, 1).then_inc(used["down"], 1)

            turn(0, 0)
            blocks(pe, body)

        @block.scalar
        def _(act):
            def wait_loaded(n, place):
                act.wait_ge(loads[n][0], ((place >> 1) + 1) * 16)
                act.wait_ge(loads[n][1], (((place + 1) >> 1) + 1) * 16)

            def take_head(place, b, n):
                wait_loaded(n, place)
                act.wait_ge(used[n], b)
                for c in range(CH):
                    nc.scalar.activation(of_head(n, c), of_half(W, place, n, c), ACT.Copy).then_inc(head[n], 1)

            def keep_h(b, g):
                act.wait_ge(h_turned, 2 * b + g + 1)
                act.wait_ge(used["down"], b)
                nc.scalar.activation(hTh[:, 2 * g:2 * g + 2, :].rearrange("p k n -> p (k n)"), m.bank(4, HALF, g * HALF), ACT.Copy
                                     ).then_inc(h_head, 1)

            def body(b, i, u):
                if_next = ahead(act, b)
                for g in range(2):
                    act.wait_ge((first_half["gate"], used["gate"])[g], b + 1)
                    act.wait_ge(mixed, 2 * b)
                    nc.scalar.activation(hs[:, g * HALF:(g + 1) * HALF], m.bank((2, 7)[g], HALF), ACT.Silu).then_inc(silued, 1)
                keep_h(b, 0)
                if_next(take_head, "gate")
                keep_h(b, 1)
                if_next(take_head, "up")
                act.wait_ge(used["down"], b + 1)
                act.wait_ge(stored[u], 16 * i)
                nc.scalar.activation(yo[u][:, :], m.psum[:, 5 * NC:5 * NC + D], ACT.Copy).then_inc(y_kept, 1)
                act.wait_ge(y_kept, b + 1)
                act.dma_start(flat(one(ybt, b)), yo[u][:, :]).then_inc(stored[u], 16)
                if_next(take_head, "down")

            for n in W:
                act.sem_inc(loads[n][1], 16)
            for n in W:
                act.wait_ge(loads[n][0], 16)
                for c in range(CH):
                    nc.scalar.activation(of_head(n, c), of_half(W, 0, n, c), ACT.Copy).then_inc(head[n], 1)
            nb = blocks(act, body)
            act.wait_ge(stored[0], ((nb + 1) >> 1) * 16)
            act.wait_ge(stored[1], (nb >> 1) * 16)
            act.sem_inc(all_stored, 1)

        @block.vector
        def _(dve):
            tt = nc.vector.tensor_tensor

            def shape(b, i, u):
                dve.wait_ge(x_turned[u], i + 1)
                for k in range(KD):
                    last = nc.vector.tensor_scalar(xm[:, k, :], m.bank(k // 4)[:, k % 4 * P:(k % 4 + 1) * P],
                                                   modT[:, 4 * KD + k, 0:1], modT[:, 3 * KD + k, 0:1], ALU.mult, ALU.add)
                last.then_inc(x_parts, 1)
                dve.wait_ge(x_parts, 2 * b + 1)
                nc.vector.tensor_copy(xh[u][:, :, :], xm[:, :, :]).then_inc(x_parts, 1)
                dve.wait_ge(x_parts, 2 * b + 2)
                tt(xr[u][:, :, :], xm[:, :, :], xh[u][:, :, :], ALU.subtract).then_inc(x_kept[u], 1)

            def mix(b, g):
                here = slice(g * HALF, (g + 1) * HALF)
                dve.wait_ge(silued, 2 * b + g + 1)
                dve.wait_ge((first_half["up"], used["up"])[g], b + 1)
                dve.wait_ge(h_turned, 2 * b + g)
                tt(hh[:, here], hs[:, here], m.bank(3, HALF), ALU.mult).then_inc(mixed, 1)

            def keep_h(b, g):
                ks = slice(2 * g, 2 * g + 2)
                dve.wait_ge(h_head, 2 * b + g + 1)
                tt(hTr[:, ks, :].rearrange("p k n -> p (k n)"), m.bank(4, HALF, g * HALF), hTh[:, ks, :].rearrange("p k n -> p (k n)"),
                   ALU.subtract).then_inc(h_kept, 1)

            def split(place, b, n, steps):
                take_rest(dve, tt, place, n, steps)

            def body(b, i, u):
                if_next = ahead(dve, b)
                shape(b + 1, i + u, 1 - u)
                mix(b, 0)
                keep_h(b, 0)
                if_next(split, "gate", range(CH // 2))
                mix(b, 1)
                keep_h(b, 1)
                if_next(split, "gate", range(CH // 2, CH))
                if_next(split, "up", range(CH))

            shape(0, 0, 0)
            for n in ("gate", "up"):
                take_rest(dve, tt, 0, n, range(CH))
            blocks(dve, body)
    m.top = top


def combine(m):
    nc, d, gate, row = m.nc, m.dram, m.keep["gate"], m.keep["row"]
    rep_g, rep_ln = m.sb("j_rep_g", [P, D]), m.sb("j_rep_ln", [P, 2, D])
    rows_loaded = m.sem("j_rows_loaded")
    RING = 4
    x1, y1, y2 = ([m.sb(f"j_{n}{u}", [P, D]) for u in range(RING)] for n in ("x1", "y1", "y2"))
    acc = [m.sb(f"j_acc{u}", [P, D]) for u in range(RING)]
    idx = [[m.sb(f"j_idx{j}{u}", [P, 1], I32) for u in range(RING)] for j in range(2)]
    st = m.sb("j_st", [P, 2, 6])
    mv = [m.sb(f"j_mv{u}", [P, 2]) for u in range(2)]
    sd = [m.sb(f"j_sd{u}", [P, 1]) for u in range(2)]
    loaded = [m.sem(f"j_loaded{u}") for u in range(RING)]
    gathered = [m.sem(f"j_gathered{u}") for u in range(RING)]
    stored = [m.sem(f"j_stored{u}") for u in range(RING)]
    summed = m.sem("j_summed")
    idx_ready, scaled, stats, std, shaped, ready, own = (
        m.sem("j_" + n) for n in ("idx_ready", "scaled", "stats", "std", "shaped", "ready", "dve_link"))
    out = d["out"].rearrange("(t p) n -> t p n", p=P)

    with nc.Block() as block:
        @block.sync
        def _(sp):
            def load(t):
                sp.dma_start(x1[t % RING][:, :], flat(one(d["x1"], t))).then_inc(loaded[t % RING], 16)

            sp.dma_start(rep_g[:, :], d["mod_rows"][0:1, 5 * D:6 * D].to_broadcast([P, D])).then_inc(rows_loaded, 16)
            sp.dma_start(rep_ln[:, :, :], d["rep_ln"].rearrange("p (w n) -> p w n", w=4)[:, 2:4, :]).then_inc(rows_loaded, 16)
            for t in range(RING):
                load(t)
            for t in range(TL):
                sp.wait_ge(ready, t + 1)
                sp.dma_start(flat(one(out, t)), acc[t % RING][:, :]).then_inc(stored[t % RING], 16)
                if t + RING < TL:
                    load(t + RING)
            for v in range(RING):
                sp.wait_ge(stored[v], 16 * (TL // RING))

        @block.gpsimd
        def _(pool):
            def gather(t):
                v = t % RING
                if t >= RING:
                    pool.wait_ge(summed, t - RING + 1)
                for j in range(2):
                    nc.gpsimd.tensor_copy(idx[j][v][:, :], row[:, j, t:t + 1]).then_inc(idx_ready, 1)
                pool.wait_ge(idx_ready, 2 * t + 2)
                for j, y in enumerate((y1, y2)):
                    pool.indirect_dma_start(out=y[v][:, :], out_offset=None, in_=d["yb"],
                                            in_offset=bass.IndirectOffsetOnAxis(ap=idx[j][v][:, :], axis=0)).then_inc(gathered[v], 16)

            pool.wait_ge(rows_loaded, 32)
            for t in range(RING):
                gather(t)
            for t in range(TL):
                if t + RING < TL:
                    gather(t + RING)
                pool.wait_ge(shaped, t + 1)
                nc.gpsimd.tensor_tensor(acc[t % RING][:, :], acc[t % RING][:, :], rep_ln[:, 1, :], ALU.add).then_inc(ready, 1)

        @block.vector
        def _(dve):
            link = Link(dve, own)
            tt, stt = nc.vector.tensor_tensor, nc.vector.scalar_tensor_tensor

            def add(t):
                y, v = acc[t % RING][:, :], t % RING
                dve.wait_ge(scaled, t + 1)
                stt(y, y2[v][:, :], gate[:, 1, t:t + 1], y, ALU.mult, ALU.add).then_inc(summed, 1)
                dve.wait_ge(summed, t + 1)
                link(tt(y, y, rep_g[:, :], ALU.mult))
                dve.wait_ge(loaded[v], 16 * (t // RING) + 16)
                link(stt(y, x1[v][:, :], ALPHA, y, ALU.mult, ALU.add))
                layer_norm_stats(nc, dve, link, st, mv[t % 2], acc[t % RING])
                dve.sem_inc(stats, 1)

            def norm(t):
                u, y = t % 2, acc[t % RING][:, :]
                dve.wait_ge(std, t + 1)
                link(nc.vector.reciprocal(sd[u][:, :], sd[u][:, :]))
                link(nc.vector.tensor_scalar(y, y, mv[u][:, 0:1], sd[u][:, :], ALU.subtract, ALU.mult))
                tt(y, y, rep_ln[:, 0, :], ALU.mult).then_inc(shaped, 1)

            dve.wait_ge(rows_loaded, 32)
            add(0)
            for t in range(TL):
                if t + 1 < TL:
                    add(t + 1)
                norm(t)

        @block.scalar
        def _(act):
            def scale(t):
                act.wait_ge(gathered[t % RING], 32 * (t // RING) + 32)
                if t >= RING:
                    act.wait_ge(stored[t % RING], 16 * (t // RING))
                nc.scalar.activation(acc[t % RING][:, :], y1[t % RING][:, :], ACT.Copy, scale=gate[:, 0, t:t + 1]).then_inc(scaled, 1)

            scale(0)
            scale(1)
            for t in range(TL):
                act.wait_ge(stats, t + 1)
                nc.scalar.activation(sd[t % 2][:, :], mv[t % 2][:, 1:2], ACT.Sqrt, bias=m.keep["eps_ln"]).then_inc(std, 1)
                if t + 2 < TL:
                    scale(t + 2)


def program(nc, dram):
    m = Machine(nc, dram)
    for phase in PHASES:
        m.phase_sems = []
        phase(m)
        nc.clear_and_free_semaphores(m.phase_sems)
        nc.all_engine_barrier()


PHASES = [modulation, normed_transposed, delta_inputs, token_inputs,
          delta_gates, delta_rule, attention, mixed_output, residual_and_logits,
          routing, experts, combine]


def constants():
    i = np.arange(P)
    row, col = i[:, None], i[None, :]
    parts = [row == col, np.ones((P, P)), row <= col, row >= col, row < col,
             -BIG * (row > col), -BIG * (row < col)]
    for r in range(2):
        for lv in range(LEVELS):
            b = 1 << lv
            a, z = (row, col) if r == 0 else (col, row)
            parts.append((a // (2 * b) == z // (2 * b)) & (a // b % 2 == 0) & (z // b % 2 == 1))
    masks = np.concatenate([np.asarray(x, np.float32) for x in parts], axis=1)
    half = DK // 2
    freq = np.float32(10000.0) ** (-np.arange(0, half, 2, dtype=np.float32) / np.float32(half))
    t = np.arange(SEQ)
    ang = [(p.astype(np.float32)[:, None] * freq[None, :]).astype(np.float32) for p in (t // 64, t % 64)]
    rope = np.concatenate([f(a) for f in (np.cos, np.sin) for a in ang for _ in range(2)], axis=1).astype(np.float32)
    small = np.zeros((P, 96), np.float32)
    small[:, 0:4] = [4, 3, 2, 1]
    small[:, 4:12] = [8, 7, 6, 5, 4, 3, 2, 1]
    small[:, 12:20] = np.arange(8) * P
    small[:, 20:68] = np.arange(48)
    small[:, 68] = LN_EPS
    small[:, 69] = NORM_EPS
    ids = (np.arange(P)[:, None] + P * np.arange(TL)[None, :]).astype(np.int32)
    quad = np.zeros((P, P + 32), np.float32)
    quad[:, :P] = row // 32 == col // 32
    quad[:, P:] = row % 32 == np.arange(32)[None, :]
    return {"quad": quad, "masks": masks, "rope": rope, "small": small, "ids": ids}


def kernel(x, c, ctx, c_ctx, w_ada, b_ada, w_in, conv_w, gdn_a_log, gdn_dt_bias, gdn_norm_w,
           diff_lambda, diff_norm_w, w_out, ln1_g, ln1_b, w_router_group, b_router_group,
           w_router_expert, b_router_expert, w_expert_gate, w_expert_up, w_expert_down, ln2_g, ln2_b):
    import concourse.bacc as bacc
    from concourse.bass_utils import run_bass_kernel_spmd as run

    def rep(a):
        return np.ascontiguousarray(np.broadcast_to(np.asarray(a).reshape(1, -1), (P, np.asarray(a).size)))

    cc = np.stack([np.asarray(c).reshape(KD, P), np.asarray(c_ctx).reshape(KD, P)], axis=-1)
    arrays = {
        "tokens": np.concatenate([np.asarray(x)[0], np.asarray(ctx)[0]], axis=0),
        "c_cols": np.ascontiguousarray(cc.transpose(1, 0, 2)).reshape(P, 2 * KD),
        "w_ada": w_ada[0], "b_ada": np.concatenate([b_ada, b_ada], axis=0), "w_in": w_in[0],
        "conv_cols": np.ascontiguousarray(np.asarray(conv_w)[0].reshape(CONV, 3 * H, P).transpose(2, 1, 0)).reshape(P, -1),
        "rep_gates": np.concatenate([rep(gdn_dt_bias), rep(gdn_a_log)], axis=1),
        "rep_norm": np.concatenate([rep(gdn_norm_w), rep(diff_norm_w)], axis=1),
        "rep_lambda": rep(diff_lambda), "w_out": w_out[0],
        "rep_ln": np.concatenate([rep(ln1_g), rep(ln1_b), rep(ln2_g), rep(ln2_b)], axis=1),
        "w_route": np.concatenate([w_router_group[0], w_router_expert[0]], axis=1),
        "rep_route": np.concatenate([rep(b_router_group), rep(b_router_expert)], axis=1),
        "w_gate": w_expert_gate[0], "w_up": w_expert_up[0], "w_down": w_expert_down[0],
    }
    arrays.update(constants())
    nc = bacc.Bacc("TRN2", target_bir_lowering=False, num_devices=1)
    dram = {}
    for name, a in arrays.items():
        a = arrays[name] = np.ascontiguousarray(a)
        dram[name] = nc.dram_tensor("in_" + name, a.shape, mybir.dt.from_np(a.dtype), kind="ExternalInput").ap()
    dram["out"] = nc.dram_tensor("out", (SEQ, D), F32, kind="ExternalOutput").ap()
    program(nc, dram)
    r = run(nc, [{"in_" + k: a for k, a in arrays.items()}], core_ids=[0])
    return r.results[0]["out"].reshape(1, SEQ, D)
```

```python
import math
from contextlib import contextmanager

import numpy as np
import concourse.bass as bass
from concourse import mybir

F32 = mybir.dt.float32
I32 = mybir.dt.int32
F32R = mybir.dt.float32r
ALU = mybir.AluOpType
ACT = mybir.ActivationFunctionType
AX = mybir.AxisListType.X

P = 128
D = 1024
KD = D // P
SEQ, CTX = 1024, 256
TL, TC = SEQ // P, CTX // P
TT = TL + TC
TOK = SEQ + CTX
H = 4
HD = H * P
DK = 64
NC = 512
CONV = 5
NMOD = 6 * D
NG, NE, EG = 4, 32, 8
DE = 512
BLOCKS = 2 * SEQ // P + NE
PLAN_EXPERT, PLAN_END, PLAN_RANK, PLAN_BLOCKS, PLAN_EXPERTS = 0, NE, 2 * NE, 2 * NE + BLOCKS, 2 * NE + BLOCKS + 1
PLAN = PLAN_EXPERTS + 1
ALPHA = 2.0 ** 0.25
LN_EPS, NORM_EPS = 1e-5, 1e-6
LAM_INIT = 0.8 - 0.6 * math.exp(0.0)
GDN_GATES_AT = 4 * HD
DIFF_AT = GDN_GATES_AT + 16
IN_COLS = DIFF_AT + 3 * HD
TAIL = IN_COLS - 3 * HD
BIG = 1.0e30
LEVELS = 7


class Link:

    def __init__(self, eng, sem):
        self.eng, self.sem, self.base, self.n = eng, sem, 0, 0

    def __call__(self, ins, plain=False):
        ins.then_inc(self.sem, 1)
        self.n += 1
        self.eng.wait_ge(self.sem, self.base + self.n)
        if plain:
            self.eng.sem_inc(self.sem, 1)
            self.n += 1

    @contextmanager
    def loop(self, count, per):
        start = self.base + self.n
        with self.eng.Fori(0, count) as i:
            self.base, self.n = start + i * per, 0
            yield i
            assert self.n == per, f"the body links {self.n}"
        self.base, self.n = start + count * per, 0


class Machine:

    def __init__(self, nc, dram):
        self.nc, self.dram = nc, dram
        self.top, self.limit = 16512, 229312
        self.high = 229312 - 4 * (H * TOK + TT * HD + TT * 16)
        self.psum = nc.alloc_psum_tensor("psum", [P, 8 * NC], F32)
        self.keep = {}

    def sb(self, name, shape, dt=F32):
        size = 4 * int(np.prod(shape[1:]))
        t = self.nc.alloc_sbuf_tensor_at(name, shape, dt, offset=self.top)
        self.top += -(-size // 32) * 32
        assert self.top <= self.limit, f"{name} ends at {self.top}"
        return t

    def bank(self, b, n=NC, at=0):
        return self.psum[:, b * NC + at:b * NC + at + n]

    def sem(self, name, lasting=False):
        s = self.nc.alloc_semaphore(name)
        if not lasting:
            self.phase_sems.append(s)
        return s

    def scratch(self, name, shape, dt=F32):
        self.dram[name] = self.nc.dram_tensor(name, shape, dt, kind="Internal").ap()
        return self.dram[name]


def one(ap, i):
    return ap[bass.ds(i, 1)]


def cols(ap):
    return ap.rearrange("p a n -> p (a n)")


def flat(ap):
    return ap.rearrange("a b n -> (a b) n")


def modulation(m):
    nc, d = m.nc, m.dram
    mask = m.sb("mask", [P, 7 + 2 * LEVELS, P])
    modT = m.sb("modT", [P, 6 * KD, 2])
    small = m.sb("small", [P, 96])
    m.keep.update(mask=mask, modT=modT, ident=mask[:, 0, :], ones=mask[:, 1, :], tri=[mask[:, 2, :], mask[:, 3, :]],
                  before=mask[:, 4, :], neg=[mask[:, 5, :], mask[:, 6, :]],
                  level=[[mask[:, 7 + LEVELS * r + lv, :] for lv in range(LEVELS)] for r in range(2)])
    m.keep.update(small=small, eps_ln=small[:, 68:69], eps_norm=small[:, 69:70])
    ident = m.keep["ident"]
    top = m.top
    m.scratch("mod_rows", [2, NMOD])
    craw = m.sb("craw", [P, KD, 2])
    csil = m.sb("csil", [P, KD, 2])
    brow = m.sb("brow", [2, NMOD])
    mod = m.sb("mod", [2, NMOD])
    wa = [m.sb(f"wa{u}", [P, KD, NC]) for u in range(2)]
    small_loaded, c_ready, cols_ready = m.sem("ada_small"), m.sem("ada_c"), m.sem("ada_cols")
    cols_kept, rows_stored = m.sem("ada_cols_kept"), m.sem("ada_rows_stored")
    loaded = [m.sem(f"ada_loaded{u}") for u in range(2)]
    product = [m.sem(f"ada_product{u}") for u in range(2)]
    kept = [m.sem(f"ada_kept{u}") for u in range(2)]
    w = d["w_ada"].rearrange("(k p) (j n) -> j p k n", p=P, n=NC)
    steps = NMOD // NC // 2

    with nc.Block() as block:
        @block.sync
        def _(sp):
            sp.dma_start(craw[:, :, :], d["c_cols"].rearrange("p (k r) -> p k r", r=2)).then_inc(small_loaded, 16)
            sp.dma_start(brow[:, :], d["b_ada"]).then_inc(small_loaded, 16)
            sp.dma_start(mask[:, :, :], d["masks"].rearrange("p (s n) -> p s n", n=P)).then_inc(small_loaded, 16)
            sp.dma_start(small[:, :], d["small"]).then_inc(small_loaded, 16)
            with sp.Fori(0, steps) as i:
                for u in range(2):
                    sp.wait_ge(product[u], i)
                    sp.dma_start(wa[u][:, :, :], one(w, 2 * i + u).rearrange("j p k n -> (j p) k n")).then_inc(loaded[u], 16)
            sp.wait_ge(kept[0], steps)
            sp.wait_ge(kept[1], steps)
            sp.dma_start(d["mod_rows"], mod[:, :]).then_inc(rows_stored, 16)
            sp.wait_ge(rows_stored, 16)

        @block.scalar
        def _(act):
            act.wait_ge(small_loaded, 64)
            nc.scalar.activation(csil[:, :, :], craw[:, :, :], ACT.Silu).then_inc(c_ready, 1)

        @block.tensor
        def _(pe):
            pe.wait_ge(small_loaded, 64)
            pe.wait_ge(c_ready, 1)
            with pe.Fori(0, steps) as i:
                for u in range(2):
                    pe.wait_ge(loaded[u], 16 * i + 16)
                    pe.wait_ge(kept[u], i)
                    for k in range(KD):
                        last = nc.tensor.matmul(m.bank(u)[0:2, :], csil[:, k, :], wa[u][:, k, :],
                                                start=(k == 0), stop=(k == KD - 1))
                    last.then_inc(product[u], 1)
            pe.wait_ge(kept[0], steps)
            pe.wait_ge(kept[1], steps)
            for j in range(6 * KD):
                last = nc.tensor.matmul(m.bank(2)[:, 2 * j:2 * j + 2], mod[:, j * P:(j + 1) * P], ident[0:2, 0:2],
                                        start=True, stop=True)
            last.then_inc(cols_ready, 1)

        @block.vector
        def _(dve):
            dve.wait_ge(small_loaded, 64)
            with dve.Fori(0, steps) as i:
                for u in range(2):
                    dve.wait_ge(product[u], i + 1)
                    here = bass.ds((2 * i + u) * NC, NC)
                    nc.vector.tensor_tensor(mod[:, here], m.bank(u)[0:2, :], brow[:, here], ALU.add).then_inc(kept[u], 1)
            dve.wait_ge(cols_ready, 1)
            nc.vector.tensor_copy(modT[:, :, :], m.bank(2, 12 * KD).rearrange("p (j r) -> p j r", r=2)).then_inc(cols_kept, 1)
            dve.wait_ge(cols_kept, 1)
            for part in (1, 4):
                nc.vector.tensor_scalar(modT[:, part * KD:(part + 1) * KD, :], modT[:, part * KD:(part + 1) * KD, :],
                                        1.0, None, ALU.add).then_inc(cols_kept, 1)
    m.top = top


def normed_transposed(m):
    nc, d, ident, modT = m.nc, m.dram, m.keep["ident"], m.keep["modT"]
    m.base = m.top
    hT = m.keep["hT"] = m.sb("hT", [P, KD, TOK])
    top = m.top
    RING = 4
    xt = [m.sb(f"xt{u}", [P, D]) for u in range(RING)]
    xn = [m.sb(f"xn{u}", [P, D]) for u in range(2)]
    st = m.sb("ln_st", [P, 2, 6])
    mv = [m.sb(f"ln_mv{u}", [P, 2]) for u in range(2)]
    sd = [m.sb(f"ln_sd{u}", [P, 1]) for u in range(2)]
    loaded = [m.sem(f"x_loaded{u}") for u in range(RING)]
    stats, std = m.sem("x_stats"), m.sem("x_std")
    normed = [m.sem(f"x_normed{u}") for u in range(2)]
    turned = [m.sem(f"x_turned{u}") for u in range(2)]
    kept = [m.sem(f"x_kept{u}") for u in range(2)]
    own = m.sem("x_dve_link")
    x = d["tokens"].rearrange("(t p) n -> t p n", p=P)

    with nc.Block() as block:
        @block.sync
        def _(sp):
            for t in range(TT):
                if t >= RING:
                    sp.wait_ge(normed[t % 2], (t - RING) // 2 + 1)
                sp.dma_start(xt[t % RING][:, :], flat(one(x, t))).then_inc(loaded[t % RING], 16)

        @block.vector
        def _(dve):
            link = Link(dve, own)

            def measure(t):
                dve.wait_ge(loaded[t % RING], 16 * (t // RING) + 16)
                for c in range(2):
                    last = nc.vector.bn_stats(st[:, c, :], xt[t % RING][:, c * NC:(c + 1) * NC])
                link(last)
                link(nc.vector.bn_aggr(mv[t % 2][:, :], st[:, :, :].rearrange("p a b -> p (a b)")))
                dve.sem_inc(stats, 1)

            def norm(t):
                u = t % 2
                dve.wait_ge(std, t + 1)
                link(nc.vector.reciprocal(sd[u][:, :], sd[u][:, :]))
                dve.wait_ge(turned[u], t // 2)
                nc.vector.tensor_scalar(xn[u][:, :], xt[t % RING][:, :], mv[u][:, 0:1], sd[u][:, :],
                                        ALU.subtract, ALU.mult).then_inc(normed[u], 1)

            measure(0)
            for t in range(TT):
                if t + 1 < TT:
                    measure(t + 1)
                norm(t)

        @block.tensor
        def _(pe):
            with pe.Fori(0, TT // 2) as i:
                for u in range(2):
                    pe.wait_ge(normed[u], i + 1)
                    pe.wait_ge(kept[u], i)
                    for k in range(KD):
                        last = nc.tensor.transpose(m.bank(2 * u + k // 4)[:, k % 4 * P:(k % 4 + 1) * P],
                                                   xn[u][:, k * P:(k + 1) * P], ident)
                    last.then_inc(turned[u], 1)

        @block.scalar
        def _(act):
            def deviation(t, i, u):
                act.wait_ge(stats, t + 1)
                act.wait_ge(normed[u], i)
                nc.scalar.activation(sd[u][:, :], mv[u][:, 1:2], ACT.Sqrt, bias=m.keep["eps_ln"]).then_inc(std, 1)

            def leave(t, i, u, r):
                act.wait_ge(turned[u], i + 1)
                for k in range(KD):
                    last = nc.scalar.activation(hT[:, k, bass.ds(t * P, P)],
                                                m.bank(2 * u + k // 4)[:, k % 4 * P:(k % 4 + 1) * P], ACT.Identity,
                                                scale=modT[:, KD + k, r:r + 1], bias=modT[:, k, r:r + 1])
                last.then_inc(kept[u], 1)

            deviation(0, 0, 0)
            deviation(1, 0, 1)
            with act.Fori(0, TL // 2) as i:
                for u in range(2):
                    deviation(2 * i + u + 2, i + 1, u)
                    leave(2 * i + u, i, u, 0)
            for u in range(2):
                leave(TL + u, TL // 2, u, 1)
    m.top = top


def delta_inputs(m):
    nc, d, ident, hT = m.nc, m.dram, m.keep["ident"], m.keep["hT"]
    gap = CONV // 2
    wide = TOK + gap
    wt = m.keep["wt"] = m.sb("wt", [P, KD, TAIL])
    m.keep["wt_loaded"] = m.sem("wt_loaded", lasting=True)
    top = m.top
    m.scratch("qT", [H, P, SEQ])
    m.scratch("kT", [H, P, TOK])
    m.scratch("k", [TT, P, HD])
    m.scratch("v", [TT, P, HD])
    cw = m.sb("cw", [P, 3 * H * CONV])
    wm = [m.sb(f"wm{u}", [P, KD, P]) for u in range(2)]
    padded = [m.sb(f"padded{u}", [P, TOK + 3 * gap]) for u in range(2)]
    conv = [m.sb(f"conv{u}", [P, wide]) for u in range(2)]
    act_out = [m.sb(f"silu{u}", [P, wide]) for u in range(2)]
    raw = [m.sb(f"raw{u}", [P, TT, P]) for u in range(2)]
    nrm = [m.sb(f"nrm{u}", [P, TT, P]) for u in range(2)]
    back = [m.sb(f"back{u}", [P, TOK]) for u in range(2)]
    ssq = m.sb("ssq", [P, TT])
    sd = m.sb("ssd", [P, TT])
    cw_loaded, zeroed = m.sem("cw_loaded"), m.sem("pads_zeroed")
    wm_loaded = [m.sem(f"wm_loaded{u}") for u in range(2)]
    tok_stored = [m.sem(f"heads_tok_stored{u}") for u in range(2)]
    ch_stored = [m.sem(f"heads_ch_stored{u}") for u in range(2)]
    proj, evac, conved, silued = m.sem("c_proj"), m.sem("c_evac"), m.sem("c_conved"), m.sem("c_silued")
    turned, kept, summed, rooted = m.sem("c_turned"), m.sem("c_kept"), m.sem("c_summed"), m.sem("c_rooted")
    normed, returned, rekept = m.sem("c_normed"), m.sem("c_returned"), m.sem("c_rekept")
    own = m.sem("c_dve_link")
    PARTS = 3 * H
    QK = 2 * H

    def tiles(c):
        return TL if c < H else TT

    def groups(c):
        return 2 * c if c < H else 3 * c - H

    def tok_count(c, u):
        return 16 * sum(b >= H for b in range(c) if b % 2 == u)

    with nc.Block() as block:
        @block.sync
        def _(sp):
            sp.dma_start(cw[:, :], d["conv_cols"]).then_inc(cw_loaded, 16)
            for c in range(PARTS):
                if c >= 2:
                    sp.wait_ge(proj, c - 1)
                sp.dma_start(wm[c % 2][:, :, :], d["w_in"][:, c * P:(c + 1) * P].rearrange("(k p) n -> p k n", p=P)
                             ).then_inc(wm_loaded[c % 2], 16)
                if c == 1:
                    sp.dma_start(wt[:, :, :], d["w_in"][:, 3 * HD:].rearrange("(k p) n -> p k n", p=P)
                                 ).then_inc(m.keep["wt_loaded"], 16)

        @block.gpsimd
        def _(pool):
            for u in range(2):
                for at in (0, gap + SEQ, 2 * gap + TOK):
                    last = nc.gpsimd.memset(padded[u][:, at:at + gap], 0.0)
            last.then_inc(zeroed, 1)
            for c in range(PARTS):
                u, h = c % 2, c % H
                if c >= H:
                    pool.wait_ge(normed if c < QK else kept, c + 1)
                    src = nrm[u] if c < QK else raw[u]
                    dst = d["k" if c < QK else "v"][:, :, h * P:(h + 1) * P].rearrange("t p n -> p t n")
                    pool.dma_start(dst, src[:, :, :]).then_inc(tok_stored[u], 16)
                if c < QK:
                    pool.wait_ge(rekept, groups(c + 1))
                    pool.dma_start(d["qT" if c < H else "kT"][h], back[u][:, 0:tiles(c) * P]).then_inc(ch_stored[u], 16)
            for u in range(2):
                pool.wait_ge(tok_stored[u], tok_count(PARTS, u))
                pool.wait_ge(ch_stored[u], 16 * (QK // 2))

        @block.tensor
        def _(pe):
            def project(c):
                pe.wait_ge(wm_loaded[c % 2], 16 * (c // 2 + 1))
                pe.wait_ge(evac, c)
                for b, n in ((0, NC), (1, NC), (2, CTX))[:2 if c < H else 3]:
                    for k in range(KD):
                        last = nc.tensor.matmul(m.bank(b, n), wm[c % 2][:, k, :], hT[:, k, b * NC:b * NC + n],
                                                start=(k == 0), stop=(k == KD - 1))
                last.then_inc(proj, 1)

            def turn(c):
                pe.wait_ge(silued, c + 1)
                pe.wait_ge(kept, c)
                for t in range(tiles(c)):
                    at = t * P + (gap if t >= TL else 0)
                    last = nc.tensor.transpose(m.psum[:, 3 * NC + t * P:3 * NC + (t + 1) * P],
                                               act_out[c % 2][:, at:at + P], ident)
                last.then_inc(turned, 1)

            def turn_back(c):
                pe.wait_ge(normed, c + 1)
                for g, t0 in enumerate(range(0, tiles(c), 4)):
                    n = groups(c) + g
                    if n >= 2:
                        pe.wait_ge(rekept, n - 1)
                    for t in range(t0, min(t0 + 4, tiles(c))):
                        last = nc.tensor.transpose(m.bank(6 + n % 2, P, (t - t0) * P), nrm[c % 2][:, t, :], ident)
                    last.then_inc(returned, 1)

            for c in range(PARTS + 1):
                if c < PARTS:
                    project(c)
                if 2 <= c < QK + 2:
                    turn_back(c - 2)
                if c:
                    turn(c - 1)

        @block.scalar
        def _(act):
            for c in range(PARTS + 1):
                if c:
                    b, u = c - 1, (c - 1) % 2
                    act.wait_ge(conved, b + 1)
                    if b >= 2:
                        act.wait_ge(turned, b - 1)
                    nc.scalar.activation(act_out[u][:, :], conv[u][:, :], ACT.Silu).then_inc(silued, 1)
                if c < PARTS:
                    u = c % 2
                    act.wait_ge(proj, c + 1)
                    if c >= 2:
                        act.wait_ge(conved, c - 1)
                    if c >= H or c < 2:
                        src = m.psum[:, SEQ:TOK] if c >= H else hT[:, 0, SEQ:TOK]
                        nc.scalar.activation(padded[u][:, 2 * gap + SEQ:2 * gap + TOK], src, ACT.Copy)
                    nc.scalar.activation(padded[u][:, gap:gap + SEQ], m.psum[:, 0:SEQ], ACT.Copy).then_inc(evac, 1)
                if 2 <= c < QK + 2:
                    b, u = c - 2, (c - 2) % 2
                    if b >= 2:
                        act.wait_ge(ch_stored[u], 16 * (b // 2))
                    for g, t0 in enumerate(range(0, tiles(b), 4)):
                        n = groups(b) + g
                        act.wait_ge(returned, n + 1)
                        w = (min(t0 + 4, tiles(b)) - t0) * P
                        nc.scalar.activation(back[u][:, t0 * P:t0 * P + w], m.bank(6 + n % 2, w), ACT.Copy
                                             ).then_inc(rekept, 1)
                if c:
                    b, u = c - 1, (c - 1) % 2
                    act.wait_ge(turned, b + 1)
                    if 2 <= b < QK + 2:
                        act.wait_ge(normed, b - 1)
                    if b - 2 >= QK:
                        act.wait_ge(tok_stored[u], tok_count(b - 1, u))
                    n = tiles(b)
                    nc.scalar.activation(raw[u][:, 0:n, :], m.psum[:, 3 * NC:3 * NC + n * P].rearrange("p (t n) -> p t n", n=P),
                                         ACT.Copy).then_inc(kept, 1)
                    if b < QK:
                        act.wait_ge(summed, b + 1)
                        nc.scalar.activation(sd[:, :], ssq[:, :], ACT.Sqrt, bias=m.keep["eps_norm"]).then_inc(rooted, 1)

        @block.vector
        def _(dve):
            link = Link(dve, own)
            dve.wait_ge(cw_loaded, 16)
            dve.wait_ge(zeroed, 1)
            for c in range(PARTS):
                if c < PARTS:
                    u = c % 2
                    dve.wait_ge(evac, c + 1)
                    if c >= 2:
                        dve.wait_ge(silued, c - 1)
                    y = conv[u][:, :]
                    link(nc.vector.tensor_scalar(y, padded[u][:, 0:wide], cw[:, c * CONV:c * CONV + 1], None, ALU.mult))
                    for j in range(1, CONV):
                        ins = nc.vector.scalar_tensor_tensor(y, padded[u][:, j:j + wide], cw[:, c * CONV + j:c * CONV + j + 1],
                                                             y, ALU.mult, ALU.add)
                        if j < CONV - 1:
                            link(ins)
                    ins.then_inc(conved, 1)
                if 1 <= c <= QK:
                    b, u = c - 1, (c - 1) % 2
                    n = tiles(b)
                    dve.wait_ge(kept, b + 1)
                    if b >= 2:
                        dve.wait_ge(returned, groups(b - 1))
                        if b - 2 >= H:
                            dve.wait_ge(tok_stored[u], tok_count(b - 1, u))
                    link(nc.vector.tensor_tensor(nrm[u][:, 0:n, :], raw[u][:, 0:n, :], raw[u][:, 0:n, :], ALU.mult))
                    if n < TT and b == 0:
                        link(nc.vector.memset(ssq[:, TL:TT], 1.0))
                    if b:
                        dve.wait_ge(rooted, b)
                    nc.vector.tensor_reduce(ssq[:, 0:n], nrm[u][:, 0:n, :], AX, ALU.add).then_inc(summed, 1)
                    dve.wait_ge(rooted, b + 1)
                    link(nc.vector.reciprocal(sd[:, :], sd[:, :]))
                    if b < H:
                        link(nc.vector.tensor_scalar(sd[:, :], sd[:, :], float(P) ** -0.5, None, ALU.mult))
                    nc.vector.tensor_tensor(nrm[u][:, 0:n, :], raw[u][:, 0:n, :], sd[:, 0:n].unsqueeze(2).to_broadcast([P, n, P]),
                                            ALU.mult).then_inc(normed, 1)
    m.top = top


def token_inputs(m):
    nc, d, ident, hT, wt = m.nc, m.dram, m.keep["ident"], m.keep["hT"], m.keep["wt"]
    top, m.limit = m.top, m.high
    dkT = m.keep["dkT"] = m.nc.alloc_sbuf_tensor_at("dkT", [P, H, TOK], F32, offset=m.high)
    dv = m.keep["dv"] = m.nc.alloc_sbuf_tensor_at("dv", [P, TT, HD], F32, offset=m.high + 4 * H * TOK)
    gates = m.keep["gates"] = m.nc.alloc_sbuf_tensor_at("gates", [P, TT, 16], F32, offset=m.high + 4 * (H * TOK + TT * HD))
    m.scratch("z", [TL, P, HD])
    m.scratch("dqT", [TL, P, HD])
    lhs = [m.sb(f"lhs{u}", [P, KD, P]) for u in range(2)]
    rope = m.sb("rope", [P, TL, 2, DK])
    qs = [m.sb(f"rope_{n}", [P, HD]) for n in ("qcos", "qsin", "q")]
    ks = [m.sb(f"rope_{n}", [P, HD]) for n in ("kcos", "ksin", "k")]
    zst = [m.sb(f"zst{u}", [P, HD]) for u in range(2)]
    qst = [m.sb(f"qst{u}", [P, HD]) for u in range(2)]
    rope_loaded, lhs_ready = m.sem("rope_loaded"), m.sem("d_lhs_ready")
    qk_proj, rest_kept = m.sem("d_qk_proj"), m.sem("d_rest_kept")
    qk_read, roped, turned, turned_kept = m.sem("d_qk_read"), m.sem("d_roped"), m.sem("d_turned"), m.sem("d_turned_kept")
    rest_proj = [m.sem(f"d_rest_proj{u}") for u in range(2)]
    z_stored = [m.sem(f"z_stored{u}") for u in range(2)]
    q_stored = [m.sem(f"q_stored{u}") for u in range(2)]
    own = m.sem("d_dve_link")
    Z, G, Q, K, V = 0, HD, HD + 16, 2 * HD + 16, 3 * HD + 16

    def tiles(eng, body):
        with eng.Fori(0, TL // 2) as i:
            for u in range(2):
                body(i, u, True)
        for u in range(2):
            body(TL // 2, u, False)

    with nc.Block() as block:
        @block.sync
        def _(sp):
            sp.dma_start(rope[:, :, :, :], d["rope"].rearrange("(t p) (f n) -> p t f n", p=P, f=2)).then_inc(rope_loaded, 16)
            with sp.Fori(0, TL // 2) as i:
                for u in range(2):
                    sp.wait_ge(rest_kept, 2 * i + u + 1)
                    sp.dma_start(flat(one(d["z"], 2 * i + u)), zst[u][:, :]).then_inc(z_stored[u], 16)
                    sp.wait_ge(turned_kept, 2 * i + u + 1)
                    sp.dma_start(flat(one(d["dqT"], 2 * i + u)), qst[u][:, :]).then_inc(q_stored[u], 16)
            for u in range(2):
                sp.wait_ge(z_stored[u], 16 * TL // 2)
                sp.wait_ge(q_stored[u], 16 * TL // 2)

        @block.gpsimd
        def _(pool):
            def body(i, u, latent):
                pool.wait_ge(rest_proj[u], i)
                nc.gpsimd.tensor_copy(lhs[u][:, :, :], hT[:, :, bass.ds((2 * i + u) * P, P)]).then_inc(lhs_ready, 1)
            tiles(pool, body)

        @block.tensor
        def _(pe):
            def group(b, u, at, n):
                for k in range(KD):
                    last = nc.tensor.matmul(m.bank(b, n), lhs[u][:, k, :], wt[:, k, at:at + n],
                                            start=(k == 0), stop=(k == KD - 1))
                return last

            def body(i, u, latent):
                t = 2 * i + u
                pe.wait_ge(lhs_ready, t + 1)
                pe.wait_ge(qk_read, t)
                if latent:
                    group(2, u, Q, HD)
                group(3, u, K, HD).then_inc(qk_proj, 1)
                pe.wait_ge(rest_kept, t)
                if latent:
                    group(0, u, Z, HD)
                group(1, u, V, HD)
                group(4, u, G, 16).then_inc(rest_proj[u], 1)
                pe.wait_ge(roped, t + 1)
                pe.wait_ge(turned_kept, t)
                for b, src in ((5, qs[2]), (6, ks[2])):
                    if latent or b == 6:
                        for h in range(H):
                            last = nc.tensor.transpose(m.bank(b, P, h * P), src[:, h * P:(h + 1) * P], ident)
                last.then_inc(turned, 1)

            pe.wait_ge(m.keep["wt_loaded"], 16)
            tiles(pe, body)

        @block.scalar
        def _(act):
            def body(i, u, latent):
                t = 2 * i + u
                act.wait_ge(rest_proj[u], i + 1)
                if latent:
                    act.wait_ge(z_stored[u], 16 * i)
                    nc.scalar.activation(zst[u][:, :], m.bank(0), ACT.Copy)
                nc.scalar.activation(cols(dv[:, bass.ds(t, 1), :]), m.bank(1), ACT.Copy)
                nc.scalar.activation(cols(gates[:, bass.ds(t, 1), :]), m.bank(4, 16), ACT.Copy).then_inc(rest_kept, 1)
                act.wait_ge(turned, t + 1)
                if latent:
                    act.wait_ge(q_stored[u], 16 * i)
                    nc.scalar.activation(qst[u][:, :], m.bank(5), ACT.Copy)
                nc.scalar.activation(dkT[:, :, bass.ds(t * P, P)], m.bank(6).rearrange("p (h n) -> p h n", h=H),
                                     ACT.Copy).then_inc(turned_kept, 1)
            tiles(act, body)

        @block.vector
        def _(dve):
            def heads(ap):
                return ap.rearrange("p (h n) -> p h n", n=DK)

            def rotate(out, c, s):
                o, c, s = (x[:, :].rearrange("p (h a n) -> p h a n", a=2, n=16) for x in (out, c, s))
                nc.vector.tensor_tensor(o[:, :, 0, :], c[:, :, 0, :], s[:, :, 1, :], ALU.subtract)
                return nc.vector.tensor_tensor(o[:, :, 1, :], c[:, :, 1, :], s[:, :, 0, :], ALU.add)

            dve.wait_ge(rope_loaded, 16)
            with dve.Fori(0, TL // 2) as i:
                for u in range(2):
                    t = 2 * i + u
                    dve.wait_ge(qk_proj, t + 1)
                    for b, (c, s, _) in ((2, qs), (3, ks)):
                        for f, x in enumerate((c, s)):
                            table = rope[:, bass.ds(t, 1), f, :].to_broadcast([P, 2 * H, DK])
                            last = nc.vector.tensor_tensor(heads(x[:, :]), heads(m.bank(b)), table, ALU.mult)
                    last.then_inc(qk_read, 1)
                    dve.wait_ge(qk_read, t + 1)
                    dve.wait_ge(turned, t)
                    rotate(qs[2], qs[0], qs[1])
                    rotate(ks[2], ks[0], ks[1]).then_inc(roped, 1)
                    dve.wait_ge(roped, t + 1)
            for u in range(2):
                t = TL + u
                dve.wait_ge(qk_proj, t + 1)
                dve.wait_ge(turned, t)
                nc.vector.tensor_copy(ks[2][:, :], m.bank(3)).then_inc(roped, 1)
                dve.wait_ge(roped, t + 1)
                dve.sem_inc(qk_read, 1)
    m.top = top


class Events:

    def __init__(self, m, label, names):
        self.names = names.split()
        self.sems = [m.sem(f"{label}_{way}") for way in ("forward", "reverse")]

    def at(self, name, s):
        return s * len(self.names) + self.names.index(name) + 1

    def done(self, ins, name, r):
        assert name in self.names
        ins.then_inc(self.sems[r], 1)

    def wait(self, eng, name, r, s):
        eng.wait_ge(self.sems[r], self.at(name, s))

    def wait_last(self, eng, name, r, s):
        if isinstance(s, int) and s == 0:
            return
        eng.wait_ge(self.sems[r], self.at(name, s - 1))


GATE_KINDS = 7
G_G, G_BETA, G_NGC, G_NEGC, G_EGC, G_ETOT, G_TAIL = range(GATE_KINDS)


def delta_gates(m):
    nc, d = m.nc, m.dram
    gates, tri, ones = m.keep["gates"], m.keep["tri"], m.keep["ones"]
    m.top = m.base
    G = m.keep["G"] = m.sb("G", [P, 2, TT, GATE_KINDS, H])
    top = m.top
    rg = m.sb("rg", [P, 2, 2, H])
    a = m.sb("ga", [P, 2, TT, H])
    b = m.sb("gb", [P, 2, TT, H])
    e = m.sb("ge", [P, 2, TT, H])
    gc = m.sb("ggc", [P, 2, 2, TT, H])
    loaded, dve_did, act_did, sums = m.sem("g_loaded"), m.sem("g_dve"), m.sem("g_act"), m.sem("g_sums")

    def gate(raw, r):
        return raw.rearrange("p t (k r h) -> p t k r h", k=2, r=2)[:, :, :, r, :]

    with nc.Block() as block:
        @block.sync
        def _(sp):
            sp.dma_start(rg[:, :, :, :], d["rep_gates"].rearrange("p (w r h) -> p w r h", w=2, r=2)).then_inc(loaded, 16)

        @block.vector
        def _(dve):
            link = Link(dve, dve_did)
            cp = nc.vector.tensor_copy
            dve.wait_ge(loaded, 16)
            for k, dst in ((0, b), (1, a)):
                cp(dst[:, 0, TC:TT, :], gate(gates, 0)[:, 0:TL, k, :])
                cp(dst[:, 0, 0:TC, :], gate(gates, 0)[:, TL:TT, k, :])
                for s in range(TT):
                    last = cp(dst[:, 1, s, :], gate(gates, 1)[:, TT - 1 - s, k, :])
            link(last)
            link(nc.vector.tensor_tensor(a[:, :, :, :], a[:, :, :, :], rg[:, 0, :, :].unsqueeze(2).to_broadcast([P, 2, TT, H]),
                                         ALU.add))
            link(nc.vector.tensor_scalar(e[:, :, :, :], a[:, :, :, :], -1.0, None, ALU.mult))
            link(nc.vector.tensor_tensor(e[:, :, :, :], e[:, :, :, :], a[:, :, :, :], ALU.min))
            dve.wait_ge(act_did, 4)
            nc.vector.tensor_scalar(a[:, :, :, :], a[:, :, :, :], 0.0, None, ALU.max)
            link(nc.vector.tensor_copy(G[:, :, :, G_BETA, :], b[:, :, :, :]))
            link(nc.vector.tensor_tensor(a[:, :, :, :], a[:, :, :, :], e[:, :, :, :], ALU.add))
            link(nc.vector.tensor_tensor(a[:, :, :, :], a[:, :, :, :], rg[:, 1, :, :].unsqueeze(2).to_broadcast([P, 2, TT, H]),
                                         ALU.mult))
            link(nc.vector.tensor_scalar(a[:, :, :, :], a[:, :, :, :], -1.0, None, ALU.mult))
            nc.vector.tensor_copy(G[:, :, :, G_G, :], a[:, :, :, :])
            dve.wait_ge(sums, 1)
            link(nc.vector.tensor_copy(gc[:, :, :, :, :], m.bank(0, 4 * TT * H).rearrange("p (w r t h) -> p w r t h", w=2, r=2, h=H)))
            link(nc.vector.tensor_scalar(G[:, :, :, G_NGC, :], gc[:, 0], -1.0, None, ALU.mult))
            link(nc.vector.tensor_tensor(e[:, :, :, :], gc[:, 1], gc[:, 0], ALU.subtract))
            dve.wait_ge(act_did, 7)
            nc.vector.tensor_scalar(G[:, :, :, G_NEGC, :], G[:, :, :, G_EGC, :], -1.0, None, ALU.mult)

        @block.scalar
        def _(act):
            link = Link(act, act_did)
            act.wait_ge(dve_did, 4)
            link(nc.scalar.activation(e[:, :, :, :], e[:, :, :, :], ACT.Exp))
            link(nc.scalar.activation(rg[:, 1, :, :], rg[:, 1, :, :], ACT.Exp))
            link(nc.scalar.activation(e[:, :, :, :], e[:, :, :, :], ACT.Ln, bias=1.0))
            link(nc.scalar.activation(b[:, :, :, :], b[:, :, :, :], ACT.Sigmoid))
            act.wait_ge(dve_did, 11)
            link(nc.scalar.activation(G[:, :, :, G_EGC, :], gc[:, 0], ACT.Exp))
            link(nc.scalar.activation(G[:, :, :, G_ETOT, :], gc[:, 1], ACT.Exp))
            link(nc.scalar.activation(G[:, :, :, G_TAIL, :], e[:, :, :, :], ACT.Exp))

        @block.tensor
        def _(pe):
            pe.wait_ge(dve_did, 8)
            n = TT * H
            for w in range(2):
                for r in range(2):
                    last = nc.tensor.matmul(m.bank(0, n, (2 * w + r) * n), ones if w else tri[r],
                                            a[:, r].rearrange("p t h -> p (t h)"), start=True, stop=True)
            last.then_inc(sums, 1)
    m.top = top


def delta_rule(m):
    nc, d = m.nc, m.dram
    BF = mybir.dt.bfloat16
    G, ident, ones, tri, level, neg = (m.keep[n] for n in ("G", "ident", "ones", "tri", "level", "neg"))
    top = m.top
    R2 = range(2)
    m.scratch("o", [2, TT, P, HD])
    W = [P, H, P]
    Q32 = P // 4

    def both(name, shape=W, dt=F32):
        return [m.sb(f"{name}{r}", shape, dt) for r in R2]

    def twice(name):
        return [[m.sb(f"{name}{r}{u}", W) for u in R2] for r in R2]

    kT, qT, kt, vt = twice("e_kT"), twice("e_qT"), twice("e_k"), twice("e_v")
    TTf, attn = twice("e_TT"), twice("e_attn")
    am = twice("e_am")
    tg, dec, at = both("e_tg"), both("e_dec"), both("e_at")
    Tf, pf, R, vn, vn2, osb, S = (both("e_" + n) for n in ("T", "pf", "R", "vn", "vn2", "o", "S"))
    Tc, TTc, pc = (both("e_" + n, [P, H, Q32]) for n in ("Tc", "TTc", "pc"))
    identc = m.sb("identc", [P, Q32])
    quad = m.sb("quad", [P, P])
    nego = m.sb("nego", [P, 2, H, P], BF)
    identb = m.sb("identb", [P, P], BF)
    quad_loaded = m.sem("quad_loaded")
    A, B, C, Sb = (lambda r: r), (lambda r: 2 + r), (lambda r: 4 + r), (lambda r: 6 + r)

    loaded = [[m.sem(f"e_loaded{r}{u}") for u in R2] for r in R2]
    stored = [m.sem(f"o_stored{r}") for r in R2]
    order, ready = m.sem("e_dve_link"), m.sem("e_ready")
    pool_prep = Events(m, "e_pool_prep", "TG " + " ".join(f"AM{lv}" for lv in range(LEVELS)))
    pe_prep = Events(m, "e_pe_prep", "RB KK P0 P1 X1 P2 X2 P3 X3 P4 X4 P5 X5 Y5 KQ P6 Y6")
    act_prep = Events(m, "e_act_prep", "dec P1 P2 P3 P4 P5 P6")
    dve_prep = Events(m, "e_dve_prep", "AT Tc0 T0 Tc1 T1 Tc2 T2 Tc3 T3 Tc4 T4 Tf T5 attn TT")
    pe_scan = Events(m, "e_pe_scan", "KS QS TR AV KV")
    act_scan = Events(m, "e_act_scan", "QS vn2")
    dve_scan = Events(m, "e_dve_scan", "R vn S o")

    def gs(r, s, kind, h=None):
        g = G[:, r, bass.ds(s, 1), kind, :].rearrange("p t h -> p (t h)")
        return g if h is None else g[:, h:h + 1]

    def heads(b, n=P):
        return m.bank(b, H * n).rearrange("p (h n) -> p h n", h=H)

    def own(b):
        return m.psum[:, b * NC:b * NC + H * (P + Q32)].rearrange("p (h n) -> p h n", h=H)[:, :, 0:Q32]

    def halves(ap, b, later):
        v = ap.rearrange("p (g t n) -> p g t n", t=2, n=b)
        return v[:, :, int(later), :]

    def halves_h(ap, b, later):
        v = ap.rearrange("p h (g t n) -> p h g t n", t=2, n=b)
        return v[:, :, :, int(later), :]

    def rounds(eng, order, stages, link=None, links=0):
        def run(s_scan, s_prep):
            for name in order.split():
                kind, s = ("scan", s_scan) if name.startswith("*") else ("prep", s_prep)
                if s is not None:
                    for r in R2:
                        stages[kind, name.lstrip("*")](r, *s)

        link = link or Link(eng, None)
        run(None, (0, 0))
        run((0, 0), (1, 1))
        run((1, 1), (2, 0))
        with link.loop(TT // 2 - 2, 2 * links) as i:
            run((2 * i + 2, 0), (2 * i + 3, 1))
            run((2 * i + 3, 1), (2 * i + 4, 0))
        run((TT - 2, 0), (TT - 1, 1))
        run((TT - 1, 1), None)

    with nc.Block() as block:
        @block.sync
        def _(sp):
            sp.dma_start(quad[:, :], d["quad"][:, 0:P]).then_inc(quad_loaded, 16)
            sp.dma_start(identc[:, :], d["quad"][:, P:P + Q32]).then_inc(quad_loaded, 16)

            def load(r, u, q_src, t, s):
                span = bass.ds(t * P, P)
                for h_src, dst in ((d["kT"], kT), (q_src, qT)):
                    sp.dma_start(dst[r][u][:, :, :], h_src[:, :, span].rearrange("h p n -> p h n")).then_inc(loaded[r][u], 16)
                for src, dst in ((d["k"], kt), (d["v"], vt)):
                    sp.dma_start(dst[r][u][:, :, :], flat(one(src, t)).rearrange("p (h n) -> p h n", h=H)
                                 ).then_inc(loaded[r][u], 16)

            def store(r, s):
                dve_scan.wait(sp, "o", r, s)
                sp.dma_start(flat(one(d["o"][r], s)), osb[r][:, :, :].rearrange("p h n -> p (h n)")).then_inc(stored[r], 16)

            for s in R2:
                for r in R2:
                    load(r, s, d["kT"], TL + s if r == 0 else TT - 1 - s, s)
            with sp.Fori(0, TL // 2) as i:
                mirrored = [i * -2 + (TL - 1 - u) for u in R2]
                for u in R2:
                    s = 2 * i + u
                    for r in R2:
                        pe_scan.wait(sp, "KV", r, s)
                        load(r, u, d["qT"], s if r == 0 else mirrored[u], s)
                        store(r, s)
            for s in (TL, TL + 1):
                for r in R2:
                    store(r, s)
            for r in R2:
                sp.wait_ge(stored[r], 16 * TT)

        @block.gpsimd
        def _(pool):
            def TG(r, s, u):
                pe_prep.wait_last(pool, "RB", r, s)
                ins = nc.gpsimd.tensor_tensor(tg[r][:, :, :], tri[r].unsqueeze(1).to_broadcast(W),
                                              gs(r, s, G_G).unsqueeze(2).to_broadcast(W), ALU.mult)
                pool_prep.done(ins, "TG", r)

            def masked(lv):
                def AM(r, s, u):
                    if lv == 0:
                        dve_prep.wait(pool, "AT", r, s)
                    if lv < 2:
                        pe_prep.wait_last(pool, "P6" if lv == 0 else "P5", r, s)
                    else:
                        pe_prep.wait(pool, f"P{lv - 2}", r, s)
                    ins = nc.gpsimd.tensor_tensor(am[r][lv % 2][:, :, :], at[r][:, :, :],
                                                  level[r][lv].unsqueeze(1).to_broadcast(W), ALU.mult)
                    pool_prep.done(ins, f"AM{lv}", r)
                return AM

            stages = {("prep", "TG"): TG} | {("prep", f"AM{lv}"): masked(lv) for lv in range(LEVELS)}
            rounds(pool, "TG " + " ".join(f"AM{lv}" for lv in range(LEVELS)), stages)

        @block.tensor
        def _(pe):
            mm = nc.tensor.matmul

            def each(out, lhsT, rhs):
                for h in range(H):
                    last = mm(out(h), lhsT(h), rhs(h), start=True, stop=True)
                return last

            def RB(r, s, u):
                pool_prep.wait(pe, "TG", r, s)
                dve_prep.wait_last(pe, "TT", r, s)
                mm(m.bank(A(r)), identb[:, :], nego[:, r, :, :].rearrange("p h n -> p (h n)"), start=True, stop=False)
                pe_prep.done(mm(m.bank(A(r)), ones, tg[r][:, :, :].rearrange("p h n -> p (h n)"), start=False, stop=True),
                             "RB", r)

            def KK(r, s, u):
                pe.wait_ge(loaded[r][u], (s - u) * 32 + 64)
                dve_prep.wait_last(pe, "T5", r, s)
                k = kT[r][u]
                pe_prep.done(each(lambda h: heads(B(r))[:, h, :], lambda h: k[:, h, :], lambda h: k[:, h, :]), "KK", r)

            def KQ(r, s, u):
                dve_scan.wait_last(pe, "o", r, s)
                pe_prep.done(each(lambda h: heads(C(r))[:, h, :], lambda h: kT[r][u][:, h, :], lambda h: qT[r][u][:, h, :]),
                             "KQ", r)

            def compact(b, lhsT, rhs):
                return each(lambda h: heads(b)[:, h, :], lhsT, lambda h: rhs)

            def product(lv):
                def PL(r, s, u):
                    pool_prep.wait(pe, f"AM{lv}", r, s)
                    a = am[r][lv % 2]
                    if lv == 0:
                        act_prep.wait(pe, "dec", r, s)
                        last = compact(A(r), lambda h: a[:, h, :], identc[:, :].unsqueeze(1).to_broadcast([P, H, Q32]))
                    elif lv < 5:
                        dve_prep.wait(pe, f"Tc{lv - 1}", r, s)
                        last = compact(A(r), lambda h: a[:, h, :], Tc[r][:, :, :])
                    else:
                        dve_prep.wait(pe, "Tf" if lv == 5 else "T5", r, s)
                        last = each(lambda h: heads(A(r))[:, h, :], lambda h: a[:, h, :], lambda h: Tf[r][:, h, :])
                    pe_prep.done(last, f"P{lv}", r)
                return PL

            def left(lv):
                def XL(r, s, u):
                    act_prep.wait(pe, f"P{lv}", r, s)
                    dve_prep.wait(pe, f"T{lv - 1}", r, s)
                    if lv < 5:
                        last = compact(B(r), lambda h: TTf[r][u][:, h, :], pc[r][:, :, :])
                    else:
                        last = each(lambda h: heads(B(r), P // 2)[:, h, :], lambda h: TTf[r][u][:, h, :],
                                    lambda h: halves(pf[r][:, h, :], 32, r == 1))
                    pe_prep.done(last, f"X{lv}", r)
                return XL

            def right(lv):
                def YL(r, s, u):
                    act_prep.wait(pe, f"P{lv}", r, s)
                    last = each(lambda h: heads(A(r), P // 2)[:, h, :], lambda h: pf[r][:, h, :],
                                lambda h: halves(TTf[r][u][:, h, :], 1 << lv, r == 0))
                    pe_prep.done(last, f"Y{lv}", r)
                return YL

            def KS(r, s, u):
                dve_scan.wait_last(pe, "S", r, s)
                pe_scan.done(each(lambda h: heads(Sb(r))[:, h, :], lambda h: kT[r][u][:, h, :], lambda h: S[r][:, h, :]), "KS", r)

            def QS(r, s, u):
                dve_prep.wait(pe, "attn", r, s)
                pe_scan.done(each(lambda h: heads(C(r))[:, h, :], lambda h: qT[r][u][:, h, :], lambda h: S[r][:, h, :]), "QS", r)

            def TR(r, s, u):
                dve_scan.wait(pe, "R", r, s)
                dve_prep.wait(pe, "TT", r, s)
                pe_scan.done(each(lambda h: heads(Sb(r))[:, h, :], lambda h: TTf[r][u][:, h, :], lambda h: R[r][:, h, :]), "TR", r)

            def AV(r, s, u):
                dve_scan.wait(pe, "vn", r, s)
                act_scan.wait(pe, "QS", r, s)
                pe_scan.done(each(lambda h: heads(C(r))[:, h, :], lambda h: attn[r][u][:, h, :], lambda h: vn[r][:, h, :]), "AV", r)

            def KV(r, s, u):
                act_scan.wait(pe, "vn2", r, s)
                pe_scan.done(each(lambda h: heads(Sb(r))[:, h, :], lambda h: kt[r][u][:, h, :], lambda h: vn2[r][:, h, :]), "KV", r)

            stages = {("prep", "RB"): RB, ("prep", "KK"): KK, ("prep", "KQ"): KQ, ("prep", "X5"): left(5),
                      ("prep", "Y5"): right(5), ("prep", "Y6"): right(6), ("scan", "KS"): KS, ("scan", "QS"): QS,
                      ("scan", "TR"): TR, ("scan", "AV"): AV, ("scan", "KV"): KV}
            stages |= {("prep", f"P{lv}"): product(lv) for lv in range(LEVELS)}
            stages |= {("prep", f"X{lv}"): left(lv) for lv in range(1, 5)}
            pe.wait_ge(ready, 1)
            pe.wait_ge(quad_loaded, 32)
            rounds(pe, "RB KK *KS *QS P0 P1 X1 *TR P2 X2 P3 X3 *AV *KV P4 X4 P5 X5 Y5 KQ P6 Y6", stages)

        @block.scalar
        def _(act):
            def dec_(r, s, u):
                pe_prep.wait(act, "RB", r, s)
                dve_prep.wait_last(act, "attn", r, s)
                for h in range(H):
                    last = nc.scalar.activation(dec[r][:, h, :], heads(A(r))[:, h, :], ACT.Exp, bias=gs(r, s, G_NGC, h))
                act_prep.done(last, "dec", r)

            def copy(lv):
                def CP(r, s, u):
                    pe_prep.wait(act, f"P{lv}", r, s)
                    if lv == 1:
                        pe_prep.wait_last(act, "X4", r, s)
                    elif lv == 5:
                        pe_prep.wait_last(act, "Y6", r, s)
                    src, dst = (own(A(r)), pc[r]) if lv < 5 else (heads(A(r)), pf[r])
                    act_prep.done(nc.scalar.activation(dst[:, :, :], src, ACT.Copy), f"P{lv}", r)
                return CP

            def QS(r, s, u):
                pe_scan.wait(act, "QS", r, s)
                act.wait_ge(stored[r], s * 16)
                for h in range(H):
                    last = nc.scalar.activation(osb[r][:, h, :], heads(C(r))[:, h, :], ACT.Copy, scale=gs(r, s, G_EGC, h))
                act_scan.done(last, "QS", r)

            def vn2_(r, s, u):
                dve_scan.wait(act, "vn", r, s)
                pe_scan.wait_last(act, "KV", r, s)
                for h in range(H):
                    last = nc.scalar.activation(vn2[r][:, h, :], vn[r][:, h, :], ACT.Copy, scale=gs(r, s, G_TAIL, h))
                act_scan.done(last, "vn2", r)

            stages = {("prep", "dec"): dec_, ("scan", "QS"): QS, ("scan", "vn2"): vn2_}
            stages |= {("prep", f"P{lv}"): copy(lv) for lv in range(1, LEVELS)}
            rounds(act, "dec *QS P1 *vn2 P2 P3 P4 P5 P6", stages)

        @block.vector
        def _(dve):
            link = Link(dve, order)
            tt, cp, stt = nc.vector.tensor_tensor, nc.vector.tensor_copy, nc.vector.scalar_tensor_tensor
            cp(nego[:, 0, :, :], neg[0].unsqueeze(1).to_broadcast(W))
            cp(nego[:, 1, :, :], neg[1].unsqueeze(1).to_broadcast(W))
            for r in R2:
                nc.vector.memset(S[r][:, :, :], 0.0)
            cp(identb[:, :], ident).then_inc(ready, 1)
            dve.wait_ge(quad_loaded, 32)

            def AT(r, s, u):
                pe_prep.wait(dve, "KK", r, s)
                act_prep.wait(dve, "dec", r, s)
                pool_prep.wait_last(dve, "AM6", r, s)
                for h in range(H):
                    last = stt(at[r][:, h, :], heads(B(r))[:, h, :], gs(r, s, G_BETA, h), dec[r][:, h, :], ALU.mult, ALU.mult)
                dve_prep.done(last, "AT", r)

            def spread(dst, src):
                return tt(dst[:, :, :].rearrange("p h (q n) -> p h q n", q=4), src[:, :, :].unsqueeze(2).to_broadcast([P, H, 4, Q32]),
                          quad[:, :].rearrange("p (q n) -> p q n", q=4).unsqueeze(1).to_broadcast([P, H, 4, Q32]), ALU.mult)

            def doubled(lv):
                def TL_(r, s, u):
                    if lv == 0:
                        pe_prep.wait(dve, "P0", r, s)
                        new = tt(Tc[r][:, :, :], identc[:, :].unsqueeze(1).to_broadcast([P, H, Q32]), own(A(r)), ALU.subtract)
                        dve_prep.done(new, "Tc0", r)
                    else:
                        pe_prep.wait(dve, f"X{lv}", r, s)
                        dve_prep.done(tt(Tc[r][:, :, :], Tc[r][:, :, :], own(B(r)), ALU.subtract), f"Tc{lv}", r)
                    dve_prep.wait(dve, f"Tc{lv}", r, s)
                    link(nc.vector.transpose(TTc[r][:, :, :].rearrange("p h n -> p (h n)"),
                                             Tc[r][:, :, :].rearrange("p h n -> p (h n)")))
                    if lv == 0 and not (isinstance(s, int) and s < 2):
                        pe_scan.wait(dve, "TR", r, s - 2)
                    dve_prep.done(spread(TTf[r][u], TTc[r]), f"T{lv}", r)
                return TL_

            def Tf_(r, s, u):
                dve_prep.done(spread(Tf[r], Tc[r]), "Tf", r)

            def T5(r, s, u):
                pe_prep.wait(dve, "Y5", r, s)
                dve_prep.wait(dve, "Tf", r, s)
                for dst, b, later in ((Tf[r], B(r), r == 1), (TTf[r][u], A(r), r == 0)):
                    for h in range(H):
                        v = halves(dst[:, h, :], 32, later)
                        last = tt(v, v, m.bank(b, P // 2, h * P // 2).rearrange("p (g n) -> p g n", g=2), ALU.subtract)
                dve_prep.done(last, "T5", r)

            def TT_(r, s, u):
                pe_prep.wait(dve, "Y6", r, s)
                v = halves_h(TTf[r][u][:, :, :], 64, r == 0).rearrange("p h g n -> p h (g n)")
                dve_prep.done(tt(v, v, heads(A(r), P // 2), ALU.subtract), "TT", r)

            def attn_(r, s, u):
                pe_prep.wait(dve, "KQ", r, s)
                if not (isinstance(s, int) and s < 2):
                    pe_scan.wait(dve, "AV", r, s - 2)
                dve_prep.done(tt(attn[r][u][:, :, :], heads(C(r)), dec[r][:, :, :], ALU.mult), "attn", r)

            def R_(r, s, u):
                pe_scan.wait(dve, "KS", r, s)
                pe_scan.wait_last(dve, "TR", r, s)
                for h in range(H):
                    last = stt(R[r][:, h, :], heads(Sb(r))[:, h, :], gs(r, s, G_NEGC, h), vt[r][u][:, h, :], ALU.mult, ALU.add)
                dve_scan.done(last, "R", r)

            def vn_(r, s, u):
                pe_scan.wait(dve, "TR", r, s)
                dve_scan.done(tt(vn[r][:, :, :], heads(Sb(r)), gs(r, s, G_BETA).unsqueeze(2).to_broadcast(W), ALU.mult), "vn", r)

            def S_(r, s, u):
                pe_scan.wait(dve, "KV", r, s)
                for h in range(H):
                    last = stt(S[r][:, h, :], S[r][:, h, :], gs(r, s, G_ETOT, h), heads(Sb(r))[:, h, :], ALU.mult, ALU.add)
                dve_scan.done(last, "S", r)

            def o_(r, s, u):
                pe_scan.wait(dve, "AV", r, s)
                dve_scan.done(tt(osb[r][:, :, :], osb[r][:, :, :], heads(C(r)), ALU.add), "o", r)

            stages = {("prep", "AT"): AT, ("prep", "Tf"): Tf_, ("prep", "T5"): T5, ("prep", "TT"): TT_, ("prep", "attn"): attn_,
                      ("scan", "R"): R_, ("scan", "vn"): vn_, ("scan", "S"): S_, ("scan", "o"): o_}
            stages |= {("prep", f"T{lv}"): doubled(lv) for lv in range(5)}
            rounds(dve, "AT *R T0 T1 *vn T2 T3 *S *o T4 Tf T5 attn TT", stages, link, 2 * 5)
    m.top = top


def attention(m):
    nc, d, ident = m.nc, m.dram, m.keep["ident"]
    dkT, dv = m.keep["dkT"], m.keep["dv"]
    top = m.top
    m.scratch("od", [TL, P, HD])
    SC = float(DK) ** -0.5
    lamr = m.sb("lamr", [P, 4, DK])
    lprod = m.sb("lprod", [P, 2, DK])
    lsum = m.sb("lsum", [P, 2])
    nlam = m.sb("nlam", [P, 1])
    qT = [m.sb(f"f_qT{u}", [P, H, P]) for u in range(2)]
    E = [[m.sb(f"f_E{p}{c}", [P, TOK]) for c in range(2)] for p in range(2)]
    A = [m.sb(f"f_A{p}", [P, TOK]) for p in range(2)]
    AT = [m.sb(f"f_AT{p}", [P, TT, P]) for p in range(2)]
    mx = [[m.sb(f"f_mx{p}{c}", [P, 1]) for c in range(2)] for p in range(2)]
    rs = [[m.sb(f"f_rs{p}{c}", [P, 1]) for c in range(2)] for p in range(2)]
    cf = m.sb("f_cf", [P, 1])
    r1 = [m.sb(f"f_r1{u}", [P, H]) for u in range(2)]
    ob = [m.sb(f"f_o{u}", [P, H, P]) for u in range(2)]
    lam_loaded, dve_lam, act_lam = m.sem("lam_loaded"), m.sem("lam_dve"), m.sem("lam_act")
    q_loaded = [m.sem(f"f_q_loaded{u}") for u in range(2)]
    stored = [m.sem(f"f_stored{u}") for u in range(2)]
    scored, maxed, exped = ([m.sem(f"f_{n}{c}") for c in range(2)] for n in ("scored", "maxed", "exped"))
    mixed, summed, tile_kept = m.sem("f_mixed"), m.sem("f_summed"), m.sem("f_tile_kept")
    turned = [m.sem(f"f_turned{p}") for p in range(2)]
    kept = m.sem("f_kept")
    own = m.sem("f_dve_link")
    GROUPS = [(0, 4), (4, 4), (8, 2)]

    def tiles(eng, body, link=None, links=0):
        link = link or Link(eng, None)
        with link.loop(TL // 2 - 1, 2 * links) as i:
            for u in range(2):
                body(2 * i + u, i, u, False)
        body(TL - 2, TL // 2 - 1, 0, False)
        body(TL - 1, TL // 2 - 1, 1, True)

    with nc.Block() as block:
        @block.sync
        def _(sp):
            sp.dma_start(lamr[:, :, :], d["rep_lambda"].rearrange("p (a n) -> p a n", n=DK)).then_inc(lam_loaded, 16)

            def load(t, i, u):
                sp.dma_start(qT[u][:, :, :], flat(one(d["dqT"], t)).rearrange("p (h n) -> p h n", h=H)).then_inc(q_loaded[u], 16)

            def store(t, u):
                sp.wait_ge(tile_kept, t + 1)
                sp.dma_start(flat(one(d["od"], t)), ob[u][:, :, :].rearrange("p h n -> p (h n)")).then_inc(stored[u], 16)

            load(0, 0, 0)
            load(1, 0, 1)
            with sp.Fori(0, TL // 2 - 1) as i:
                for u in range(2):
                    t = 2 * i + u
                    store(t, u)
                    load(t + 2, i, u)
            for t in (TL - 2, TL - 1):
                store(t, t % 2)
            for u in range(2):
                sp.wait_ge(stored[u], 16 * (TL // 2))

        @block.tensor
        def _(pe):
            def score(n, u, h, c, pieces):
                rows = slice(c * DK, (c + 1) * DK)
                if 0 in pieces:
                    pe.wait_ge(exped[c], n)
                for piece in pieces:
                    key, w = piece * NC, min(NC, TOK - piece * NC)
                    last = nc.tensor.matmul(m.bank(3 * c + piece, w), qT[u][rows, h, :], dkT[rows, h, key:key + w], start=True, stop=True)
                if 2 in pieces:
                    last.then_inc(scored[c], 1)

            def turn(n, h, g):
                t0, w = GROUPS[g]
                if g == 0:
                    pe.wait_ge(mixed, n + 1)
                pe.wait_ge(kept, 3 * n + g)
                for t in range(t0, t0 + w):
                    last = nc.tensor.transpose(m.bank(6, P, (t - t0) * P), A[h % 2][:, t * P:(t + 1) * P], ident)
                last.then_inc(turned[h % 2], 1)

            def apply(n, h, g):
                t0, w = GROUPS[g]
                pe.wait_ge(kept, 3 * n + g + 1)
                for t in range(t0, t0 + w):
                    last = nc.tensor.matmul(m.bank(7, P, h * P), AT[h % 2][:, t, :], dv[:, t, h * P:(h + 1) * P],
                                            start=(t == 0), stop=(t == TT - 1))
                if g == 2:
                    last.then_inc(summed, 1)

            def body(t, i, u, final):
                for h in range(H):
                    n = t * H + h
                    more = h < H - 1 or not final
                    v, k = (u, h + 1) if h < H - 1 else (1 - u, 0)
                    if more:
                        if k == 0:
                            pe.wait_ge(q_loaded[v], 16 * (i + u) + 16)
                        score(n + 1, v, k, 0, (0, 1, 2))
                        score(n + 1, v, k, 1, (0,))
                    turn(n, h, 0)
                    if more:
                        score(n + 1, v, k, 1, (1, 2))
                    turn(n, h, 1)
                    if h == 0:
                        pe.wait_ge(tile_kept, t)
                    apply(n, h, 0)
                    turn(n, h, 2)
                    apply(n, h, 1)
                    apply(n, h, 2)

            pe.wait_ge(q_loaded[0], 16)
            for c in range(2):
                score(0, 0, 0, c, (0, 1, 2))
            tiles(pe, body)

        @block.scalar
        def _(act):
            act.wait_ge(dve_lam, 2)
            nc.scalar.activation(lsum[:, :], lsum[:, :], ACT.Exp).then_inc(act_lam, 1)

            def exp(n, h, c):
                act.wait_ge(maxed[c], n + 1)
                nc.scalar.activation(E[h % 2][c][:, :], m.psum[:, 3 * c * NC:3 * c * NC + TOK], ACT.Exp, bias=mx[h % 2][c][:, :],
                                     scale=SC, accum_out=rs[h % 2][c][:, :]).then_inc(exped[c], 1)

            def keep(t, h, g):
                t0, w = GROUPS[g]
                act.wait_ge(turned[h % 2], 3 * (t * (H // 2) + h // 2) + g + 1)
                nc.scalar.activation(AT[h % 2][:, t0:t0 + w, :].rearrange("p t n -> p (t n)"), m.bank(6, w * P), ACT.Copy
                                     ).then_inc(kept, 1)

            def body(t, i, u, final):
                for h in range(H):
                    n = t * H + h
                    more = h < H - 1 or not final
                    keep(t, h, 0)
                    if more:
                        exp(n + 1, (h + 1) % H, 0)
                    keep(t, h, 1)
                    keep(t, h, 2)
                    if more:
                        exp(n + 1, (h + 1) % H, 1)

            for c in range(2):
                exp(0, 0, c)
            tiles(act, body)

        @block.vector
        def _(dve):
            link = Link(dve, own)
            dve.wait_ge(lam_loaded, 16)
            for w in range(2):
                last = nc.vector.tensor_tensor(lprod[:, w, :], lamr[:, 2 * w, :], lamr[:, 2 * w + 1, :], ALU.mult)
            last.then_inc(dve_lam, 1)
            dve.wait_ge(dve_lam, 1)
            nc.vector.tensor_reduce(lsum[:, :], lprod[:, :, :], AX, ALU.add).then_inc(dve_lam, 1)
            dve.wait_ge(act_lam, 1)
            link(nc.vector.tensor_tensor(nlam[:, :], lsum[:, 1:2], lsum[:, 0:1], ALU.subtract))
            link(nc.vector.tensor_scalar(nlam[:, :], nlam[:, :], -LAM_INIT, None, ALU.add))

            def maxes(n, h):
                for c in range(2):
                    dve.wait_ge(scored[c], n + 1)
                    link(nc.vector.tensor_reduce(mx[h % 2][c][:, :], m.psum[:, 3 * c * NC:3 * c * NC + TOK], AX, ALU.max))
                    nc.vector.tensor_scalar(mx[h % 2][c][:, :], mx[h % 2][c][:, :], -SC, None, ALU.mult).then_inc(maxed[c], 1)

            def mix(t, n, h, u):
                dve.wait_ge(exped[1], n + 1)
                nc.vector.reciprocal(r1[u][:, h:h + 1], rs[h % 2][0][:, :])
                link(nc.vector.reciprocal(cf[:, :], rs[h % 2][1][:, :]))
                link(nc.vector.scalar_tensor_tensor(cf[:, :], rs[h % 2][0][:, :], nlam[:, :], cf[:, :], ALU.mult, ALU.mult))
                dve.wait_ge(turned[h % 2], 3 * (t * (H // 2) + h // 2))
                nc.vector.scalar_tensor_tensor(A[h % 2][:, :], E[h % 2][1][:, :], cf[:, :], E[h % 2][0][:, :], ALU.mult, ALU.add
                                               ).then_inc(mixed, 1)

            def body(t, i, u, final):
                for h in range(H):
                    n = t * H + h
                    mix(t, n, h, u)
                    if h < H - 1 or not final:
                        maxes(n + 1, (h + 1) % H)
                dve.wait_ge(summed, H * t + H)
                dve.wait_ge(stored[u], 16 * i)
                nc.vector.tensor_tensor(ob[u][:, :, :], m.bank(7).rearrange("p (h n) -> p h n", h=H),
                                        r1[u][:, :].unsqueeze(2).to_broadcast([P, H, P]), ALU.mult).then_inc(tile_kept, 1)

            maxes(0, 0)
            tiles(dve, body, link, 4 * H)
    m.top = top


def layer_norm_stats(nc, dve, link, st, mv, src, plain=False):
    for c in range(2):
        last = nc.vector.bn_stats(st[:, c, :], src[:, c * NC:(c + 1) * NC])
    link(last, plain=plain)
    link(nc.vector.bn_aggr(mv[:, :], st[:, :, :].rearrange("p a b -> p (a b)")))


def mixed_output(m):
    nc, d, ident, modT = m.nc, m.dram, m.keep["ident"], m.keep["modT"]
    m.top, m.limit = m.base, 229312
    lg = m.keep["lg"] = m.sb("lg", [P, TL, NG + NE])
    top = m.top
    m.scratch("x1", [TL, P, D])
    m.scratch("xn2", [SEQ, D])
    m.scratch("token_of", [(BLOCKS + 2) * P, 1], I32)
    R2 = range(2)

    def twice(name, shape):
        return [m.sb(f"g_{name}{u}", shape) for u in R2]

    rep_mod = m.sb("rep_mod", [P, D])
    rep_ln = m.sb("rep_ln", [P, 2, D])
    w_route = m.sb("w_route", [P, KD, NG + NE])
    w_out = m.sb("w_out", [P, KD, D])
    nw = m.sb("nw", [P, 2, P])
    of, orv, zt = (twice(n, [P, HD]) for n in ("of", "or", "z"))
    Y = twice("Y", [P, 2 * H, P])
    sq = m.sb("g_sq", [P, 2 * H, P])
    ms = twice("ms", [P, 2 * H])
    yT, h2T = (twice(n, [P, KD, P]) for n in ("yT", "h2T"))
    yo, xt, x1, xn = (twice(n, [P, D]) for n in ("yo", "xt", "x1", "xn"))
    st = m.sb("g_st", [P, 2, 6])
    mv, sd = ([twice(f"{n}{w}", [P, k]) for w in R2] for n, k in (("mv", 2), ("sd", 1)))
    none = m.sb("g_none", [P, BLOCKS + 2], I32)

    w_loaded, rows_loaded = m.sem("g_w_loaded"), m.sem("g_rows_loaded")
    loaded, x_loaded, x1_stored, xn_stored = ([m.sem(f"g_{n}{u}") for u in R2] for n in ("loaded", "x_loaded", "x1_stored", "xn_stored"))
    gated, summed, rooted, normed, turned, kept = (m.sem("g_" + n) for n in ("gated", "summed", "rooted", "normed", "turned", "kept"))
    projected, left, scaled = (m.sem("g_" + n) for n in ("projected", "left", "scaled"))
    stats, std = ([m.sem(f"g_{n}{w}") for w in R2] for n in ("stats", "std"))
    added, shaped, x_normed, x_turned, x_kept, routed, lg_kept = (
        m.sem("g_" + n) for n in ("added", "shaped", "x_normed", "x_turned", "x_kept", "routed", "lg_kept"))
    cleared, clear_stored, order = m.sem("g_cleared"), m.sem("g_clear_stored"), m.sem("g_dve_link")
    x = d["tokens"].rearrange("(t p) n -> t p n", p=P)
    xn2 = d["xn2"].rearrange("(t p) n -> t p n", p=P)

    def steps(*stages):
        for t in range(-3, TL + 5):
            for stage, lead in stages:
                if 0 <= t + lead < TL:
                    stage(t + lead)

    with nc.Block() as block:
        @block.sync
        def _(sp):
            def load(t):
                u = t % 2
                if t >= 2:
                    sp.wait_ge(kept, t - 1)
                for dst, src in ((of[u][:, :], d["o"][0, t + TC]), (orv[u][:, :], d["o"][1, TT - 1 - t]), (zt[u][:, :], d["z"][t]),
                                 (Y[u][:, H:, :].rearrange("p h n -> p (h n)"), d["od"][t])):
                    sp.dma_start(dst, src).then_inc(loaded[u], 16)

            def load_x(t):
                if t >= 2:
                    sp.wait_ge(added, t - 1)
                sp.dma_start(xt[t % 2][:, :], x[t]).then_inc(x_loaded[t % 2], 16)

            def store_x1(t):
                sp.wait_ge(shaped, t + 1)
                sp.dma_start(d["x1"][t], x1[t % 2][:, :]).then_inc(x1_stored[t % 2], 16)

            def store_xn(t):
                sp.wait_ge(x_normed, t + 1)
                sp.dma_start(xn2[t], xn[t % 2][:, :]).then_inc(xn_stored[t % 2], 16)

            sp.dma_start(nw[:, :, :], d["rep_norm"].rearrange("p (w n) -> p w n", w=2)).then_inc(w_loaded, 16)
            load(0)
            sp.dma_start(w_out[:, :, :], d["w_out"].rearrange("(k p) n -> p k n", p=P)).then_inc(w_loaded, 16)
            load(1)
            sp.dma_start(rep_mod[:, :], d["mod_rows"][0:1, 2 * D:3 * D].to_broadcast([P, D])).then_inc(rows_loaded, 16)
            sp.dma_start(rep_ln[:, :, :], d["rep_ln"].rearrange("p (w n) -> p w n", w=4)[:, 0:2, :]).then_inc(rows_loaded, 16)
            sp.dma_start(w_route[:, :, :], d["w_route"].rearrange("(k p) n -> p k n", p=P)).then_inc(rows_loaded, 16)
            sp.wait_ge(cleared, 1)
            sp.dma_start(d["token_of"].rearrange("(p b) a -> p (b a)", p=P), none[:, :]).then_inc(clear_stored, 16)
            steps((lambda t: load(t) if t >= 2 else None, 3), (load_x, 1), (store_x1, -2), (store_xn, -3))
            for u in R2:
                sp.wait_ge(x1_stored[u], 16 * (TL // 2))
                sp.wait_ge(xn_stored[u], 16 * (TL // 2))
            sp.wait_ge(clear_stored, 16)

        @block.gpsimd
        def _(pool):
            nc.gpsimd.memset(none[:, :], 0).then_inc(cleared, 1)
            pool.wait_ge(rows_loaded, 48)
            for t in range(TL):
                pool.wait_ge(left, 2 * t + 2)
                y = yo[t % 2][:, :]
                nc.gpsimd.tensor_tensor(y, y, rep_mod[:, :], ALU.mult).then_inc(scaled, 1)

        @block.scalar
        def _(act):
            def gate(t):
                u = t % 2
                act.wait_ge(loaded[u], 64 * (t // 2) + 64)
                nc.scalar.activation(zt[u][:, :], zt[u][:, :], ACT.Silu).then_inc(gated, 1)
                act.wait_ge(summed, t + 1)
                nc.scalar.activation(ms[u][:, :], ms[u][:, :], ACT.Sqrt, bias=m.keep["eps_norm"], scale=1.0 / P).then_inc(rooted, 1)

            def keep(t):
                act.wait_ge(turned, t + 1)
                if t >= 2:
                    act.wait_ge(projected, 2 * t - 2)
                nc.scalar.activation(yT[t % 2][:, :, :].rearrange("p k n -> p (k n)"), m.psum[:, 0:D], ACT.Copy).then_inc(kept, 1)

            def leave(t):
                for c in range(2):
                    act.wait_ge(projected, 2 * t + c + 1)
                    if t >= 2:
                        act.wait_ge(added, t - 1)
                    nc.scalar.activation(yo[t % 2][:, c * NC:(c + 1) * NC], m.bank(2 + c), ACT.Copy).then_inc(left, 1)

            def deviation(w):
                def stage(t):
                    act.wait_ge(stats[w], t + 1)
                    nc.scalar.activation(sd[w][t % 2][:, :], mv[w][t % 2][:, 1:2], ACT.Sqrt, bias=m.keep["eps_ln"]).then_inc(std[w], 1)
                return stage

            def keep_x(t):
                act.wait_ge(x_turned, t + 1)
                if t >= 2:
                    act.wait_ge(routed, t - 1)
                for k in range(KD):
                    last = nc.scalar.activation(h2T[t % 2][:, k, :], m.bank(4 + k // 4)[:, k % 4 * P:(k % 4 + 1) * P], ACT.Identity,
                                                scale=modT[:, 4 * KD + k, 0:1], bias=modT[:, 3 * KD + k, 0:1])
                last.then_inc(x_kept, 1)

            def keep_logits(t):
                act.wait_ge(routed, t + 1)
                nc.scalar.activation(lg[:, t, :], m.bank(6, NG + NE), ACT.Copy).then_inc(lg_kept, 1)

            steps((keep, 1), (keep_logits, -5), (deviation(1), -2), (deviation(0), -1), (gate, 2), (keep_x, -4), (leave, 0))

        @block.vector
        def _(dve):
            link = Link(dve, order)
            tt, stt = nc.vector.tensor_tensor, nc.vector.scalar_tensor_tensor
            W8 = [P, 2 * H, P]

            def mix(t):
                u = t % 2
                ya, yb = Y[u][:, 0:H, :], Y[u][:, H:, :]
                flat_a = ya.rearrange("p h n -> p (h n)")
                dve.wait_ge(loaded[u], 64 * (t // 2) + 64)
                link(tt(flat_a, of[u][:, :], orv[u][:, :], ALU.add))
                link(tt(sq[:, :, :], Y[u][:, :, :], Y[u][:, :, :], ALU.mult))
                nc.vector.tensor_reduce(ms[u][:, :], sq[:, :, :], AX, ALU.add).then_inc(summed, 1)
                dve.wait_ge(rooted, t + 1)
                link(nc.vector.reciprocal(ms[u][:, :], ms[u][:, :]))
                link(tt(Y[u][:, :, :], Y[u][:, :, :], ms[u][:, :].unsqueeze(2).to_broadcast(W8), ALU.mult))
                tt(ya, ya, nw[:, 0, :].unsqueeze(1).to_broadcast([P, H, P]), ALU.mult)
                link(tt(yb, yb, nw[:, 1, :].unsqueeze(1).to_broadcast([P, H, P]), ALU.mult))
                dve.wait_ge(gated, t + 1)
                tt(flat_a, flat_a, zt[u][:, :], ALU.mult).then_inc(normed, 1)

            def add(t):
                u = t % 2
                dve.wait_ge(scaled, t + 1)
                dve.wait_ge(x_loaded[u], 16 * (t // 2) + 16)
                if t >= 2:
                    dve.wait_ge(x1_stored[u], 16 * (t // 2))
                stt(x1[u][:, :], xt[u][:, :], ALPHA, yo[u][:, :], ALU.mult, ALU.add).then_inc(added, 1)
                dve.wait_ge(added, t + 1)
                layer_norm_stats(nc, dve, link, st, mv[0][u], x1[u])
                dve.sem_inc(stats[0], 1)

            def norm(t):
                u = t % 2
                dve.wait_ge(std[0], t + 1)
                link(nc.vector.reciprocal(sd[0][u][:, :], sd[0][u][:, :]))
                link(nc.vector.tensor_scalar(x1[u][:, :], x1[u][:, :], mv[0][u][:, 0:1], sd[0][u][:, :], ALU.subtract, ALU.mult))
                link(tt(x1[u][:, :], x1[u][:, :], rep_ln[:, 0, :], ALU.mult))
                tt(x1[u][:, :], x1[u][:, :], rep_ln[:, 1, :], ALU.add).then_inc(shaped, 1)
                dve.wait_ge(shaped, t + 1)
                layer_norm_stats(nc, dve, link, st, mv[1][u], x1[u])
                dve.sem_inc(stats[1], 1)

            def norm_again(t):
                u = t % 2
                dve.wait_ge(std[1], t + 1)
                link(nc.vector.reciprocal(sd[1][u][:, :], sd[1][u][:, :]))
                if t >= 2:
                    dve.wait_ge(x_turned, t - 1)
                    dve.wait_ge(xn_stored[u], 16 * (t // 2))
                link(nc.vector.tensor_scalar(xn[u][:, :], x1[u][:, :], mv[1][u][:, 0:1], sd[1][u][:, :], ALU.subtract, ALU.mult))
                dve.sem_inc(x_normed, 1)

            dve.wait_ge(w_loaded, 32)
            link(nc.vector.tensor_scalar(nw[:, 1, :], nw[:, 1, :], 1.0 - LAM_INIT, None, ALU.mult))
            dve.wait_ge(rows_loaded, 48)
            steps((norm_again, -3), (norm, -2), (add, -1), (mix, 2))

        @block.tensor
        def _(pe):
            def turn(t):
                pe.wait_ge(normed, t + 1)
                if t:
                    pe.wait_ge(kept, t)
                for k in range(KD):
                    last = nc.tensor.transpose(m.psum[:, k * P:(k + 1) * P], Y[t % 2][:, k, :], ident)
                last.then_inc(turned, 1)

            def project(t):
                pe.wait_ge(kept, t + 1)
                for c in range(2):
                    if t:
                        pe.wait_ge(left, 2 * t - 1 + c)
                    for k in range(KD):
                        last = nc.tensor.matmul(m.bank(2 + c), yT[t % 2][:, k, :], w_out[:, k, c * NC:(c + 1) * NC],
                                                start=(k == 0), stop=(k == KD - 1))
                    last.then_inc(projected, 1)

            def turn_x(t):
                pe.wait_ge(x_normed, t + 1)
                if t:
                    pe.wait_ge(x_kept, t)
                for k in range(KD):
                    last = nc.tensor.transpose(m.psum[:, 4 * NC + k * P:4 * NC + (k + 1) * P], xn[t % 2][:, k * P:(k + 1) * P], ident)
                last.then_inc(x_turned, 1)

            def route(t):
                pe.wait_ge(x_kept, t + 1)
                if t:
                    pe.wait_ge(lg_kept, t)
                for k in range(KD):
                    last = nc.tensor.matmul(m.bank(6, NG + NE), h2T[t % 2][:, k, :], w_route[:, k, :], start=(k == 0), stop=(k == KD - 1))
                last.then_inc(routed, 1)

            pe.wait_ge(w_loaded, 32)
            pe.wait_ge(rows_loaded, 48)
            steps((turn, 1), (project, 0), (route, -4), (turn_x, -3))
    m.top = top


def load_expert(m, sp, place, u, used):
    plan = m.keep["plan"]
    e = sp.value_load(plan[0:1, bass.ds(place + PLAN_EXPERT, 1)], min_val=0, max_val=NE - 1)
    if used:
        end = sp.value_load(plan[0:1, bass.ds(place + (PLAN_END - 2), 1)], min_val=1, max_val=BLOCKS)
    for n, W in m.keep["weights"].items():
        if used:
            sp.wait_ge(used[n], end)
        src = m.dram[f"w_{n}"].rearrange("e (k p) n -> e p k n", p=P)
        sp.dma_start(W[:, u, :, :], one(src, e).rearrange("e p k n -> (e p) k n")).then_inc(m.keep["weights_loaded"][n][u], 16)


def routing(m):
    nc, d, small, ones, before, lg = m.nc, m.dram, m.keep["small"], m.keep["ones"], m.keep["before"], m.keep["lg"]
    gate = m.keep["gate"] = m.sb("gate", [P, 2, TL])
    row = m.keep["row"] = m.sb("row", [P, 2, TL], I32)
    plan = m.keep["plan"] = m.sb("plan", [P, PLAN], I32)
    tok = m.keep["tok"] = m.sb("tok", [P, BLOCKS + 2], I32)
    weights_at = m.top
    weights = m.keep["weights"] = {"gate": m.sb("w_gate", [P, 2, KD, DE]), "up": m.sb("w_up", [P, 2, KD, DE]),
                                   "down": m.sb("w_down", [P, 2, DE // P, D])}
    m.keep["rests"] = {n: nc.alloc_sbuf_tensor_at(f"rest_{n}", w.shape, F32R, offset=weights_at + at * 8 * KD * DE)
                       for at, (n, w) in enumerate(weights.items())}
    weights_loaded = m.keep["weights_loaded"] = {n: [m.sem(f"w_{n}_loaded{u}", lasting=True) for u in range(2)] for n in weights}
    top = m.top
    T8 = [P, TL]
    names = "gmax gsum pg best tie m1 m2 e2 den".split()
    v = {n: m.sb("r_" + n, T8) for n in names}
    rb = m.sb("r_bias", [P, NG + NE])
    oh = m.sb("r_group", [P, TL, NG])
    eg = m.sb("r_eg", [P, TL, NG])
    pick = m.sb("r_pick", [P, TL, NG, EG])
    li = m.sb("r_li", [P, TL, EG])
    ohs = [m.sb(f"r_first{j}", [P, TL, EG]) for j in range(2)]
    E = [m.sb(f"r_E{j}", [P, TL, NE]) for j in range(2)]
    M = m.sb("r_M", [P, TL, NE])
    rank = m.sb("r_rank", [P, TL, NE])
    upto_tile = m.sb("r_upto_tile", [P, TL + 1, NE])
    nblk = m.sb("r_nblk", [P, NE])
    ends = m.sb("r_ends", [P, NE])
    base = m.sb("r_base", [P, NE])
    onesr = m.sb("r_ones", [P, NE])
    over = m.sb("r_over", [P, NE, EG])
    own_of = m.sb("r_own", [P, BLOCKS, NE])
    some = m.sb("r_some", [P, NE])
    nth = m.sb("r_nth", [P, NE])
    upto = m.sb("r_upto", [P, NE, NE])
    last_ = m.sb("r_last", [P, 1])
    planf = m.sb("r_planf", [P, PLAN])
    rowf = m.sb("r_rowf", [P, 2, TL])
    ids = m.sb("r_ids", [P, TL], I32)
    loaded, dve_did, act_did, counted = m.sem("r_loaded"), m.sem("r_dve"), m.sem("r_act"), m.sem("r_counted")
    planned = m.sem("r_planned")
    rows_ready, chosen, scattered, tok_loaded = m.sem("r_rows_ready"), m.sem("r_chosen"), m.sem("r_scattered"), m.sem("r_tok_loaded")
    desc = {NG: small[:, 0:4], EG: small[:, 4:12]}

    with nc.Block() as block:
        @block.sync
        def _(sp):
            sp.dma_start(ids[:, :], d["ids"]).then_inc(loaded, 16)
            sp.dma_start(rb[:, :], d["rep_route"]).then_inc(loaded, 16)
            sp.wait_ge(planned, 1)
            load_expert(m, sp, 0, 0, None)
            load_expert(m, sp, 1, 1, None)

        @block.gpsimd
        def _(pool):
            pool.wait_ge(loaded, 32)
            pool.wait_ge(rows_ready, 1)
            for j in range(2):
                for t in range(TL):
                    pool.indirect_dma_start(out=d["token_of"], out_offset=bass.IndirectOffsetOnAxis(ap=row[:, j, t:t + 1], axis=0),
                                            in_=ids[:, t:t + 1], in_offset=None).then_inc(scattered, 16)

        @block.vector
        def _(dve):
            link = Link(dve, dve_did)
            tt, ts, red = nc.vector.tensor_tensor, nc.vector.tensor_scalar, nc.vector.tensor_reduce

            def wide(ap, n):
                return ap.unsqueeze(2).to_broadcast([P, TL, n])

            def first_of(out, values, top_, n):
                link(tt(out, values, wide(top_[:, :], n), ALU.is_equal))
                link(tt(out, out, desc[n].unsqueeze(1).to_broadcast([P, TL, n]), ALU.mult))
                link(red(v["tie"][:, :], out, AX, ALU.max))
                link(tt(out, out, wide(v["tie"][:, :], n), ALU.is_equal))

            dve.wait_ge(loaded, 32)
            link(tt(lg[:, :, :], lg[:, :, :], rb[:, :].unsqueeze(1).to_broadcast([P, TL, NG + NE]), ALU.add))
            g, e = lg[:, :, 0:NG], lg[:, :, NG:]
            link(red(v["gmax"][:, :], g, AX, ALU.max))
            link(tt(eg[:, :, :], g, wide(v["gmax"][:, :], NG), ALU.subtract))
            dve.sem_inc(chosen, 1)
            first_of(oh[:, :, :], g, v["gmax"], NG)
            link(tt(pick[:, :, :, :], e.rearrange("p t (g e) -> p t g e", g=NG),
                    oh[:, :, :].unsqueeze(3).to_broadcast([P, TL, NG, EG]), ALU.mult))
            link(red(li[:, :, :], pick[:, :, :, :].rearrange("p t g e -> p t e g"), AX, ALU.add))
            link(red(v["m1"][:, :], li[:, :, :], AX, ALU.max))
            first_of(ohs[0][:, :, :], li[:, :, :], v["m1"], EG)
            link(nc.vector.scalar_tensor_tensor(li[:, :, :], ohs[0][:, :, :], -BIG, li[:, :, :], ALU.mult, ALU.add))
            link(red(v["m2"][:, :], li[:, :, :], AX, ALU.max))
            first_of(ohs[1][:, :, :], li[:, :, :], v["m2"], EG)
            link(tt(v["e2"][:, :], v["m2"][:, :], v["m1"][:, :], ALU.subtract))
            dve.sem_inc(chosen, 1)
            for j in range(2):
                last = tt(E[j][:, :, :].rearrange("p t (g e) -> p t g e", g=NG), oh[:, :, :].unsqueeze(3).to_broadcast([P, TL, NG, EG]),
                          ohs[j][:, :, :].unsqueeze(2).to_broadcast([P, TL, NG, EG]), ALU.mult)
            link(last)
            link(tt(M[:, :, :], E[0][:, :, :], E[1][:, :, :], ALU.add))
            dve.sem_inc(chosen, 1)
            dve.wait_ge(act_did, 2)
            link(red(v["gsum"][:, :], eg[:, :, :], AX, ALU.add))
            link(ts(v["den"][:, :], v["e2"][:, :], 1.0, None, ALU.add))
            link(tt(v["den"][:, :], v["den"][:, :], v["gsum"][:, :], ALU.mult))
            link(nc.vector.reciprocal(gate[:, 0, :], v["den"][:, :]))
            link(tt(gate[:, 1, :], gate[:, 0, :], v["e2"][:, :], ALU.mult))
            dve.wait_ge(counted, 1)
            nc.vector.memset(onesr[:, :], 1.0)
            link(nc.vector.memset(upto_tile[:, 0, :], 0.0))
            for t in range(TL):
                link(tt(upto_tile[:, t + 1, :], upto_tile[:, t, :], m.bank(1, NE, t * NE), ALU.add))
            link(tt(rank[:, :, :], m.bank(0, TL * NE).rearrange("p (t e) -> p t e", e=NE), upto_tile[:, 0:TL, :], ALU.add))
            link(tt(over[:, :, :], upto_tile[:, TL, :].unsqueeze(2).to_broadcast([P, NE, EG]), small[:, 12:20].unsqueeze(1).to_broadcast([P, NE, EG]),
                    ALU.is_gt))
            link(red(nblk[:, :], over[:, :, :], AX, ALU.add))
            link(nc.vector.tensor_tensor_scan(ends[:, :], onesr[:, :], nblk[:, :], 0.0, ALU.mult, ALU.add))
            link(tt(base[:, :], ends[:, :], nblk[:, :], ALU.subtract))
            link(ts(base[:, :], base[:, :], float(P), None, ALU.mult))
            link(tt(rank[:, :, :], rank[:, :, :], base[:, :].unsqueeze(1).to_broadcast([P, TL, NE]), ALU.add))
            for j in range(2):
                link(tt(M[:, :, :], E[j][:, :, :], rank[:, :, :], ALU.mult))
                link(red(rowf[:, j, :], M[:, :, :], AX, ALU.add))
            nc.vector.tensor_copy(row[:, :, :], rowf[:, :, :]).then_inc(rows_ready, 1)
            link(ts(some[:, :], nblk[:, :], 1.0, None, ALU.min))
            link(nc.vector.tensor_tensor_scan(nth[:, :], onesr[:, :], some[:, :], 0.0, ALU.mult, ALU.add))
            place = small[:, 20:20 + NE].unsqueeze(2).to_broadcast([P, NE, NE])
            link(tt(upto[:, :, :], nth[:, :].unsqueeze(1).to_broadcast([P, NE, NE]), place, ALU.is_le))
            link(red(planf[:, PLAN_EXPERT:PLAN_EXPERT + NE], upto[:, :, :], AX, ALU.add))
            link(ts(planf[:, PLAN_EXPERT:PLAN_EXPERT + NE], planf[:, PLAN_EXPERT:PLAN_EXPERT + NE], float(NE - 1), None, ALU.min))
            place = small[:, 21:21 + NE].unsqueeze(2).to_broadcast([P, NE, NE])
            link(tt(upto[:, :, :], nth[:, :].unsqueeze(1).to_broadcast([P, NE, NE]), place, ALU.is_le))
            link(tt(upto[:, :, :], upto[:, :, :], nblk[:, :].unsqueeze(1).to_broadcast([P, NE, NE]), ALU.mult))
            link(red(planf[:, PLAN_END:PLAN_END + NE], upto[:, :, :], AX, ALU.add))
            link(tt(own_of[:, :, :], ends[:, :].unsqueeze(1).to_broadcast([P, BLOCKS, NE]),
                    small[:, 20:20 + BLOCKS].unsqueeze(2).to_broadcast([P, BLOCKS, NE]), ALU.is_le))
            link(tt(own_of[:, :, :], own_of[:, :, :], some[:, :].unsqueeze(1).to_broadcast([P, BLOCKS, NE]), ALU.mult))
            rank_of = planf[:, PLAN_RANK:PLAN_RANK + BLOCKS]
            link(red(rank_of, own_of[:, :, :], AX, ALU.add))
            link(ts(last_[:, :], nth[:, NE - 1:NE], -1.0, None, ALU.add))
            link(tt(rank_of, rank_of, last_[:, :].to_broadcast([P, BLOCKS]), ALU.min))
            link(nc.vector.tensor_copy(planf[:, PLAN_BLOCKS:PLAN_BLOCKS + 1], ends[:, NE - 1:NE]))
            link(nc.vector.tensor_copy(planf[:, PLAN_EXPERTS:], nth[:, NE - 1:NE]))
            nc.vector.tensor_copy(plan[:, :], planf[:, :]).then_inc(planned, 1)

        @block.scalar
        def _(act):
            act.wait_ge(chosen, 1)
            nc.scalar.activation(eg[:, :, :], eg[:, :, :], ACT.Exp).then_inc(act_did, 1)
            act.wait_ge(chosen, 2)
            nc.scalar.activation(v["e2"][:, :], v["e2"][:, :], ACT.Exp).then_inc(act_did, 1)
            act.wait_ge(scattered, 16 * 2 * TL)
            act.dma_start(tok[:, :], d["token_of"].rearrange("(b p) a -> p (b a)", p=P),
                          allow_slow_non_contiguous=True).then_inc(tok_loaded, 16)
            act.wait_ge(tok_loaded, 16)

        @block.tensor
        def _(pe):
            pe.wait_ge(chosen, 3)
            every = M[:, :, :].rearrange("p t e -> p (t e)")
            nc.tensor.matmul(m.bank(0, TL * NE), before, every, start=True, stop=True)
            last = nc.tensor.matmul(m.bank(1, TL * NE), ones, every, start=True, stop=True)
            last.then_inc(counted, 1)
    m.top = top


def experts(m):
    nc, d, ident, modT, plan, tok = m.nc, m.dram, m.keep["ident"], m.keep["modT"], m.keep["plan"], m.keep["tok"]
    top = m.top
    m.scratch("yb", [BLOCKS * P, D])
    KE, HALF = DE // P, DE // 2
    CH = 4
    W, rests, loads = m.keep["weights"], m.keep["rests"], m.keep["weights_loaded"]
    heads = {"gate": m.sb("head_gate", [P, KD, DE], F32R), "up": m.sb("head_up", [P, KD, DE], F32R),
             "down": m.sb("head_down", [P, KE, D], F32R)}
    idx = [m.sb(f"i_idx{u}", [P, 1], I32) for u in range(2)]
    xg = [m.sb(f"i_x{u}", [P, D]) for u in range(2)]
    xm = m.sb("i_xm", [P, KD, P])
    xh, xr = ([m.sb(f"i_x_{n}{u}", [P, KD, P], F32R) for u in range(2)] for n in ("head", "rest"))
    nothing = m.sb("i_nothing", [P, D])
    hs = m.sb("i_silu", [P, DE])
    hh = m.sb("i_h", [P, DE])
    hTh, hTr = (m.sb(f"i_hT_{n}", [P, KE, P], F32R) for n in ("head", "rest"))
    yo = [m.sb(f"i_y{u}", [P, D]) for u in range(2)]
    U2 = range(2)
    used = {n: m.sem(f"i_{n}_used") for n in W}
    first_half = {n: m.sem(f"i_{n}_first_half") for n in ("gate", "up")}
    head, rest = ({n: m.sem(f"i_{n}_{part}") for n in W} for part in ("head", "rest"))
    nothing_ready, nothing_stored = m.sem("i_nothing_ready"), m.sem("i_nothing_stored")
    idx_ready, all_stored = m.sem("i_idx_ready"), m.sem("i_all_stored")
    gathered = [m.sem(f"i_gathered{u}") for u in U2]
    stored = [m.sem(f"i_stored{u}") for u in U2]
    x_turned = [m.sem(f"i_x_turned{u}") for u in U2]
    x_kept = [m.sem(f"i_x_kept{u}") for u in U2]
    x_parts = m.sem("i_x_parts")
    silued, mixed, h_turned, h_head, h_kept, y_kept = (
        m.sem("i_" + n) for n in ("silued", "mixed", "h_turned", "h_head", "h_kept", "y_kept"))
    ybt = d["yb"].rearrange("(b p) n -> b p n", p=P)
    LOW = 2 * SEQ // P

    def blocks(eng, body):
        nb = eng.value_load(plan[0:1, PLAN_BLOCKS:PLAN_BLOCKS + 1], min_val=LOW, max_val=BLOCKS - 1)
        with eng.Fori(0, BLOCKS // 2) as i:
            for u in range(2):
                with eng.If(2 * i + u < nb):
                    body(2 * i + u, i, u)
        return nb

    def place_of(eng, b):
        return eng.value_load(plan[0:1, bass.ds(b + PLAN_RANK, 1)], min_val=0, max_val=NE - 1)

    def ahead(eng, b):
        place, after = place_of(eng, b), place_of(eng, b + 1)

        def run(split, *args):
            with eng.If(place < after):
                split(place + 1, b + 1, *args)
        return run

    def of_half(w, place, n, c):
        step = W[n].shape[2] // CH
        if isinstance(place, int):
            return w[n][:, place, c * step:(c + 1) * step, :].rearrange("p k n -> p (k n)")
        return w[n][:, bass.ds(place & 1, 1), c * step:(c + 1) * step, :].rearrange("p a k n -> p (a k n)")

    def of_head(n, c):
        step = W[n].shape[2] // CH
        return heads[n][:, c * step:(c + 1) * step, :].rearrange("p k n -> p (k n)")

    def take_rest(eng, op, place, n, steps):
        for c in steps:
            eng.wait_ge(head[n], place * CH + c + 1)
            op(of_half(rests, place, n, c), of_half(W, place, n, c), of_head(n, c), ALU.subtract).then_inc(rest[n], 1)

    with nc.Block() as block:
        @block.sync
        def _(sp):
            experts_ = sp.value_load(plan[0:1, PLAN_EXPERTS:PLAN_EXPERTS + 1], min_val=2, max_val=NE)
            nb = sp.value_load(plan[0:1, PLAN_BLOCKS:PLAN_BLOCKS + 1], min_val=LOW, max_val=BLOCKS)
            with sp.Fori(0, NE // 2 - 1) as i:
                for u in range(2):
                    with sp.If(2 * i + u + 2 < experts_):
                        load_expert(m, sp, 2 * i + u + 2, u, used)
            sp.wait_ge(nothing_ready, 1)
            with sp.Fori(0, BLOCKS - LOW) as j:
                with sp.If(nb < j + LOW + 1):
                    sp.dma_start(flat(one(ybt, j + LOW)), nothing[:, :]).then_inc(nothing_stored, 16)
                with sp.If(j + LOW < nb):
                    sp.sem_inc(nothing_stored, 16)
            sp.wait_ge(nothing_stored, 16 * (BLOCKS - LOW))
            sp.sem_inc(all_stored, 1)

        @block.gpsimd
        def _(pool):
            nc.gpsimd.memset(nothing[:, :], 0.0).then_inc(nothing_ready, 1)

            def gather(b, i, u):
                pool.wait_ge(x_turned[u], i)
                nc.gpsimd.tensor_copy(idx[u][:, :], tok[:, bass.ds(b, 1)]).then_inc(idx_ready, 1)
                pool.wait_ge(idx_ready, 2 * b + 1)
                pool.sem_inc(idx_ready, 1)
                pool.indirect_dma_start(out=xg[u][:, :], out_offset=None, in_=d["xn2"],
                                        in_offset=bass.IndirectOffsetOnAxis(ap=idx[u][:, :], axis=0)).then_inc(gathered[u], 16)

            def split(place, b):
                take_rest(pool, nc.gpsimd.tensor_tensor, place, "down", range(CH))

            def body(b, i, u):
                gather(b + 2, i + 1, u)
                ahead(pool, b)(split)

            gather(0, 0, 0)
            gather(1, 0, 1)
            take_rest(pool, nc.gpsimd.tensor_tensor, 0, "down", range(CH))
            blocks(pool, body)

        @block.tensor
        def _(pe):
            def turn(i, u):
                pe.wait_ge(gathered[u], 16 * i + 16)
                pe.wait_ge(x_kept[u], i)
                for k in range(KD):
                    last = nc.tensor.transpose(m.bank(k // 4)[:, k % 4 * P:(k % 4 + 1) * P], xg[u][:, k * P:(k + 1) * P], ident)
                last.then_inc(x_turned[u], 1)

            def product(out, xs, ws, first, final):
                passes = ((xs[0], ws[0]), (xs[1], ws[0]), (xs[0], ws[1]))
                for n, (x, w) in enumerate(passes):
                    last = nc.tensor.matmul(out, x, w, start=(first and n == 0), stop=(final and n == 2))
                return last

            def hidden(bank, n, u, place, half, g):
                here = slice(g * HALF, (g + 1) * HALF)
                for k in range(KD):
                    last = product(m.bank(bank, HALF), (xh[u][:, k, :], xr[u][:, k, :]),
                                   (heads[n][:, k, here], cols(rests[n][:, bass.ds(half, 1), k, here])), k == 0, k == KD - 1)
                last.then_inc(used[n] if g else first_half[n], 1)

            def turn_h(b, g):
                pe.wait_ge(mixed, 2 * b + g + 1)
                pe.wait_ge(h_kept, 2 * b + g)
                for k in (2 * g, 2 * g + 1):
                    last = nc.tensor.transpose(m.bank(4, P, k * P), hh[:, k * P:(k + 1) * P], ident)
                last.then_inc(h_turned, 1)

            def down(b, place, half, g):
                pe.wait_ge(h_kept, 2 * b + g + 1)
                pe.wait_ge(rest["down"], place * CH + 2 * g + 2)
                for k in (2 * g, 2 * g + 1):
                    for c in range(2):
                        here = slice(c * NC, (c + 1) * NC)
                        last = product(m.bank(5 + c), (hTh[:, k, :], hTr[:, k, :]),
                                       (heads["down"][:, k, here], cols(rests["down"][:, bass.ds(half, 1), k, here])), k == 0, k == KE - 1)
                return last

            def body(b, i, u):
                place = place_of(pe, b)
                half = place & 1
                pe.wait_ge(x_kept[u], i + 1)
                pe.wait_ge(silued, 2 * b)
                pe.wait_ge(rest["gate"], place * CH + CH)
                hidden(2, "gate", u, place, half, 0)
                turn(i + u, 1 - u)
                pe.wait_ge(mixed, 2 * b)
                pe.wait_ge(rest["up"], place * CH + CH)
                hidden(3, "up", u, place, half, 0)
                hidden(7, "gate", u, place, half, 1)
                turn_h(b, 0)
                pe.wait_ge(mixed, 2 * b + 1)
                hidden(3, "up", u, place, half, 1)
                pe.wait_ge(y_kept, b)
                down(b, place, half, 0)
                turn_h(b, 1)
                down(b, place, half, 1).then_inc(used["down"], 1)

            turn(0, 0)
            blocks(pe, body)

        @block.scalar
        def _(act):
            def wait_loaded(n, place):
                act.wait_ge(loads[n][0], ((place >> 1) + 1) * 16)
                act.wait_ge(loads[n][1], (((place + 1) >> 1) + 1) * 16)

            def take_head(place, b, n):
                wait_loaded(n, place)
                act.wait_ge(used[n], b)
                for c in range(CH):
                    nc.scalar.activation(of_head(n, c), of_half(W, place, n, c), ACT.Copy).then_inc(head[n], 1)

            def keep_h(b, g):
                act.wait_ge(h_turned, 2 * b + g + 1)
                act.wait_ge(used["down"], b)
                nc.scalar.activation(hTh[:, 2 * g:2 * g + 2, :].rearrange("p k n -> p (k n)"), m.bank(4, HALF, g * HALF), ACT.Copy
                                     ).then_inc(h_head, 1)

            def body(b, i, u):
                if_next = ahead(act, b)
                for g in range(2):
                    act.wait_ge((first_half["gate"], used["gate"])[g], b + 1)
                    act.wait_ge(mixed, 2 * b)
                    nc.scalar.activation(hs[:, g * HALF:(g + 1) * HALF], m.bank((2, 7)[g], HALF), ACT.Silu).then_inc(silued, 1)
                keep_h(b, 0)
                if_next(take_head, "gate")
                keep_h(b, 1)
                if_next(take_head, "up")
                act.wait_ge(used["down"], b + 1)
                act.wait_ge(stored[u], 16 * i)
                nc.scalar.activation(yo[u][:, :], m.psum[:, 5 * NC:5 * NC + D], ACT.Copy).then_inc(y_kept, 1)
                act.wait_ge(y_kept, b + 1)
                act.dma_start(flat(one(ybt, b)), yo[u][:, :]).then_inc(stored[u], 16)
                if_next(take_head, "down")

            for n in W:
                act.sem_inc(loads[n][1], 16)
            for n in W:
                act.wait_ge(loads[n][0], 16)
                for c in range(CH):
                    nc.scalar.activation(of_head(n, c), of_half(W, 0, n, c), ACT.Copy).then_inc(head[n], 1)
            nb = blocks(act, body)
            act.wait_ge(stored[0], ((nb + 1) >> 1) * 16)
            act.wait_ge(stored[1], (nb >> 1) * 16)
            act.sem_inc(all_stored, 1)

        @block.vector
        def _(dve):
            tt = nc.vector.tensor_tensor

            def shape(b, i, u):
                dve.wait_ge(x_turned[u], i + 1)
                for k in range(KD):
                    last = nc.vector.tensor_scalar(xm[:, k, :], m.bank(k // 4)[:, k % 4 * P:(k % 4 + 1) * P],
                                                   modT[:, 4 * KD + k, 0:1], modT[:, 3 * KD + k, 0:1], ALU.mult, ALU.add)
                last.then_inc(x_parts, 1)
                dve.wait_ge(x_parts, 2 * b + 1)
                nc.vector.tensor_copy(xh[u][:, :, :], xm[:, :, :]).then_inc(x_parts, 1)
                dve.wait_ge(x_parts, 2 * b + 2)
                tt(xr[u][:, :, :], xm[:, :, :], xh[u][:, :, :], ALU.subtract).then_inc(x_kept[u], 1)

            def mix(b, g):
                here = slice(g * HALF, (g + 1) * HALF)
                dve.wait_ge(silued, 2 * b + g + 1)
                dve.wait_ge((first_half["up"], used["up"])[g], b + 1)
                dve.wait_ge(h_turned, 2 * b + g)
                tt(hh[:, here], hs[:, here], m.bank(3, HALF), ALU.mult).then_inc(mixed, 1)

            def keep_h(b, g):
                ks = slice(2 * g, 2 * g + 2)
                dve.wait_ge(h_head, 2 * b + g + 1)
                tt(hTr[:, ks, :].rearrange("p k n -> p (k n)"), m.bank(4, HALF, g * HALF), hTh[:, ks, :].rearrange("p k n -> p (k n)"),
                   ALU.subtract).then_inc(h_kept, 1)

            def split(place, b, n, steps):
                take_rest(dve, tt, place, n, steps)

            def body(b, i, u):
                if_next = ahead(dve, b)
                shape(b + 1, i + u, 1 - u)
                mix(b, 0)
                keep_h(b, 0)
                if_next(split, "gate", range(CH // 2))
                mix(b, 1)
                keep_h(b, 1)
                if_next(split, "gate", range(CH // 2, CH))
                if_next(split, "up", range(CH))

            shape(0, 0, 0)
            for n in ("gate", "up"):
                take_rest(dve, tt, 0, n, range(CH))
            blocks(dve, body)
    m.top = top


def combine(m):
    nc, d, gate, row = m.nc, m.dram, m.keep["gate"], m.keep["row"]
    rep_g, rep_ln = m.sb("j_rep_g", [P, D]), m.sb("j_rep_ln", [P, 2, D])
    rows_loaded = m.sem("j_rows_loaded")
    RING = 4
    x1, y1, y2 = ([m.sb(f"j_{n}{u}", [P, D]) for u in range(RING)] for n in ("x1", "y1", "y2"))
    acc = [m.sb(f"j_acc{u}", [P, D]) for u in range(RING)]
    idx = [[m.sb(f"j_idx{j}{u}", [P, 1], I32) for u in range(RING)] for j in range(2)]
    st = m.sb("j_st", [P, 2, 6])
    mv = [m.sb(f"j_mv{u}", [P, 2]) for u in range(2)]
    sd = [m.sb(f"j_sd{u}", [P, 1]) for u in range(2)]
    loaded = [m.sem(f"j_loaded{u}") for u in range(RING)]
    gathered = [m.sem(f"j_gathered{u}") for u in range(RING)]
    stored = [m.sem(f"j_stored{u}") for u in range(RING)]
    summed = m.sem("j_summed")
    idx_ready, scaled, stats, std, shaped, ready, own = (
        m.sem("j_" + n) for n in ("idx_ready", "scaled", "stats", "std", "shaped", "ready", "dve_link"))
    out = d["out"].rearrange("(t p) n -> t p n", p=P)

    with nc.Block() as block:
        @block.sync
        def _(sp):
            def load(t):
                sp.dma_start(x1[t % RING][:, :], flat(one(d["x1"], t))).then_inc(loaded[t % RING], 16)

            sp.dma_start(rep_g[:, :], d["mod_rows"][0:1, 5 * D:6 * D].to_broadcast([P, D])).then_inc(rows_loaded, 16)
            sp.dma_start(rep_ln[:, :, :], d["rep_ln"].rearrange("p (w n) -> p w n", w=4)[:, 2:4, :]).then_inc(rows_loaded, 16)
            for t in range(RING):
                load(t)
            for t in range(TL):
                sp.wait_ge(ready, t + 1)
                sp.dma_start(flat(one(out, t)), acc[t % RING][:, :]).then_inc(stored[t % RING], 16)
                if t + RING < TL:
                    load(t + RING)
            for v in range(RING):
                sp.wait_ge(stored[v], 16 * (TL // RING))

        @block.gpsimd
        def _(pool):
            def gather(t):
                v = t % RING
                if t >= RING:
                    pool.wait_ge(summed, t - RING + 1)
                for j in range(2):
                    nc.gpsimd.tensor_copy(idx[j][v][:, :], row[:, j, t:t + 1]).then_inc(idx_ready, 1)
                pool.wait_ge(idx_ready, 2 * t + 2)
                for j, y in enumerate((y1, y2)):
                    pool.indirect_dma_start(out=y[v][:, :], out_offset=None, in_=d["yb"],
                                            in_offset=bass.IndirectOffsetOnAxis(ap=idx[j][v][:, :], axis=0)).then_inc(gathered[v], 16)

            pool.wait_ge(rows_loaded, 32)
            for t in range(RING):
                gather(t)
            for t in range(TL):
                if t + RING < TL:
                    gather(t + RING)
                pool.wait_ge(shaped, t + 1)
                nc.gpsimd.tensor_tensor(acc[t % RING][:, :], acc[t % RING][:, :], rep_ln[:, 1, :], ALU.add).then_inc(ready, 1)

        @block.vector
        def _(dve):
            link = Link(dve, own)
            tt, stt = nc.vector.tensor_tensor, nc.vector.scalar_tensor_tensor

            def add(t):
                y, v = acc[t % RING][:, :], t % RING
                dve.wait_ge(scaled, t + 1)
                stt(y, y2[v][:, :], gate[:, 1, t:t + 1], y, ALU.mult, ALU.add).then_inc(summed, 1)
                dve.wait_ge(summed, t + 1)
                link(tt(y, y, rep_g[:, :], ALU.mult))
                dve.wait_ge(loaded[v], 16 * (t // RING) + 16)
                link(stt(y, x1[v][:, :], ALPHA, y, ALU.mult, ALU.add))
                layer_norm_stats(nc, dve, link, st, mv[t % 2], acc[t % RING])
                dve.sem_inc(stats, 1)

            def norm(t):
                u, y = t % 2, acc[t % RING][:, :]
                dve.wait_ge(std, t + 1)
                link(nc.vector.reciprocal(sd[u][:, :], sd[u][:, :]))
                link(nc.vector.tensor_scalar(y, y, mv[u][:, 0:1], sd[u][:, :], ALU.subtract, ALU.mult))
                tt(y, y, rep_ln[:, 0, :], ALU.mult).then_inc(shaped, 1)

            dve.wait_ge(rows_loaded, 32)
            add(0)
            for t in range(TL):
                if t + 1 < TL:
                    add(t + 1)
                norm(t)

        @block.scalar
        def _(act):
            def scale(t):
                act.wait_ge(gathered[t % RING], 32 * (t // RING) + 32)
                if t >= RING:
                    act.wait_ge(stored[t % RING], 16 * (t // RING))
                nc.scalar.activation(acc[t % RING][:, :], y1[t % RING][:, :], ACT.Copy, scale=gate[:, 0, t:t + 1]).then_inc(scaled, 1)

            scale(0)
            scale(1)
            for t in range(TL):
                act.wait_ge(stats, t + 1)
                nc.scalar.activation(sd[t % 2][:, :], mv[t % 2][:, 1:2], ACT.Sqrt, bias=m.keep["eps_ln"]).then_inc(std, 1)
                if t + 2 < TL:
                    scale(t + 2)


def program(nc, dram):
    m = Machine(nc, dram)
    for phase in PHASES:
        m.phase_sems = []
        phase(m)
        nc.clear_and_free_semaphores(m.phase_sems)
        nc.all_engine_barrier()


PHASES = [modulation, normed_transposed, delta_inputs, token_inputs,
          delta_gates, delta_rule, attention, mixed_output,
          routing, experts, combine]


def constants():
    i = np.arange(P)
    row, col = i[:, None], i[None, :]
    parts = [row == col, np.ones((P, P)), row <= col, row >= col, row < col,
             -BIG * (row > col), -BIG * (row < col)]
    for r in range(2):
        for lv in range(LEVELS):
            b = 1 << lv
            a, z = (row, col) if r == 0 else (col, row)
            parts.append((a // (2 * b) == z // (2 * b)) & (a // b % 2 == 0) & (z // b % 2 == 1))
    masks = np.concatenate([np.asarray(x, np.float32) for x in parts], axis=1)
    half = DK // 2
    freq = np.float32(10000.0) ** (-np.arange(0, half, 2, dtype=np.float32) / np.float32(half))
    t = np.arange(SEQ)
    ang = [(p.astype(np.float32)[:, None] * freq[None, :]).astype(np.float32) for p in (t // 64, t % 64)]
    rope = np.concatenate([f(a) for f in (np.cos, np.sin) for a in ang for _ in range(2)], axis=1).astype(np.float32)
    small = np.zeros((P, 96), np.float32)
    small[:, 0:4] = [4, 3, 2, 1]
    small[:, 4:12] = [8, 7, 6, 5, 4, 3, 2, 1]
    small[:, 12:20] = np.arange(8) * P
    small[:, 20:68] = np.arange(48)
    small[:, 68] = LN_EPS
    small[:, 69] = NORM_EPS
    ids = (np.arange(P)[:, None] + P * np.arange(TL)[None, :]).astype(np.int32)
    quad = np.zeros((P, P + 32), np.float32)
    quad[:, :P] = row // 32 == col // 32
    quad[:, P:] = row % 32 == np.arange(32)[None, :]
    return {"quad": quad, "masks": masks, "rope": rope, "small": small, "ids": ids}


def kernel(x, c, ctx, c_ctx, w_ada, b_ada, w_in, conv_w, gdn_a_log, gdn_dt_bias, gdn_norm_w,
           diff_lambda, diff_norm_w, w_out, ln1_g, ln1_b, w_router_group, b_router_group,
           w_router_expert, b_router_expert, w_expert_gate, w_expert_up, w_expert_down, ln2_g, ln2_b):
    import concourse.bacc as bacc
    from concourse.bass_utils import run_bass_kernel_spmd as run

    def rep(a):
        return np.ascontiguousarray(np.broadcast_to(np.asarray(a).reshape(1, -1), (P, np.asarray(a).size)))

    cc = np.stack([np.asarray(c).reshape(KD, P), np.asarray(c_ctx).reshape(KD, P)], axis=-1)
    arrays = {
        "tokens": np.concatenate([np.asarray(x)[0], np.asarray(ctx)[0]], axis=0),
        "c_cols": np.ascontiguousarray(cc.transpose(1, 0, 2)).reshape(P, 2 * KD),
        "w_ada": w_ada[0], "b_ada": np.concatenate([b_ada, b_ada], axis=0), "w_in": w_in[0],
        "conv_cols": np.ascontiguousarray(np.asarray(conv_w)[0].reshape(CONV, 3 * H, P).transpose(2, 1, 0)).reshape(P, -1),
        "rep_gates": np.concatenate([rep(gdn_dt_bias), rep(gdn_a_log)], axis=1),
        "rep_norm": np.concatenate([rep(gdn_norm_w), rep(diff_norm_w)], axis=1),
        "rep_lambda": rep(diff_lambda), "w_out": w_out[0],
        "rep_ln": np.concatenate([rep(ln1_g), rep(ln1_b), rep(ln2_g), rep(ln2_b)], axis=1),
        "w_route": np.concatenate([w_router_group[0], w_router_expert[0]], axis=1),
        "rep_route": np.concatenate([rep(b_router_group), rep(b_router_expert)], axis=1),
        "w_gate": w_expert_gate[0], "w_up": w_expert_up[0], "w_down": w_expert_down[0],
    }
    arrays.update(constants())
    nc = bacc.Bacc("TRN2", target_bir_lowering=False, num_devices=1)
    dram = {}
    for name, a in arrays.items():
        a = arrays[name] = np.ascontiguousarray(a)
        dram[name] = nc.dram_tensor("in_" + name, a.shape, mybir.dt.from_np(a.dtype), kind="ExternalInput").ap()
    dram["out"] = nc.dram_tensor("out", (SEQ, D), F32, kind="ExternalOutput").ap()
    program(nc, dram)
    r = run(nc, [{"in_" + k: a for k, a in arrays.items()}], core_ids=[0])
    return r.results[0]["out"].reshape(1, SEQ, D)
```
